# Optimizing a Trainium2 kernel written in Bass

```python
import math, functools
import jax, jax.numpy as jnp
from jax import lax
import numpy as np

D_MODEL = 1024
BATCH = 1
SEQ = 1024
DEPTH = 1
DEC_BATCH = 8
DEC_SEQ = 8
PAST_LEN = 8192
PAGE_SIZE = 128

H_A = 4
DK_A = 128
DV_A = 128
CONV_A = 4
CHUNK_A = 64
H_B = 4
DH_B = 128
H_IDX = 8
D_IDX = 64
TOPK_MAX = 256
Q_BLOCK = 128
N_BUCKETS = 32
MAX_DIST = 2048
D_FF = 2816
CONV_F = 3
EPS = 1e-6

QKV_A = H_A * (2 * DK_A + DV_A)
IN_SIZES = (QKV_A, H_A, H_A, H_A * DV_A, 3 * H_B * DH_B, H_IDX * D_IDX, D_IDX, H_IDX, D_MODEL, D_MODEL)
IN_TOTAL = sum(IN_SIZES)

kernel_name = 'hybrid_deltanet_dsa_convffn_step'

def rms_norm(x, g):
    xf = x.astype(jnp.float32)
    y = xf * lax.rsqrt(jnp.mean(xf * xf, axis=-1, keepdims=True) + EPS)
    return (y * g.astype(jnp.float32)).astype(x.dtype)

def l2_normalize(x):
    xf = x.astype(jnp.float32)
    return (xf * lax.rsqrt(jnp.sum(xf * xf, axis=-1, keepdims=True) + EPS)).astype(x.dtype)

def split_cols(h):
    parts, start = [], 0
    for size in IN_SIZES:
        parts.append(h[..., start:start + size])
        start += size
    return parts

def causal_dwconv(x, buf, w):
    width, t = w.shape[0], x.shape[1]
    xp = jnp.concatenate([buf.astype(x.dtype), x], axis=1)
    out = xp[:, 0:t] * w[0]
    for j in range(1, width):
        out = out + xp[:, j:j + t] * w[j]
    return out, xp[:, t:]

def gated_delta_rule(q, k, v, g, beta, s0):
    f32 = jnp.float32
    b, t, h, dk = q.shape
    dv = v.shape[-1]
    c = math.gcd(t, CHUNK_A)
    n = t // c

    def blocks(a):
        a = a.astype(f32).reshape((b, n, c, h) + a.shape[3:])
        return jnp.moveaxis(a, 3, 2).swapaxes(0, 1)

    qc, kc, vc, gc, bc = blocks(q), blocks(k), blocks(v), blocks(g), blocks(beta)
    gcum = jnp.cumsum(gc, axis=-1)
    tril = jnp.tril(jnp.ones((c, c), bool))
    strict = jnp.tril(jnp.ones((c, c), bool), -1)
    gamma = jnp.exp(jnp.where(tril, gcum[..., :, None] - gcum[..., None, :], -jnp.inf))
    kb = kc * bc[..., None]
    a_mat = jnp.where(strict, jnp.einsum('nbhid,nbhjd->nbhij', kb, kc) * gamma, 0.0)
    rhs = jnp.concatenate([kb * jnp.exp(gcum)[..., None], vc * bc[..., None]], axis=-1)
    sol = lax.linalg.triangular_solve(jnp.eye(c, dtype=f32) + a_mat, rhs,
                                      left_side=True, lower=True, unit_diagonal=True)
    w_mat, u_mat = sol[..., :dk], sol[..., dk:]
    attn = jnp.where(tril, jnp.einsum('nbhid,nbhjd->nbhij', qc, kc) * gamma, 0.0)
    g_last = gcum[..., -1]
    q_dec = qc * jnp.exp(gcum)[..., None]
    k_dec = kc * jnp.exp(g_last[..., None] - gcum)[..., None]

    def step(s, xs):
        w_c, u_c, q_c, attn_c, k_c, gl = xs
        v_new = u_c - jnp.einsum('bhcd,bhde->bhce', w_c, s)
        o = jnp.einsum('bhcd,bhde->bhce', q_c, s) + jnp.einsum('bhij,bhje->bhie', attn_c, v_new)
        s = s * jnp.exp(gl)[..., None, None] + jnp.einsum('bhcd,bhce->bhde', k_c, v_new)
        return s, o

    s_fin, o = lax.scan(step, s0.astype(f32), (w_mat, u_mat, q_dec, attn, k_dec, g_last))
    o = jnp.moveaxis(o.swapaxes(0, 1), 2, 3).reshape(b, t, h, dv)
    return o.astype(q.dtype), s_fin.astype(s0.dtype)

def rel_bucket(dist):
    nd = jnp.maximum(dist, 0)
    max_exact = N_BUCKETS // 2
    nf = jnp.maximum(nd, max_exact).astype(jnp.float32)
    large = max_exact + (jnp.log(nf / max_exact) / math.log(MAX_DIST / max_exact)
                         * (N_BUCKETS - max_exact)).astype(jnp.int32)
    large = jnp.minimum(large, N_BUCKETS - 1)
    return jnp.where(nd < max_exact, nd, large)

def dsa_attend(q, q_idx, w_idx, q_pos, k_idx_keys, gather_kv, rel_bias):
    f32 = jnp.float32
    n_keys = k_idx_keys.shape[1]
    top_k = min(TOPK_MAX, n_keys // 4)
    key_pos = jnp.arange(n_keys, dtype=jnp.int32)
    dots = jnp.einsum('bthd,bsd->bths', q_idx, k_idx_keys) * (D_IDX ** -0.5)
    score = jnp.einsum('bths,bth->bts', jax.nn.relu(dots), w_idx).astype(f32)
    admissible = key_pos[None, :] <= q_pos[:, None]
    score = jnp.where(admissible[None], score, -jnp.inf)
    _, idx = lax.top_k(score, top_k)
    k_sel, v_sel = gather_kv(idx)
    dist = q_pos[None, :, None] - idx
    bias = jnp.moveaxis(rel_bias[rel_bucket(dist)], 3, 2)
    logits = jnp.einsum('bthd,btkhd->bthk', q, k_sel).astype(f32) * (DH_B ** -0.5) + bias.astype(f32)
    logits = jnp.where((dist >= 0)[:, :, None, :], logits, -jnp.inf)
    p = jax.nn.softmax(logits, axis=-1)
    return jnp.einsum('bthk,btkhd->bthd', p.astype(v_sel.dtype), v_sel)

def prompt_attention(qb, kb, vb, q_idx, k_idx, w_idx, rel_bias):
    b, t = qb.shape[:2]
    nb = t // Q_BLOCK
    bidx = jnp.arange(b)[:, None, None]

    def gather(idx):
        return kb[bidx, idx], vb[bidx, idx]

    def to_blocks(a):
        return jnp.moveaxis(a.reshape((b, nb, Q_BLOCK) + a.shape[2:]), 1, 0)

    def one_block(xs):
        q_blk, qi_blk, wi_blk, i = xs
        q_pos = i * Q_BLOCK + jnp.arange(Q_BLOCK, dtype=jnp.int32)
        return dsa_attend(q_blk, qi_blk, wi_blk, q_pos, k_idx, gather, rel_bias)

    out = lax.map(one_block, (to_blocks(qb), to_blocks(q_idx), to_blocks(w_idx), jnp.arange(nb, dtype=jnp.int32)))
    return jnp.moveaxis(out, 0, 1).reshape(b, t, H_B, DH_B)

def sample_attention(qb, kb, vb, q_idx, k_idx, w_idx, cache_k, cache_v, cache_idx_k, page_table, layer, rel_bias):
    b, t = qb.shape[:2]
    past = page_table.shape[1] * PAGE_SIZE
    k_idx_past = cache_idx_k[layer, page_table].reshape(b, past, D_IDX)
    k_idx_keys = jnp.concatenate([k_idx_past.astype(k_idx.dtype), k_idx], axis=1)
    bidx = jnp.arange(b)[:, None, None]

    def gather(idx):
        in_past = (idx < past)[..., None, None]
        pidx = jnp.minimum(idx, past - 1)
        phys = page_table[bidx, pidx // PAGE_SIZE]
        off = pidx % PAGE_SIZE
        nidx = jnp.clip(idx - past, 0, t - 1)
        k_sel = jnp.where(in_past, cache_k[layer, phys, off].astype(kb.dtype), kb[bidx, nidx])
        v_sel = jnp.where(in_past, cache_v[layer, phys, off].astype(vb.dtype), vb[bidx, nidx])
        return k_sel, v_sel

    q_pos = past + jnp.arange(t, dtype=jnp.int32)
    return dsa_attend(qb, q_idx, w_idx, q_pos, k_idx_keys, gather, rel_bias)

def decoder_layer(x, conv_a_buf, rec_a, ffn_buf, attend, w_in, conv_a_w, a_log, dt_bias, norm_a_g,
                  w_proj_a, w_proj_b, w_out, norm1_g, norm2_g, w_up, conv_f_w, conv_f_b, w_down):
    f32 = jnp.float32
    b, t, _ = x.shape
    xn = rms_norm(x, norm1_g)
    (qkv_a, beta_raw, a_raw, z_a, qkv_b, q_idx, k_idx, w_idx, gate_a, gate_b) = split_cols(xn @ w_in)
    conv_qkv, conv_a_new = causal_dwconv(qkv_a, conv_a_buf, conv_a_w)
    conv_qkv = jax.nn.silu(conv_qkv)
    hk = H_A * DK_A
    qa = l2_normalize(conv_qkv[..., :hk].reshape(b, t, H_A, DK_A)) * (DK_A ** -0.5)
    ka = l2_normalize(conv_qkv[..., hk:2 * hk].reshape(b, t, H_A, DK_A))
    va = conv_qkv[..., 2 * hk:].reshape(b, t, H_A, DV_A)
    beta = jax.nn.sigmoid(beta_raw)
    g = -jnp.exp(a_log.astype(f32)) * jax.nn.softplus(a_raw.astype(f32) + dt_bias.astype(f32))
    o_a, rec_a_new = gated_delta_rule(qa, ka, va, g, beta, rec_a)
    o_a = rms_norm(o_a, norm_a_g) * jax.nn.silu(z_a.reshape(b, t, H_A, DV_A))
    hb = H_B * DH_B
    qb = qkv_b[..., :hb].reshape(b, t, H_B, DH_B)
    kb = qkv_b[..., hb:2 * hb].reshape(b, t, H_B, DH_B)
    vb = qkv_b[..., 2 * hb:].reshape(b, t, H_B, DH_B)
    o_b = attend(qb, kb, vb, q_idx.reshape(b, t, H_IDX, D_IDX), k_idx, w_idx * (H_IDX ** -0.5))
    merged = (jax.nn.sigmoid(gate_a) * (o_a.reshape(b, t, -1) @ w_proj_a)
              + jax.nn.sigmoid(gate_b) * (o_b.reshape(b, t, -1) @ w_proj_b))
    x = x + merged @ w_out
    up, ffn_new = causal_dwconv(rms_norm(x, norm2_g) @ w_up, ffn_buf, conv_f_w)
    gate_f, val_f = jnp.split(up + conv_f_b, 2, axis=-1)
    x = x + (jax.nn.silu(gate_f) * val_f) @ w_down
    return x, (kb, vb, k_idx, conv_a_new, rec_a_new, ffn_new)

def setup_inputs(seed: int = 0) -> dict:
    key = jax.random.key(seed)
    ks = jax.random.split(key, 32)
    f32 = jnp.float32
    n_pages = PAST_LEN // PAGE_SIZE
    n_used = DEC_BATCH * n_pages
    n_pool = n_used + n_used // 4

    def nrm(k, shape, scale):
        return jax.random.normal(k, shape, f32) * scale

    page_table = jax.random.permutation(ks[0], n_pool)[:n_used].reshape(DEC_BATCH, n_pages).astype(jnp.int32)
    dt = jnp.exp(jax.random.uniform(ks[13], (DEPTH, H_A), f32, math.log(1e-3), math.log(1e-1)))
    return {
        'x_prompt': nrm(ks[1], (BATCH, SEQ, D_MODEL), 1.0),
        'x_sample': nrm(ks[2], (DEC_BATCH, DEC_SEQ, D_MODEL), 1.0),
        'cache_k': nrm(ks[3], (DEPTH, n_pool, PAGE_SIZE, H_B, DH_B), 1.0),
        'cache_v': nrm(ks[4], (DEPTH, n_pool, PAGE_SIZE, H_B, DH_B), 1.0),
        'cache_idx_k': nrm(ks[5], (DEPTH, n_pool, PAGE_SIZE, D_IDX), 1.0),
        'state_a_conv': nrm(ks[6], (DEPTH, DEC_BATCH, CONV_A - 1, QKV_A), 1.0),
        'state_a_rec': nrm(ks[7], (DEPTH, DEC_BATCH, H_A, DK_A, DV_A), 0.1),
        'state_ffn_conv': nrm(ks[8], (DEPTH, DEC_BATCH, CONV_F - 1, 2 * D_FF), 1.0),
        'page_table': page_table,
        'w_in': nrm(ks[9], (DEPTH, D_MODEL, IN_TOTAL), D_MODEL ** -0.5),
        'conv_a_w': nrm(ks[10], (DEPTH, CONV_A, QKV_A), CONV_A ** -0.5),
        'a_log': jnp.log(jax.random.uniform(ks[11], (DEPTH, H_A), f32, 1.0, 16.0)),
        'dt_bias': dt + jnp.log(-jnp.expm1(-dt)),
        'norm_a_g': 1.0 + nrm(ks[12], (DEPTH, DV_A), 0.02),
        'w_proj_a': nrm(ks[14], (DEPTH, H_A * DV_A, D_MODEL), (H_A * DV_A) ** -0.5),
        'w_proj_b': nrm(ks[15], (DEPTH, H_B * DH_B, D_MODEL), (H_B * DH_B) ** -0.5),
        'w_out': nrm(ks[16], (DEPTH, D_MODEL, D_MODEL), D_MODEL ** -0.5),
        'rel_bias': nrm(ks[17], (N_BUCKETS, H_B), 0.5),
        'norm1_g': 1.0 + nrm(ks[18], (DEPTH, D_MODEL), 0.02),
        'norm2_g': 1.0 + nrm(ks[19], (DEPTH, D_MODEL), 0.02),
        'w_up': nrm(ks[20], (DEPTH, D_MODEL, 2 * D_FF), D_MODEL ** -0.5),
        'conv_f_w': nrm(ks[21], (DEPTH, CONV_F, 2 * D_FF), CONV_F ** -0.5),
        'conv_f_b': nrm(ks[22], (DEPTH, 2 * D_FF), 0.02),
        'w_down': nrm(ks[23], (DEPTH, D_FF, D_MODEL), D_FF ** -0.5),
        'final_g': 1.0 + nrm(ks[24], (D_MODEL,), 0.02),
    }

def reference(x_prompt, x_sample, cache_k, cache_v, cache_idx_k, state_a_conv, state_a_rec, state_ffn_conv,
              page_table, w_in, conv_a_w, a_log, dt_bias, norm_a_g, w_proj_a, w_proj_b, w_out, rel_bias,
              norm1_g, norm2_g, w_up, conv_f_w, conv_f_b, w_down, final_g):
    bp = x_prompt.shape[0]
    dtp = x_prompt.dtype
    attend_prompt = functools.partial(prompt_attention, rel_bias=rel_bias)
    xp, xs = x_prompt, x_sample
    new_p, new_s = [], []
    for l in range(DEPTH):
        lw = (w_in[l], conv_a_w[l], a_log[l], dt_bias[l], norm_a_g[l], w_proj_a[l], w_proj_b[l], w_out[l],
              norm1_g[l], norm2_g[l], w_up[l], conv_f_w[l], conv_f_b[l], w_down[l])
        attend_sample = functools.partial(sample_attention, cache_k=cache_k, cache_v=cache_v,
                                          cache_idx_k=cache_idx_k, page_table=page_table, layer=l,
                                          rel_bias=rel_bias)
        xp, st_p = decoder_layer(xp, jnp.zeros((bp, CONV_A - 1, QKV_A), dtp),
                                 jnp.zeros((bp, H_A, DK_A, DV_A), dtp),
                                 jnp.zeros((bp, CONV_F - 1, 2 * D_FF), dtp), attend_prompt, *lw)
        new_p.append(st_p)
        xs, st_s = decoder_layer(xs, state_a_conv[l], state_a_rec[l], state_ffn_conv[l], attend_sample, *lw)
        new_s.append(st_s)
    y_prompt = rms_norm(xp, final_g)
    y_sample = rms_norm(xs, final_g)
    k_p, v_p, kidx_p, conv_a_p, rec_a_p, ffn_conv_p = [jnp.stack(a) for a in zip(*new_p)]
    k_s, v_s, kidx_s, conv_a_s, rec_a_s, ffn_conv_s = [jnp.stack(a) for a in zip(*new_s)]
    return (y_prompt, y_sample, k_p, v_p, kidx_p, conv_a_p, rec_a_p, ffn_conv_p,
            k_s, v_s, kidx_s, conv_a_s, rec_a_s, ffn_conv_s)


_drawn_inputs = setup_inputs


def setup_inputs(seed=0):
    import zlib

    import numpy as np

    out = dict(_drawn_inputs(seed))
    spreads = {}
    factors = {'norm_a_g': 8.0, 'norm2_g': 2.807, 'conv_f_b': 4.082, 'final_g': 8.119, 'rel_bias': 3.41}
    for name, (base, spread) in spreads.items():
        noise = np.random.default_rng([zlib.crc32(name.encode()), seed]).standard_normal(out[name].shape)
        drawn = base * np.exp(spread * noise) if base else spread * noise
        out[name] = __import__('jax').numpy.asarray(drawn.astype(out[name].dtype))
    for name, factor in factors.items():
        out[name] = (out[name] * factor).astype(out[name].dtype)
    return out
```

```python
from contextlib import ExitStack

import numpy as np
import concourse.bass as bass
from concourse import mybir

F32 = mybir.dt.float32
BF16 = mybir.dt.bfloat16
I32 = mybir.dt.int32
U32 = mybir.dt.uint32
ALU = mybir.AluOpType
ACT = mybir.ActivationFunctionType
AX = mybir.AxisListType

P = 128
DM, SEQ, DEC_B, DEC_T = 1024, 1024, 8, 8
NS = DEC_B * DEC_T
T = SEQ + NS
KD = DM // P
H, DH = 4, 128
HI, DI = 8, 64
PAST, PAGE = 8192, 128
N_PAGES = PAST // PAGE
TOPK = 256
NT = SEQ // P
FF = 2816
FC = FF // P
EPS = 1e-6
N_BUCKETS, MAX_DIST = 32, 2048
CK_ROWS = 640 * PAGE
CI_ROWS = 640 * 8
ARENA = 53000
NEG, MARK = -1e30, -3e38
FAR = 1e6
TOKENS = [(0, 512), (512, 512), (1024, NS)]
A_CH = 3 * H
PR_Z, PR_Q, PR_K, PR_GA, PR_GB, PR_N = 12, 16, 20, 24, 32, 40
REV = SEQ + P
VEC = {}


def _vec_columns():
    at = 0
    for name, n in (("g1", KD), ("g2", KD), ("gf", KD), ("gn", 1), ("wa", 4 * A_CH), ("wf", 3 * 2 * FC),
                    ("bf", 2 * FC), ("alog", H), ("dtb", H), ("rb", H * N_BUCKETS)):
        VEC[name] = at
        at += n
    return at


N_VEC = _vec_columns()

CONSTS = ["IDN", "ONES", "UP", "UPS", "ST", "STS", "BLK", "CAU", "NEW", "L0", "L1", "L2", "L3", "L4", "L5", "L6",
          "THR", "BEQ", "IOT"]
C_AT = {n: i * P for i, n in enumerate(CONSTS)}
N_CONST = len(CONSTS) * P


def bucket_of(d):
    d = np.maximum(d, 0)
    half = N_BUCKETS // 2
    nf = np.maximum(d, half).astype(np.float64)
    large = half + (np.log(nf / half) / np.log(MAX_DIST / half) * (N_BUCKETS - half) + 1e-9).astype(np.int64)
    return np.where(d < half, d, np.minimum(large, N_BUCKETS - 1))


def shape_constants():
    j, i = np.meshgrid(np.arange(P), np.arange(P), indexing="ij")
    c = {n: np.zeros((P, P), np.float32) for n in CONSTS}
    c["IDN"] = (j == i)
    c["ONES"] = np.ones((P, P))
    c["UP"] = (j <= i)
    inb = (j < NS) & (i < NS) & (j // DEC_T == i // DEC_T)
    c["UPS"] = (j <= i) & inb
    c["ST"] = (j < i)
    c["STS"] = (j < i) & inb
    c["BLK"] = inb
    c["CAU"] = np.where(i <= j, 0.0, NEG)
    q = j - NS
    c["NEW"] = np.where((j >= NS) & (i < NS) & (q // DEC_T == i // DEC_T) & (i <= q), 0.0, NEG)
    for lev in range(7):
        s = 1 << lev
        c[f"L{lev}"] = (j // (2 * s) == i // (2 * s)) & ((i // s) % 2 == 1) & ((j // s) % 2 == 0)
    dist = np.arange(PAST + DEC_T)
    b = bucket_of(dist)
    thr = np.array([np.argmax(b >= m) for m in range(1, N_BUCKETS)] + [3e9])
    row = np.zeros(P)
    row[0:N_BUCKETS] = thr
    row[N_BUCKETS:2 * N_BUCKETS] = np.arange(N_BUCKETS)
    c["THR"] = np.broadcast_to(row, (P, P)).copy()
    p = np.arange(P)
    c["THR"][:, 64] = EPS
    c["THR"][:, 65] = 8192 + (p % DEC_T)
    c["THR"][:, 66] = DEC_T * ((p % NS) // DEC_T)
    c["THR"][:, 67] = p // NS
    c["IOT"] = i
    c["BEQ"][:NS, :DEC_B] = (p[:NS, None] // DEC_T == np.arange(DEC_B))
    c["BEQ"][:NS, 64:128] = (p[:NS, None] % DEC_T == (np.arange(64) % DEC_T))
    const = np.concatenate([np.asarray(c[n], np.float32) for n in CONSTS], axis=1)
    r = np.arange(P)
    col = np.arange(DEC_B * P)
    cb, cpar, cb2, ct = col // P, (col % P) // NS, (col % NS) // DEC_T, col % DEC_T
    comb = ((r[:, None] // NS == cpar) & (r[:, None] % DEC_T == ct) & (cb == cb2)).astype(np.float32)
    onehot = np.zeros((N_BUCKETS, REV), np.float32)
    y = np.arange(REV)
    onehot[bucket_of(SEQ - 1 - y), y] = 1.0
    return const, comb, onehot


def program(nc, a, o, s):
    with ExitStack() as ctx:
        def sb(name, n, dt=F32, parts=P):
            return ctx.enter_context(nc.sbuf_tensor(name, [parts, n], dt))

        def lasting(name):
            return ctx.enter_context(nc.semaphore(name))

        phase = []

        def sem(name):
            phase.append(nc.alloc_semaphore(name))
            return phase[-1]

        def end_phase():
            nc.all_engine_barrier()
            nc.clear_and_free_semaphores(phase)
            nc.all_engine_barrier()
            phase.clear()

        def sems(name, n):
            return [sem(f"{name}{k}") for k in range(n)]

        arena = sb("arena", ARENA)
        psum = ctx.enter_context(nc.psum_tensor("psum", [P, 4096], F32))

        def at(off, n, dt=F32):
            v = arena[:, off:off + n]
            return v if dt == F32 else v.bitcast(dt)

        PP = [psum[:, 0:1536], psum[:, 1536:3072]]
        BK = [psum[:, k * 512:(k + 1) * 512] for k in range(8)]

        top = [0]

        def take(n):
            top[0] += n
            return top[0] - n

        const = at(take(N_CONST), N_CONST)
        vec = at(take(N_VEC), N_VEC)

        def C(name, rows=P, cols=P):
            return const[0:rows, C_AT[name]:C_AT[name] + cols]

        def V(name, k=0, n=1):
            return vec[:, VEC[name] + k:VEC[name] + k + n]

        def column(k, rows=P):
            return const[0:rows, C_AT["THR"] + k:C_AT["THR"] + k + 1]
        eps, qpos, newat, parity = column(64), column(65, NS), column(66, NS), column(67)
        ident = C("IDN")
        smw = at(take(160), 160).rearrange("p (t c) -> p t c", c=16)
        wabs = at(take(80), 80).rearrange("p (t c) -> p t c", c=8)
        wsgn = at(take(80), 80).rearrange("p (t c) -> p t c", c=8)
        ws = at(take(80), 80).rearrange("p (t c) -> p t c", c=8)
        mask = at(take(2304), 2304, BF16)
        mask_at = [P * (i * (i + 1) // 2) for i in range(NT)]
        idx_cache = at(take(P), P, I32)
        new_sel = at(take(DEC_T), DEC_T)
        dist_t = at(take(P), P)
        lgs = at(take(512), 512)
        work = top[0]

        QI = at(take(4 * T), 4 * T).rearrange("p (c t) -> p c t", t=T)
        KI = at(take(T), T)
        XN = at(take(KD * T), KD * T).rearrange("p (k t) -> p k t", t=T)
        wb = take(4096)
        wb2 = take(KD * 640)
        WB = [at(w, 4096).rearrange("p (k n) -> p k n", n=512) for w in (wb, wb2)]
        WIX = at(wb2, KD * 640).rearrange("p (k n) -> p k n", n=640)
        WSM = at(take(KD * 16), KD * 16).rearrange("p (k n) -> p k n", n=16)
        stg = take(4 * T)
        STG = [at(stg + b * T, T) for b in range(4)]
        VST = [at(take(512), 512) for b in range(2)]
        z = take(KD * T)
        X = at(z, KD * T).rearrange("p (k t) -> p k t", t=T)
        SCW = PAST // 2 + NS
        SC = at(z, SCW)
        QB = at(z + SCW, 1024).rearrange("p (b n) -> p b n", n=P)
        CM = at(z + SCW + 1024, 1024).rearrange("p (b n) -> p b n", n=P)
        KT = [at(z + SCW + 2048 + b * 1024, 1024).rearrange("p (o n) -> p o n", n=P) for b in range(2)]
        assert SCW + 4096 <= KD * T
        RP = [at(z + b * 1024, 1024) for b in range(2)]
        WK = [at(z + 2048 + b * 1024, 1024) for b in range(2)]
        pg = take(4096)
        PG = [at(pg + b * 1024, 1024).rearrange("p (o n) -> p o n", n=P) for b in range(4)]
        names = ["LV", "LI", "BV", "BI", "LA", "LB", "KEY", "KPG", "KOF", "KNEW", "ACC", "LT1", "LT2", "LT3"]
        LST = {n: at(pg + k * TOPK, TOPK) for k, n in enumerate(names)}
        assert len(names) * TOPK <= 4096
        EQ4 = at(pg, 4 * TOPK)[0:NS, :].rearrange("p (k n) -> p k n", n=TOPK)
        kg2 = take(4096)
        RL = [at(kg2 + b * 512, 512) for b in range(2)]
        PTI = at(kg2 + 1024, 4, I32)
        PIX = at(kg2 + 1032, 32, I32)
        PIF = at(kg2 + 1064, 4)
        WLT = at(kg2 + 1072, P)
        WCOL = at(kg2 + 1200, 8)
        NK = at(kg2 + 1216, 512)
        PTR = at(kg2 + 1728, N_PAGES)
        PTRI = at(kg2 + 1792, N_PAGES, I32)
        KINT = at(kg2 + 1856, TOPK, I32)
        M8 = at(take(8), 8)
        MI8 = at(take(8), 8, U32)
        DMY = at(take(8), 8)
        KG = [at(z + 4096, 4096).rearrange("p (n d) -> p n d", d=512), at(kg2, 4096).rearrange("p (n d) -> p n d", d=512)]
        QBC = [at(pg + b * 2048, 2048) for b in range(2)]
        QKS = at(take(512), 512).rearrange("p (c t) -> p c t", t=NS)
        ISC = [at(take(8), 8, I32) for b in range(2)]
        PDM = at(take(4), 4)
        LG8 = at(take(32), 32)
        assert top[0] <= ARENA, top[0]

        own_a, own_v, own_g, s_const = lasting("own_act"), lasting("own_dve"), lasting("own_pool"), lasting("consts_in")
        s_wix, s_x = sem("idx_weights_in"), sems("x_in", 4)
        s_sq, s_sqmm, s_std, s_xn = sem("squares"), sem("squares_summed"), sem("deviation"), sem("normed")
        s_full, s_free = sems("pp_full", 2), sems("pp_free", 2)
        s_sm, s_smc, s_wl, s_wcolp, s_wcol = sem("small"), sem("small_out"), sem("wl"), sem("wcol_psum"), sem("wcol")
        s_kidx = sem("kidx_stored")
        s_cmd, s_cm, s_qb = sem("comb_in"), sem("comb"), sem("qb")
        s_pt, s_pix, s_pg = sem("page_table_in"), sem("page_rows"), sems("pages_in", 4)
        s_ktp, s_kte, s_dot, s_dotp = sem("kt_psum"), sems("kt_out", 2), sems("dots_done", 2), sems("dots_psum", 2)
        s_rle, s_cmb, s_sce = sems("relu_out", 2), sems("combined", 2), sem("scores_out")
        s_nk, s_nke = sem("new_scores_psum"), sem("new_scores_out")
        s_load, _, s_sto = sems("weights_in", 2), None, sems("stored", 4)
        s_vps, s_vst, s_vo = sem("v_psum"), sems("v_staged", 2), sems("v_stored", 2)
        s_qks, s_qkp, s_qke, s_qso = sem("qk_sample_in"), sem("qk_sample_psum"), sem("qk_sample_out"), sem("qk_sample_stored")
        s_ptr, s_lists, s_ltp, s_idx = sem("page_rows_in"), sem("lists"), sem("lists_psum"), sem("indices")
        s_lg, s_rpe, s_rpu = sem("prompt_dots"), sems("prompt_relu", 2), sems("prompt_relu_used", 2)
        s_kgi, s_kgm, s_kgu = sems("keys_in", 2), sems("keys_times_queries", 2), sems("keys_summed", 2)
        s_qbc = sems("queries_in", 2)
        N_A = 6
        s_gp, s_gat = sem("gates_psum"), sem("gates_out")
        GATES_AFTER = {i: g for i, g in zip(range(2, NT), (0, 4, 4, 10, 10, 16))}
        K_POOL = 8
        KEYS_AFTER = {i: g for i, g in zip(range(2, NT), (0, 2, 2, 5, 5, K_POOL))}
        U0 = 3

        class Own:

            def __init__(self, eng, s, n=0):
                self.eng, self.s, self.n = eng, s, n

            def __call__(self, ins):
                ins.then_inc(self.s, 1)
                self.n = self.n + 1
                return ins

            def settle(self):
                self.eng.wait_ge(self.s, self.n)

        def gather_rows(pool, own, ring, cache, s_in, s_u, isc, pdm, beside=None, then=None):
            own(pool.memset(pdm, 0.0))
            for b in range(2):
                own(pool.memset(ring[b], 0.0))
            n0 = own.n

            def carry(k):
                pool.wait_ge(own_g, i * 6 + (n0 + k))
                pool.tensor_tensor(pdm[:, 2:4], pdm[:, 0:2], pdm[:, 0:2], ALU.add).then_inc(own_g, 1)

            for first, last in ((0, K_POOL // 2), (K_POOL // 2, 8)):
                with pool.Fori(first, last) as i:
                    for b in range(2):
                        pool.wait_ge(s_u[b], i)
                        carry(3 * b)
                        pool.tensor_copy(isc[b], idx_cache[:, bass.ds(i * 16 + 8 * b, 8)]).then_inc(own_g, 1)
                        carry(3 * b + 2)
                        if beside:
                            beside(i, b)
                        for n in range(8):
                            pool.indirect_dma_start(out=ring[b][:, n, :], out_offset=None, in_=a[cache],
                                                    in_offset=bass.IndirectOffsetOnAxis(ap=isc[b][:, n:n + 1], axis=0),
                                                    bounds_check=CK_ROWS - 1, oob_is_err=False).then_inc(s_in[b], 16)
                    if then and first == 0:
                        for b in range(2):
                            then(i, b)
            own.n = n0 + 48

        def times_queries(eng, i, b):
            eng.wait_ge(s_qbc[b], i * 16 + 16)
            eng.wait_ge(s_kgi[b], i * P + P)
            kv = KG[b].rearrange("p (q f) d -> p q f d", f=2)
            eng.tensor_tensor(kv, kv, QBC[b].rearrange("p (q d) -> p q d", d=512).unsqueeze(2)
                              .to_broadcast([P, 4, 2, 512]), ALU.mult).then_inc(s_kgm[b], 1)

        def alone(eng):
            eng.wait_ge(s_const, 32)

        counts = {}

        with nc.Block() as block:
            @block.sync
            def _(sp):
                for q in range(4):
                    sp.dma_start(X[:, 2 * q:2 * q + 2, :], a["X"][:, 2 * q:2 * q + 2, :]).then_inc(s_x[q], 16)
                sp.dma_start(WIX, a["WIX"]).then_inc(s_wix, 16)
                sp.dma_start(WSM, a["WSM"]).then_inc(s_wix, 16)
                sp.dma_start(WB[0], a["WG"][0]).then_inc(s_load[0], 16)
                sp.wait_ge(s_xn, KD)
                sp.dma_start(CM, a["COMB"]).then_inc(s_cmd, 16)
                sp.wait_ge(s_free[1], 3)
                sp.dma_start(o["KIDX"], KI[0:DI, :]).then_inc(s_kidx, 16)
                sp.wait_ge(s_sm, 1)
                sp.dma_start(WB[1], a["WG"][1]).then_inc(s_load[1], 16)
                with sp.Fori(0, N_A // 2) as i:
                    for b in range(2):
                        for c in range(4):
                            sp.wait_ge(s_free[c % 2], i * 4 + (U0 + 2 * b + c // 2 + 1))
                            sp.dma_start(s["PR"][bass.ds(i * 8 + (4 * b + c), 1), :, :].rearrange("o p n -> p (o n)"),
                                         STG[c]).then_inc(s_sto[c], 16)
                        sp.wait_ge(s_full[1], i * 4 + (U0 + 2 * b + 2))
                        sp.dma_start(WB[b], a["WG"][bass.ds(i * 2 + (b + 2), 1), :, :].rearrange("o p n -> p (o n)")
                                     .rearrange("p (k n) -> p k n", n=512)).then_inc(s_load[b], 16)
                for c in range(4):
                    sp.wait_ge(s_sto[c], 16 * N_A)
                sp.dma_start(QKS, s["PR"][PR_Q:PR_Q + 8, :, SEQ:T].rearrange("c p t -> p c t")).then_inc(s_qks, 16)
                for t in range(NT + 1):
                    sp.wait_ge(s_vst[t % 2], t // 2 + 1)
                    dst = o["VP"][t * P:(t + 1) * P, :] if t < NT else o["VS"]
                    rows = P if t < NT else NS
                    sp.dma_start(dst, VST[t % 2][0:rows, :]).then_inc(s_vo[t % 2], 16)
                sp.wait_ge(s_vps, NT + 1)
                sp.dma_start(WB[0], a["WG"][8].rearrange("p (k n) -> p k n", n=512)).then_inc(s_load[0], 16)
                for b, dst in ((0, s["QS"]), (1, o["KS"])):
                    sp.wait_ge(s_qke, b + 1)
                    sp.dma_start(dst, VST[b][0:NS, :]).then_inc(s_qso, 16)
                sp.wait_ge(s_sce, 8)
                sp.dma_start(PTRI[0:NS, :], a["PTR"]).then_inc(s_ptr, 16)
                for g in range(4):
                    for c in range(4):
                        sp.wait_ge(s_gat, 4 * g + c + 1)
                        sp.dma_start(s["PR"][PR_GA + 4 * g + c], STG[c]).then_inc(s_sto[c], 16)
                    if g < 2:
                        b = (g + 1) % 2
                        sp.dma_start(WB[b], a["WG"][9 + g].rearrange("p (k n) -> p k n", n=512)).then_inc(s_load[b], 16)
                sp.wait_ge(s_kidx, 16)
                for b in range(2):
                    sp.wait_ge(s_vo[b], 16 * (5 - b))
                for c in range(4):
                    sp.wait_ge(s_sto[c], 16 * (N_A + 4))

            @block.gpsimd
            def _(pool):
                own = Own(pool, own_g)
                pool.dma_start(PTI, a["PTI"]).then_inc(s_pt, 16)
                pool.wait_ge(s_pix, 1)
                for j in range(8):
                    for g in range(4):
                        if j:
                            pool.wait_ge(s_ktp, 2 * (4 * (j - 1) + g) + 2)
                        n = g * 8 + j
                        pool.indirect_dma_start(
                            out=PG[g].rearrange("p o n -> p (o n)"), out_offset=None, in_=a["CI"],
                            in_offset=bass.IndirectOffsetOnAxis(ap=PIX[:, n:n + 1], axis=0),
                            bounds_check=CI_ROWS - 1, oob_is_err=False).then_inc(s_pg[g], 16)
                pool.wait_ge(s_idx, 1)

                def multiply(i, b):
                    times_queries(pool, i, b)

                def load_queries(i, b):
                    pool.dma_start(QBC[b], s["QS"][bass.ds(i * 8 + 4 * b, 4), :].rearrange("q n -> (q n)")
                                   .partition_broadcast(P)).then_inc(s_qbc[b], 16)
                pool.wait_ge(s_qso, 32)
                gather_rows(pool, own, KG, "CK", s_kgi, s_kgu, ISC, PDM, load_queries, multiply)
                counts["pool"] = own.n

            @block.tensor
            def _(pe):
                pe.wait_ge(s_const, 32)
                uses = [0, 0]

                def project(b, K, weights, rhs, used=None):
                    n = uses[b] if used is None else used
                    if used is not None or n:
                        pe.wait_ge(s_free[b], n)
                    for k in range(K):
                        for t0, n in TOKENS:
                            last = pe.matmul(PP[b][:, t0:t0 + n], weights(k), rhs(k)[:, t0:t0 + n],
                                             start=(k == 0), stop=(k == K - 1))
                    last.then_inc(s_full[b], 1)
                    uses[b] += 1

                for k in range(KD):
                    pe.wait_ge(s_sq, k + 1)
                    for t0, n in TOKENS:
                        last = pe.matmul(PP[0][:, t0:t0 + n], C("ONES"), STG[k % 2][:, t0:t0 + n], start=(k == 0), stop=(k == KD - 1))
                    last.then_inc(s_sqmm if k < KD - 1 else s_full[0], 1)
                uses[0] = 1
                pe.wait_ge(s_wix, 32)
                pe.wait_ge(s_xn, KD)
                for c in range(5):
                    project((c + 1) % 2, KD, lambda k: WIX[:, k, c * P:(c + 1) * P], lambda k: XN[:, k, :])
                for t in range(NT + 2):
                    t0, n = (t * P, P) if t < NT else (SEQ, NS) if t == NT else (T - P, P)
                    for k in range(KD):
                        last = pe.matmul(BK[6][0:n, t * 16:(t + 1) * 16], XN[:, k, t0:t0 + n], WSM[:, k, :],
                                         start=(k == 0), stop=(k == KD - 1))
                last.then_inc(s_sm, 1)
                pe.wait_ge(s_wl, 1)
                pe.matmul(BK[7][:, 0:DEC_B], WLT[0:NS, :], C("BEQ", NS, DEC_B), start=True, stop=True).then_inc(s_wcolp, 1)

                pe.wait_ge(s_qb, 1)
                pe.wait_ge(s_cm, 1)
                for b in range(2):
                    pe.wait_ge(s_free[b], uses[b])

                def transpose_keys(j, g):
                    pe.wait_ge(s_pg[g], j * 16 + 16)
                    for hh in range(2):
                        pe.wait_ge(s_kte[hh], j * 4 + g)
                        for q in range(4):
                            last = pe.transpose(BK[hh][:, q * P:(q + 1) * P], PG[g][:, 4 * hh + q, :], ident)
                        last.then_inc(s_ktp, 1)

                def scores(j, final):
                    for g in range(4):
                        for hh in range(2):
                            pe.wait_ge(s_kte[hh], j * 4 + (g + 1))
                        for bb in range(2):
                            pe.wait_ge(s_rle[bb], j * 4 + g)
                            last = pe.matmul(BK[2 + bb], QB[:, 2 * g + bb, :],
                                             KT[g % 2][:, :, bb * N_PAGES:(bb + 1) * N_PAGES], start=True, stop=True)
                            last.then_inc(s_dotp[bb], 1)
                        if g < 3:
                            transpose_keys(j, g + 1)
                        elif not final:
                            transpose_keys(j + 1, 0)
                        for bb in range(2):
                            pe.wait_ge(s_rle[bb], j * 4 + (g + 1))
                            if g == bb == 0:
                                pe.wait_ge(s_sce, j)
                            last = pe.matmul(BK[4], CM[:, 2 * g + bb, :], RL[bb], start=(g == bb == 0), stop=(g == 3 and bb == 1))
                            last.then_inc(s_cmb[bb], 1)

                transpose_keys(0, 0)
                with pe.Fori(0, 7) as j:
                    scores(j, False)
                scores(7, True)
                for h in range(HI):
                    r = slice(DI * (h % 2), DI * (h % 2) + DI)
                    last = pe.matmul(BK[(5, 3)[h % 2]][:, h // 2 * NS:(h // 2 + 1) * NS], QI[r, h // 2, T - P:T], KI[r, SEQ:T],
                                     start=True, stop=True)
                last.then_inc(s_nk, 1)
                pe.wait_ge(s_nke, 2)
                pe.wait_ge(s_sce, 8)

                base = list(uses)
                with pe.Fori(0, N_A // 2) as i:
                    for b in range(2):
                        pe.wait_ge(s_load[b], i * 16 + 16)
                        for c in range(4):
                            project(c % 2, KD, lambda k: WB[b][:, k, c * P:(c + 1) * P], lambda k: XN[:, k, :],
                                    i * 4 + (base[c % 2] + 2 * b + c // 2))
                uses[:] = [base[0] + 2 * N_A, base[1] + 2 * N_A]
                pe.wait_ge(s_load[0], 64)
                pe.wait_ge(s_smc, 1)
                for t in range(NT + 1):
                    n = P if t < NT else NS
                    if t >= 2:
                        pe.wait_ge(s_vst[t % 2], t // 2)
                    else:
                        pe.wait_ge(s_wcol, 1)
                    for k in range(KD):
                        last = pe.matmul(BK[6 + t % 2][0:n, :], XN[:, k, t * P:t * P + n], WB[0][:, k, :],
                                         start=(k == 0), stop=(k == KD - 1))
                    last.then_inc(s_vps, 1)
                pe.wait_ge(s_qks, 16)
                for b in range(2):
                    pe.wait_ge(s_vst[b], 5 - b)
                    for h in range(H):
                        last = pe.transpose(BK[6 + b][0:NS, h * P:(h + 1) * P], QKS[:, 4 * b + h, :], ident)
                    last.then_inc(s_qkp, 1)
                pe.wait_ge(s_lists, 1)
                pe.wait_ge(s_qke, 2)
                for n, name in enumerate(("LT1", "LT3")):
                    for hh in range(2):
                        last = pe.transpose(BK[6][:, (2 * n + hh) * NS:(2 * n + hh + 1) * NS],
                                            LST[name][0:NS, hh * P:(hh + 1) * P], ident[0:NS, 0:NS])
                last.then_inc(s_ltp, 1)
                for b in range(2):
                    pe.wait_ge(s_free[b], uses[b])
                u = g = 0
                for i in range(2, NT):
                    L = P * (i + 1)
                    for h in range(HI):
                        r = slice(DI * (h % 2), DI * (h % 2) + DI)
                        if u >= 2:
                            pe.wait_ge(s_rpe[u % 2], u // 2)
                        for k0 in range(0, L, 512):
                            n = min(512, L - k0)
                            last = pe.matmul(psum[:, 1024 * (u % 2) + k0:1024 * (u % 2) + k0 + n],
                                             QI[r, h // 2, i * P:(i + 1) * P], KI[r, k0:k0 + n], start=True, stop=True)
                        last.then_inc(s_lg, 1)
                        u += 1
                    while g < GATES_AFTER[i]:
                        w, c = (g // 4 + 1) % 2, g % 4
                        if c == 0:
                            pe.wait_ge(s_load[w], 16 * (g // 8) + (64 if w else 80))
                        if g:
                            pe.wait_ge(s_gat, g)
                        for k in range(KD):
                            for t0, n in TOKENS:
                                last = pe.matmul(psum[:, 2048 + t0:2048 + t0 + n], WB[w][:, k, c * P:(c + 1) * P], XN[:, k, t0:t0 + n],
                                                 start=(k == 0), stop=(k == KD - 1))
                        last.then_inc(s_gp, 1)
                        g += 1

            @block.scalar
            def _(act):
                own = Own(act, own_a)
                act.dma_start(const, a["CONST"]).then_inc(s_const, 16)
                act.dma_start(vec, a["VEC"]).then_inc(s_const, 16)
                for k in range(KD):
                    act.wait_ge(s_x[k // 2], 16)
                    if k >= 2:
                        act.wait_ge(s_sqmm, k - 1)
                    act.activation(STG[k % 2], X[:, k, :], ACT.Square).then_inc(s_sq, 1)
                act.wait_ge(s_full[0], 1)
                act.wait_ge(s_const, 32)
                own(act.activation(STG[2], PP[0][:, 0:T], ACT.Ln, scale=1.0 / DM, bias=eps))
                own.settle()
                act.activation(STG[3], STG[2], ACT.Exp, scale=-0.5).then_inc(s_free[0], 1)
                for c in range(5):
                    b = (c + 1) % 2
                    act.wait_ge(s_full[b], (c + 1) // 2 + 1)
                    act.activation(QI[:, c, :] if c < 4 else KI, PP[b][:, 0:T], ACT.Copy).then_inc(s_free[b], 1)
                act.wait_ge(s_sm, 1)
                act.activation(smw[:, 0:NT, :], BK[6][:, 0:NT * 16].rearrange("p (t c) -> p t c", c=16), ACT.Copy)
                act.activation(smw[0:NS, NT, :], BK[6][0:NS, NT * 16:(NT + 1) * 16], ACT.Copy)
                act.activation(smw[:, NT + 1, :], BK[6][:, (NT + 1) * 16:(NT + 2) * 16], ACT.Copy).then_inc(s_smc, 1)
                with act.Fori(0, 8) as j:
                    for g in range(4):
                        for bb in range(2):
                            act.wait_ge(s_cmb[bb], j * 4 + g)
                            act.wait_ge(s_dotp[bb], j * 4 + (g + 1))
                            act.activation(RL[bb], BK[2 + bb], ACT.Relu).then_inc(s_rle[bb], 1)
                with act.Fori(0, N_A // 2) as i:
                    for b in range(2):
                        for c in range(4):
                            act.wait_ge(s_sto[c], i * 32 + 16 * b)
                            act.wait_ge(s_full[c % 2], i * 4 + (U0 + 2 * b + c // 2 + 1))
                            act.activation(STG[c], PP[c % 2][:, 0:T], ACT.Copy).then_inc(s_free[c % 2], 1)
                for t in range(NT + 1):
                    n = P if t < NT else NS
                    if t >= 2:
                        act.wait_ge(s_vo[t % 2], 16 * (t // 2))
                    act.wait_ge(s_vps, t + 1)
                    act.activation(VST[t % 2][0:n, :], BK[6 + t % 2][0:n, :], ACT.Copy).then_inc(s_vst[t % 2], 1)
                for b in range(2):
                    act.wait_ge(s_vo[b], 16 * (5 - b))
                    act.wait_ge(s_qkp, b + 1)
                    act.activation(VST[b][0:NS, :], BK[6 + b][0:NS, :], ACT.Copy).then_inc(s_qke, 1)
                u = g = kg = 0
                for i in range(2, NT):
                    L = P * (i + 1)
                    for h in range(HI):
                        if u >= 2:
                            act.wait_ge(s_rpu[u % 2], u // 2)
                        act.wait_ge(s_lg, u + 1)
                        act.activation(RP[u % 2][:, 0:L], psum[:, 1024 * (u % 2):1024 * (u % 2) + L], ACT.Relu,
                                       scale=wabs[:, i, h:h + 1]).then_inc(s_rpe[u % 2], 1)
                        u += 1
                    while g < GATES_AFTER[i]:
                        act.wait_ge(s_sto[g % 4], 16 * (N_A + g // 4))
                        act.wait_ge(s_gp, g + 1)
                        act.activation(STG[g % 4], psum[:, 2048:2048 + T], ACT.Sigmoid).then_inc(s_gat, 1)
                        g += 1
                    while kg < KEYS_AFTER[i]:
                        b = kg % 2
                        act.wait_ge(s_kgm[b], kg // 2 + 1)
                        for n in range(8):
                            for h in range(H):
                                part = KG[b][:, n, h * DH:(h + 1) * DH]
                                at_col = (n % 2) * TOPK + (4 * kg + n // 2) * H + h
                                last = act.activation(part, part, ACT.Copy, accum_out=lgs[:, at_col:at_col + 1])
                        last.then_inc(s_kgu[b], 1)
                        kg += 1
                counts["act"] = own.n

            @block.vector
            def _(dve):
                own = Own(dve, own_v)
                own(dve.memset(smw, 0.0))
                own(dve.memset(mask[:, 0:mask_at[2]], 0.0))
                dve.wait_ge(s_pt, 16)
                own(dve.tensor_scalar(PIF, PTI, 8.0, None, ALU.mult))
                own.settle()
                for j in range(8):
                    last = dve.tensor_scalar(PIX.rearrange("p (g j) -> p g j", j=8)[:, :, j], PIF, float(j), None, ALU.add)
                last.then_inc(s_pix, 1)
                dve.wait_ge(s_free[0], 1)
                dve.wait_ge(s_const, 32)
                for k in range(KD):
                    dve.scalar_tensor_tensor(out=XN[:, k, :], in0=X[:, k, :], scalar=V("g1", k), in1=STG[3],
                                             op0=ALU.mult, op1=ALU.mult).then_inc(s_xn, 1)
                for i in range(2):
                    dve.tensor_copy(mask[:, mask_at[i] + i * P:mask_at[i] + (i + 1) * P], C("CAU"))
                dve.wait_ge(s_xn, KD)
                own(dve.memset(QB, 0.0))
                own(dve.memset(SC[0:NS, PAST // 2:SCW], NEG))
                for b in range(2):
                    dve.wait_ge(s_free[b], U0)
                own.settle()
                for h in range(HI):
                    src = QI[DI * (h % 2):DI * (h % 2) + DI, h // 2, SEQ:T].rearrange("p (b t) -> p b t", t=DEC_T)
                    for par in range(2):
                        c0 = par * NS + h * DEC_T
                        last = dve.tensor_copy(QB[par * DI:par * DI + DI, :, c0:c0 + DEC_T], src)
                last.then_inc(s_qb, 1)
                dve.wait_ge(s_smc, 1)
                own(dve.tensor_scalar(ws, smw[:, :, 0:HI], HI ** -0.5, DI ** -0.5, ALU.mult, ALU.mult))
                own.settle()
                own(dve.scalar_tensor_tensor(out=wabs, in0=ws, scalar=-1.0, in1=ws, op0=ALU.mult, op1=ALU.max))
                own(dve.tensor_scalar(wsgn, ws, 0.0, 2.0, ALU.is_ge, ALU.mult))
                for par in range(2):
                    last = dve.tensor_tensor(WLT[0:NS, par * NS:(par + 1) * NS].rearrange("p (h t) -> p h t", t=DEC_T),
                                             ws[0:NS, NT, :].unsqueeze(2).to_broadcast([NS, HI, DEC_T]),
                                             C("BEQ", NS)[:, 64:128].rearrange("p (h t) -> p h t", t=DEC_T), ALU.mult)
                last.then_inc(s_wl, 1)
                own.settle()
                own(dve.tensor_scalar(wsgn, wsgn, -1.0, None, ALU.add))
                dve.wait_ge(s_wcolp, 1)
                dve.tensor_copy(WCOL, BK[7][:, 0:DEC_B]).then_inc(s_wcol, 1)
                dve.wait_ge(s_wcol, 1)
                dve.wait_ge(s_cmd, 16)
                for b in range(DEC_B):
                    last = dve.tensor_scalar(CM[:, b, :], CM[:, b, :], WCOL[:, b:b + 1], None, ALU.mult)
                last.then_inc(s_cm, 1)
                with dve.Fori(0, 8) as j:
                    for g in range(4):
                        for hh in range(2):
                            dve.wait_ge(s_ktp, j * 8 + (2 * g + hh + 1))
                            dve.tensor_copy(KT[g % 2][:, 4 * hh:4 * hh + 4, :],
                                            BK[hh].rearrange("p (o n) -> p o n", n=P)).then_inc(s_kte[hh], 1)
                    dve.wait_ge(s_cmb[1], j * 4 + 4)
                    dve.tensor_scalar(SC[:, 0:PAST // 2].rearrange("p (g o) -> p g o", o=64)[:, :, bass.ds(j * 8, 8)],
                                      BK[4].rearrange("p (o g) -> p g o", o=8), 1.0, None, ALU.mult).then_inc(s_sce, 1)
                dve.wait_ge(s_nk, 1)
                up = slice(NS, P)
                nkv = NK[up, :].rearrange("p (h k) -> p h k", k=NS)
                for f, bank in ((0, 5), (1, 3)):
                    dve.tensor_scalar(NK[up, :].rearrange("p (q f k) -> p q f k", f=2, k=NS)[:, :, f, :],
                                      BK[bank][up, 0:HI // 2 * NS].rearrange("p (q k) -> p q k", k=NS), 0.0, None, ALU.max).then_inc(s_nke, 1)
                dve.wait_ge(s_nke, 2)
                own(dve.tensor_tensor(nkv, nkv, ws[up, NT + 1, :].unsqueeze(2).to_broadcast([NS, HI, NS]), ALU.mult))
                own.settle()
                own(dve.tensor_reduce(SC[up, PAST // 2:SCW], nkv.rearrange("p h k -> p k h"), AX.X, ALU.add))
                own.settle()
                own(dve.tensor_tensor(SC[up, PAST // 2:SCW], SC[up, PAST // 2:SCW], C("NEW")[up, 0:NS], ALU.add))
                own.settle()

                n0 = own.n
                with dve.Fori(0, TOPK // 8) as r:
                    own.n = r * 5 + n0
                    own(dve.max(M8, SC))
                    own.settle()
                    own(dve.tensor_scalar(LST["LV"][:, bass.ds(r * 8, 8)], M8, 1.0, None, ALU.mult))
                    own(dve.max_index(MI8, M8, SC))
                    own(dve.match_replace(SC, M8, SC, MARK))
                    own.settle()
                    own(dve.tensor_scalar(LST["LI"][:, bass.ds(r * 8, 8)], MI8, 1.0, None, ALU.mult))
                own.n = n0 + 5 * TOPK // 8
                own.settle()
                L = LST
                lo = slice(0, NS)
                own(dve.tensor_scalar(L["LA"], L["LI"], float(1 - PAST // 2), 0.0, ALU.add, ALU.max))
                own(dve.tensor_scalar(L["LB"], L["LI"], 2.0, parity, ALU.mult, ALU.add))
                own.settle()
                own(dve.tensor_tensor(L["LI"], L["LB"], L["LA"], ALU.subtract))
                own.settle()
                own(dve.tensor_copy(L["BV"][lo, :], L["LV"][up, ::-1]))
                own(dve.tensor_copy(L["BI"][lo, :], L["LI"][up, ::-1]))
                own.settle()
                own(dve.tensor_tensor(L["LA"][lo, :], L["LV"][lo, :], L["BV"][lo, :], ALU.is_gt))
                own(dve.tensor_tensor(L["LB"][lo, :], L["LV"][lo, :], L["BV"][lo, :], ALU.is_equal))
                own(dve.tensor_tensor(L["KEY"][lo, :], L["LI"][lo, :], L["BI"][lo, :], ALU.is_lt))
                own.settle()
                own(dve.tensor_tensor(L["LB"][lo, :], L["LB"][lo, :], L["KEY"][lo, :], ALU.mult))
                own(dve.tensor_tensor(L["LT1"][lo, :], L["LI"][lo, :], L["BI"][lo, :], ALU.subtract))
                own.settle()
                own(dve.tensor_tensor(L["LA"][lo, :], L["LA"][lo, :], L["LB"][lo, :], ALU.add))
                own.settle()
                own(dve.tensor_tensor(L["LT1"][lo, :], L["LT1"][lo, :], L["LA"][lo, :], ALU.mult))
                own.settle()
                own(dve.tensor_tensor(L["KEY"][lo, :], L["LT1"][lo, :], L["BI"][lo, :], ALU.add))
                own.settle()
                own(dve.tensor_scalar(L["KNEW"][lo, :], L["KEY"][lo, :], float(PAST), None, ALU.is_ge))
                own(dve.tensor_copy(KINT[lo, :], L["KEY"][lo, :]))
                dve.wait_ge(s_ptr, 16)
                own(dve.tensor_copy(PTR[lo, :], PTRI[lo, :]))
                own(dve.memset(L["ACC"][lo, :], 0.0))
                own.settle()
                kpi, koi = L["LA"][lo, :].bitcast(I32), L["LB"][lo, :].bitcast(I32)
                own(dve.tensor_scalar(kpi, KINT[lo, :], 7, None, ALU.arith_shift_right))
                own(dve.tensor_scalar(koi, KINT[lo, :], PAGE - 1, None, ALU.bitwise_and))
                own.settle()
                own(dve.tensor_copy(L["KPG"][lo, :], kpi))
                own(dve.tensor_copy(L["KOF"][lo, :], koi))
                own.settle()
                n0 = own.n
                with dve.Fori(0, N_PAGES // 2) as r:
                    own.n = r * 4 + n0
                    for k in range(2):
                        dve.wait_ge(own_v, r * 4 + (n0 - 1 + k))
                        own(dve.tensor_scalar(L["LT2" if k else "LT1"][lo, :], L["KPG"][lo, :], C("IOT", NS)[:, bass.ds(r * 2 + k, 1)],
                                              PTR[lo, bass.ds(r * 2 + k, 1)], ALU.is_equal, ALU.mult))
                    own.n = r * 4 + (n0 + 1)
                    for k in range(2):
                        dve.wait_ge(own_v, r * 4 + (n0 + (2, 3)[k]))
                        dve.tensor_tensor(L["ACC"][lo, :], L["ACC"][lo, :], L["LT2" if k else "LT1"][lo, :], ALU.add).then_inc(own_v, 1)
                own.n = n0 + 2 * N_PAGES
                own.settle()
                own(dve.scalar_tensor_tensor(out=L["LT1"][lo, :], in0=L["ACC"][lo, :], scalar=float(PAGE), in1=L["KOF"][lo, :], op0=ALU.mult, op1=ALU.add))
                own(dve.scalar_tensor_tensor(out=L["LT3"][lo, :], in0=L["KNEW"][lo, :], scalar=-100.0, in1=L["KEY"][lo, :], op0=ALU.mult, op1=ALU.subtract))
                own(dve.tensor_scalar(L["LT2"][lo, :], L["KEY"][lo, :], newat, float(-PAST), ALU.subtract, ALU.add))
                own.settle()
                own(dve.scalar_tensor_tensor(out=L["LT1"][lo, :], in0=L["KNEW"][lo, :], scalar=FAR, in1=L["LT1"][lo, :], op0=ALU.mult, op1=ALU.add))
                dve.tensor_scalar(L["LT3"][lo, :], L["LT3"][lo, :], qpos, None, ALU.add).then_inc(s_lists, 1)
                for k0 in (0, 4):
                    own(dve.tensor_tensor(EQ4, L["LT2"][lo, :].unsqueeze(1).to_broadcast([NS, 4, TOPK]),
                                          C("THR", NS)[:, N_BUCKETS + k0:N_BUCKETS + k0 + 4].unsqueeze(2).to_broadcast([NS, 4, TOPK]), ALU.is_equal))
                    own.settle()
                    own(dve.tensor_reduce(new_sel[lo, k0:k0 + 4], EQ4, AX.X, ALU.add))
                    own.settle()
                own(dve.tensor_scalar(new_sel[lo, :], new_sel[lo, :], -1.0, -NEG, ALU.add, ALU.mult))
                dve.wait_ge(s_ltp, 1)
                own(dve.tensor_copy(idx_cache.rearrange("p (q f) -> p f q", f=2), BK[6][:, 0:P].rearrange("p (f q) -> p f q", f=2)))
                dve.tensor_copy(dist_t, BK[6][:, P:2 * P]).then_inc(s_idx, 1)

                u = 0
                for i in range(2, NT):
                    W = WK[i % 2][:, 0:P * (i + 1)]
                    for h in range(HI):
                        dve.wait_ge(s_rpe[u % 2], u // 2 + 1)
                        src, sg = RP[u % 2][:, 0:P * (i + 1)], wsgn[:, i, h:h + 1]
                        if h == 0:
                            ins = dve.tensor_scalar(W, src, sg, None, ALU.mult)
                        else:
                            dve.wait_ge(s_rpu[(u - 1) % 2], (u - 1) // 2 + 1)
                            ins = dve.scalar_tensor_tensor(out=W, in0=src, scalar=sg, in1=W, op0=ALU.mult, op1=ALU.add)
                        ins.then_inc(s_rpu[u % 2], 1)
                        u += 1
                    dve.wait_ge(s_rpu[(u - 1) % 2], (u - 1) // 2 + 1)
                    D = WK[i % 2][:, P * i:P * (i + 1)]
                    own(dve.tensor_tensor(D, D, C("CAU"), ALU.add))
                    if i % 2 == 0:
                        continue
                    own.settle()
                    n0 = own.n
                    pair = [(M8, WK[0][:, 0:P * i]), (MI8.bitcast(F32), WK[1][:, 0:P * (i + 1)])]
                    def after(r, k, n):
                        dve.wait_ge(own_v, r * 8 + (n0 + n))
                        own(dve.tensor_scalar(DMY[:, 2 * k:2 * k + 2], C("ONES")[:, 0:2], 1.0, None, ALU.mult))

                    with dve.Fori(0, TOPK // 8) as r:
                        for k, (m8, W) in enumerate(pair):
                            after(r, k, 2 * k - 2)
                            own(dve.max(m8, W))
                        for k, (m8, W) in enumerate(pair):
                            after(r, 2 + k, 2 * k + 2)
                            own(dve.match_replace(W, m8, W, MARK))
                    own.n = n0 + TOPK
                    own.settle()
                    for k, (m8, W) in enumerate(pair):
                        t = i - 1 + k
                        own(dve.tensor_scalar(mask[:, mask_at[t]:mask_at[t] + P * (t + 1)], W, 0.5 * MARK, NEG, ALU.is_gt, ALU.mult))
                    own.settle()
                for g in range(K_POOL, 16):
                    b = g % 2
                    times_queries(dve, g // 2, b)
                    dve.wait_ge(s_kgm[b], g // 2 + 1)
                    for f in range(2):
                        last = dve.tensor_reduce(lgs[:, f * TOPK + 4 * H * g:f * TOPK + 4 * H * (g + 1)].rearrange("p (q h) -> p q h", h=H),
                                                 KG[b].rearrange("p (q f) (h d) -> p q f h d", f=2, h=H)[:, :, f, :, :], AX.X, ALU.add)
                    last.then_inc(s_kgu[b], 1)
                counts["dve"] = own.n

        end_phase()
        HD = H * DH
        CW = T + 3
        NSC = DEC_B * (DEC_T + 3)
        OA = at(work, H * T).rearrange("p (h t) -> p h t", t=T)
        OB = at(work + H * T, H * T).rearrange("p (h t) -> p h t", t=T)
        top[0] = work + 2 * H * T
        work2 = top[0]
        QKV = at(take(A_CH * T), A_CH * T).rearrange("p (c t) -> p c t", t=T)
        S0 = at(take(DEC_B * HD), DEC_B * HD).rearrange("p (b h e) -> p b h e", b=DEC_B, h=H)
        GATES = at(take(2 * (NT + 1) * H), 2 * (NT + 1) * H).rearrange("p (k t h) -> p k t h", k=2, h=H)
        G, BETA = GATES[:, 0, :, :], GATES[:, 1, :, :]
        GT1 = at(take((NT + 1) * H), (NT + 1) * H).rearrange("p (t h) -> p t h", h=H)
        EXPA = at(take(H), H)
        z2 = top[0]
        CI = [at(take(CW), CW) for _ in range(3)]
        CV = [at(take(SEQ), SEQ) for _ in range(3)]
        SQ = [at(take(T), T) for _ in range(2)]
        NR = [at(take(T), T) for _ in range(2)]
        RT = [at(take(T), T) for _ in range(2)]
        RN = [c[:, 0:T] for c in CI]
        SIN = at(take(A_CH * NS), A_CH * NS).rearrange("p (c t) -> p c t", t=NS)
        SAS = at(take(A_CH * 3 * DEC_B), A_CH * 3 * DEC_B).rearrange("p (c t) -> p c t", t=3 * DEC_B)
        CIS = at(take(A_CH * NSC), A_CH * NSC).rearrange("p (c b t) -> p c b t", c=A_CH, b=DEC_B)
        CVS = at(take(A_CH * NS), A_CH * NS).rearrange("p (c b t) -> p c b t", c=A_CH, b=DEC_B)
        CVT = at(take(A_CH * NS), A_CH * NS).rearrange("p (c b t) -> p c b t", c=A_CH, b=DEC_B)
        COAS = at(take(A_CH * 27), A_CH * 27).rearrange("p (c t) -> p c t", t=27)
        assert top[0] <= ARENA, top[0]
        top[0] = z2
        BUFS = ["KC", "VC", "R", "D", "GM", "ATT", "BM", "BL0", "BL1", "TI", "UI", "YS", "KBG", "KDC", "VB", "NW", "QD", "VN"]
        TILE = [{n: take(HD) for n in BUFS} for _ in range(2)]
        TILE.append(TILE[0])
        SMALL = [{n: at(take(8), 8) for n in ("GB", "GC", "EX", "GD", "BG")} for _ in range(2)]
        SMALL.append(SMALL[0])
        ST = [at(take(HD), HD) for _ in range(2)]
        GBJ = at(take(DEC_B * H), DEC_B * H)
        ELS = at(take(DEC_B * H), DEC_B * H)
        KDM = [at(take(HD), HD) for _ in range(2)]
        assert top[0] <= ARENA, top[0]

        s_ci, s_cv, s_cva = sems("conv_in", 3), sems("conv_done", 3), sems("conv_silu", 3)
        s_si, s_cvs, s_cvsa, s_coa = sem("sample_conv_in"), sem("sample_conv"), sem("sample_silu"), sem("conv_state_stored")
        s_qkn = sems("qk_normed", 2)
        s_nrt, s_ort = sems("norm_root", 2), sems("out_norm_root", 2)
        s_sqa, s_nmp, s_nme = sems("conv_squares", 2), sems("norm_psum", 2), sems("norm_out", 2)
        s_gexp, s_gabs, s_gate, s_s0 = sem("decay_rate"), sem("gate_abs"), sem("gates"), sem("sample_state_in")
        LEV = [6, 6, 2]

        def stages(lev):
            mid = [(f"y{k}", f"tu{k}") for k in range(1, lev + 1)]
            return {
                "pe": ["cols", "rows", "beta", "kk", "qk", "kt", "t0", "y1", "vt"] +
                      [n for p in mid for n in p][1:] + ["nw"] + (["ws"] if lev < 6 else []) + ["vn", "o", "s"],
                "dve": ["gb", "cols", "gd", "sub", "min", "st", "bg", "stg", "bm", "u0", "gu", "att", "qd", "kbg", "kd", "vb"] +
                       [n for k in range(1, lev) for n in (f"t{k}", f"u{k}")] + [f"u{lev}", "s"],
                "act": ["kc", "vc", "ex", "exd", "gm", "er", "t0"] + [f"y{k}" for k in range(1, lev + 1)] + ["nw"] +
                       (["ws"] if lev < 6 else []) + ["vn", "o"],
                "pool": [f"bl{k}" for k in range(lev + 1)] + (["sg"] if lev == 6 else []),
            }
        STAGES = [stages(lev) for lev in LEV]
        DONE = [{e: sem(f"tile{x}_{e}") for e in ("pe", "dve", "act", "pool")} for x in range(3)]

        def await_stage(eng, x, who, stage, i=0):
            st = STAGES[x][who]
            eng.wait_ge(DONE[x][who], i * len(st) + (st.index(stage) + 1))

        def done(x, who, ins):
            ins.then_inc(DONE[x][who], 1)

        def shapes(x):
            n = P if x < 2 else NS
            B = {k: at(v, HD) for k, v in TILE[x].items()}
            mat = {k: v[0:n, 0:H * n].rearrange("p (h i) -> p h i", h=H) for k, v in B.items()}
            tok = {k: v[0:n, :].rearrange("p (h d) -> p h d", h=H) for k, v in B.items()}
            feat = {k: v[:, 0:H * n].rearrange("p (h i) -> p h i", h=H) for k, v in B.items()}
            bank = [BK[(4 * x if x < 2 else 0) + k] for k in range(4)]
            pm = [b[0:n, 0:H * n].rearrange("p (h i) -> p h i", h=H) for b in bank]
            pt = [b[0:n, :].rearrange("p (h d) -> p h d", h=H) for b in bank]
            pf = [b[:, 0:H * n].rearrange("p (h i) -> p h i", h=H) for b in bank]
            return n, mat, tok, feat, bank, pm, pt, pf

        def over_heads(m, n):
            return m.unsqueeze(1).to_broadcast([n, H, n])

        def over_dims(col, n):
            return col.unsqueeze(2).to_broadcast([n, H, DH])
        state = ST[0].rearrange("p (h e) -> p h e", h=H)
        decayed = ST[1].rearrange("p (h e) -> p h e", h=H)
        s_kdm, s_kdu, s_sps, s_sns = sems("keys_by_batch", 2), sems("keys_by_batch_used", 2), sem("states_psum"), sem("states_new")
        s_gbj, s_els, s_elp, s_s0d = sem("decay_by_batch"), sem("decay_exp"), sem("decay_psum"), sem("states_decayed")
        s_rec, s_z, s_zs = sem("states_stored"), sems("z_in", 2), sems("z_silu", 2)
        s_osq, s_onp, s_one = sems("out_squares", 2), sems("out_norm_psum", 2), sems("out_norm", 2)
        s_on = sems("out_normed", 2)

        with nc.Block() as block:
            @block.sync
            def _(sp):
                sp.dma_start(SIN, s["PR"][0:A_CH, :, SEQ:T].rearrange("c p t -> p c t")).then_inc(s_si, 16)
                sp.dma_start(SAS, a["SA"]).then_inc(s_si, 16)
                with sp.Fori(0, 4) as i:
                    for b in range(3):
                        chunk = bass.ds(i * 2 + b, 1) if b < 2 else bass.ds(i + 8, 1)
                        sp.wait_ge(s_cv[b], i)
                        sp.dma_start(CI[b][:, 3:CW], s["PR"][chunk, :, :].rearrange("o p n -> p (o n)")).then_inc(s_ci[b], 16)
                sp.dma_start(S0, a["S0"]).then_inc(s_s0, 16)
                for b in range(3):
                    sp.wait_ge(s_cv[b], 4)
                sp.wait_ge(s_cvs, 1)
                sp.dma_start(o["COA"], COAS).then_inc(s_coa, 16)
                await_stage(sp, 1, "dve", "s", 3)
                sp.dma_start(o["REC"], state).then_inc(s_rec, 16)
                sp.wait_ge(s_sns, DEC_B)
                sp.dma_start(o["RECS"], S0).then_inc(s_rec, 16)
                for h in range(H):
                    if h >= 2:
                        sp.wait_ge(s_on[h % 2], h // 2)
                    sp.dma_start(NR[h % 2], s["PR"][PR_Z + h]).then_inc(s_z[h % 2], 16)
                sp.wait_ge(s_rec, 32)

            @block.gpsimd
            def _(pool):
                own = Own(pool, own_g, counts["pool"])

                def blocks_of_level(x, lev, i):
                    n, mat, _, _, _, _, _, _ = shapes(x)
                    await_stage(pool, x, "dve", "bm", i)
                    if lev == 2:
                        await_stage(pool, x, "dve", "u0", i)
                    elif lev > 2:
                        await_stage(pool, x, "pe", f"y{lev - 2}", i)
                    done(x, "pool", pool.tensor_tensor(mat[f"BL{lev % 2}"], mat["BM"], over_heads(C(f"L{lev}", n, n), n), ALU.mult))

                pool.wait_ge(s_coa, 16)
                with pool.Fori(0, NT // 2) as i:
                    for lev in range(LEV[0] + 1):
                        for x in range(2):
                            blocks_of_level(x, lev, i)
                    for x in range(2):
                        if x == 0:
                            pool.wait_ge(DONE[1]["dve"], i * len(STAGES[1]["dve"]))
                        else:
                            await_stage(pool, 0, "dve", "s", i)
                        await_stage(pool, x, "act", "ex", i)
                        done(x, "pool", pool.tensor_tensor(decayed, state, over_dims(SMALL[x]["EX"][:, 4:8], P), ALU.mult))
                for lev in range(LEV[2] + 1):
                    blocks_of_level(2, lev, 0)
                pool.wait_ge(s_els, 1)
                await_stage(pool, 2, "pe", "o")
                for b in range(DEC_B):
                    ins = pool.tensor_tensor(S0[:, b, :, :], S0[:, b, :, :], over_dims(ELS[:, H * b:H * b + H], P), ALU.mult)
                    ins.then_inc(s_s0d, 1)
                counts["pool"] = own.n

            @block.tensor
            def _(pe):
                with pe.Fori(0, 4) as i:
                    for b in range(2):
                        pe.wait_ge(s_sqa[b], i + 1)
                        pe.wait_ge(s_nrt[b], i)
                        for t0, n in TOKENS:
                            last = pe.matmul(PP[b][:, t0:t0 + n], C("ONES"), SQ[b][:, t0:t0 + n], start=True, stop=True)
                        last.then_inc(s_nmp[b], 1)
                for b in range(2):
                    pe.wait_ge(s_nme[b], 4)

                def gates(x, i):
                    n, mat, tok, feat, bank, pm, pt, pf = shapes(x)
                    g = SMALL[x]["GB"][0:n, 0:H]
                    up, last_of = (C("UP"), C("ONES")) if x < 2 else (C("UPS", n, n), C("BLK", n, n))
                    await_stage(pe, x, "dve", "gb", i)
                    pe.matmul(bank[0][0:n, 0:H], up, g, start=True, stop=True)
                    done(x, "pe", pe.matmul(bank[0][0:n, H:2 * H], last_of, g, start=True, stop=True))
                    for h in range(H):
                        last = pe.matmul(pf[1][:, h, :], SMALL[x]["GB"][0:n, h:h + 1].to_broadcast([n, P]), up, start=True, stop=True)
                    done(x, "pe", last)
                    for h in range(H):
                        last = pe.matmul(pm[2][:, h, :], SMALL[x]["GB"][0:n, H + h:H + h + 1].to_broadcast([n, n]), ident[0:n, 0:n],
                                         start=True, stop=True)
                    done(x, "pe", last)
                    await_stage(pe, x, "act", "kc", i)
                    for h in range(H):
                        last = pe.matmul(pm[3][:, h, :], feat["KC"][:, h, :], feat["KC"][:, h, :], start=True, stop=True)
                    done(x, "pe", last)

                def attention(x, i, queries):
                    n, mat, tok, feat, bank, pm, pt, pf = shapes(x)
                    await_stage(pe, x, "dve", "cols", i)
                    for h in range(H):
                        last = pe.matmul(pm[0][:, h, :], feat["KC"][:, h, :], queries(h), start=True, stop=True)
                    done(x, "pe", last)

                def to_tokens(x, i, src, until):
                    n, mat, tok, feat, bank, pm, pt, pf = shapes(x)
                    await_stage(pe, x, "dve", until, i)
                    if src == "VC":
                        await_stage(pe, x, "act", "vc", i)
                    for h in range(H):
                        last = pe.transpose(pt[3][:, h, :], feat[src][:, h, :], ident)
                    done(x, "pe", last)

                def first_inverse(x, i):
                    n, mat, tok, feat, bank, pm, pt, pf = shapes(x)
                    await_stage(pe, x, "dve", "u0", i)
                    await_stage(pe, x, "act", "er", i)
                    for h in range(H):
                        last = pe.transpose(pm[1][:, h, :], mat["UI"][:, h, :], ident[0:n, 0:n])
                    done(x, "pe", last)

                def level_y(x, i, lev):
                    n, mat, tok, feat, bank, pm, pt, pf = shapes(x)
                    await_stage(pe, x, "pool", f"bl{lev}", i)
                    if lev == 1:
                        await_stage(pe, x, "act", "t0", i)
                        await_stage(pe, x, "dve", "att", i)
                    else:
                        await_stage(pe, x, "dve", f"t{lev - 1}", i)
                        await_stage(pe, x, "act", f"y{lev - 1}", i)
                    for h in range(H):
                        last = pe.matmul(pm[0][:, h, :], mat[f"BL{lev % 2}"][:, h, :], mat["TI"][:, h, :], start=True, stop=True)
                    done(x, "pe", last)

                def level_tu(x, i, lev):
                    n, mat, tok, feat, bank, pm, pt, pf = shapes(x)
                    await_stage(pe, x, "act", f"y{lev}", i)
                    if lev == 1:
                        await_stage(pe, x, "dve", "st", i)
                    else:
                        await_stage(pe, x, "dve", f"u{lev - 1}", i)
                    if lev < LEV[x]:
                        for h in range(H):
                            pe.matmul(pm[1][:, h, :], mat["UI"][:, h, :], mat["YS"][:, h, :], start=True, stop=True)
                    for h in range(H):
                        last = pe.matmul(pm[2][:, h, :], mat["YS"][:, h, :], mat["UI"][:, h, :], start=True, stop=True)
                    done(x, "pe", last)

                def key_part(x, i):
                    n, mat, tok, feat, bank, pm, pt, pf = shapes(x)
                    await_stage(pe, x, "dve", f"u{LEV[x]}", i)
                    for h in range(H):
                        last = pe.matmul(pf[3][:, h, :], tok["KBG"][:, h, :], mat["UI"][:, h, :], start=True, stop=True)
                    done(x, "pe", last)

                with pe.Fori(0, NT // 2) as i:
                    for x in range(2):
                        for e in ("act", "dve"):
                            pe.wait_ge(DONE[x][e], i * len(STAGES[x][e]))
                    for x in range(2):
                        gates(x, i)
                    for x in range(2):
                        attention(x, i, lambda h: QKV[:, h, bass.ds(i * 2 * P + x * P, P)])
                    for x in range(2):
                        to_tokens(x, i, "KC", "bm")
                    for x in range(2):
                        first_inverse(x, i)
                    for x in range(2):
                        level_y(x, i, 1)
                    for x in range(2):
                        to_tokens(x, i, "VC", "kd")
                    for x in range(2):
                        level_tu(x, i, 1)
                    for lev in range(2, LEV[0] + 1):
                        for x in range(2):
                            level_y(x, i, lev)
                        for x in range(2):
                            level_tu(x, i, lev)
                    for x in range(2):
                        key_part(x, i)
                    for x in range(2):
                        n, mat, tok, feat, bank, pm, pt, pf = shapes(x)
                        if x == 0:
                            pe.wait_ge(DONE[1]["dve"], i * len(STAGES[1]["dve"]))
                        else:
                            await_stage(pe, 0, "dve", "s", i)
                        await_stage(pe, x, "act", "nw", i)
                        for h in range(H):
                            pe.matmul(pt[0][:, h, :], mat["UI"][:, h, :], tok["VB"][:, h, :], start=True, stop=False)
                            last = pe.matmul(pt[0][:, h, :], feat["NW"][:, h, :], state[:, h, :], start=False, stop=True)
                        done(x, "pe", last)
                        await_stage(pe, x, "act", "vn", i)
                        await_stage(pe, x, "dve", "u6", i)
                        for h in range(H):
                            pe.matmul(pf[1][:, h, :], state[:, h, :], feat["QD"][:, h, :], start=True, stop=False)
                            last = pe.matmul(pf[1][:, h, :], tok["VN"][:, h, :], mat["ATT"][:, h, :], start=False, stop=True)
                        done(x, "pe", last)
                        for h in range(H):
                            last = pe.matmul(pt[2][:, h, :], tok["KDC"][:, h, :], tok["VN"][:, h, :], start=True, stop=True)
                        done(x, "pe", last)

                for x in range(2):
                    for e in ("act", "dve"):
                        pe.wait_ge(DONE[x][e], 4 * len(STAGES[x][e]))
                x = 2
                n, mat, tok, feat, bank, pm, pt, pf = shapes(x)
                gates(x, 0)
                pe.wait_ge(s_gbj, 1)
                pe.matmul(BK[7][:, 0:DEC_B * H], C("ONES", NS, P), GBJ[0:NS, :], start=True, stop=True).then_inc(s_elp, 1)
                attention(x, 0, lambda h: QKV[:, h, SEQ:T])
                to_tokens(x, 0, "KC", "bm")
                first_inverse(x, 0)
                level_y(x, 0, 1)
                to_tokens(x, 0, "VC", "kd")
                level_tu(x, 0, 1)
                level_y(x, 0, 2)
                level_tu(x, 0, 2)
                key_part(x, 0)
                pe.wait_ge(s_s0, 16)
                await_stage(pe, x, "act", "nw")
                for h in range(H):
                    for b in range(DEC_B):
                        last = pe.matmul(pf[0][:, h, b * DEC_T:(b + 1) * DEC_T], S0[:, b, h, :],
                                         feat["NW"][:, h, b * DEC_T:(b + 1) * DEC_T], start=True, stop=True)
                done(x, "pe", last)
                await_stage(pe, x, "act", "ws")
                await_stage(pe, x, "dve", "t1")
                for h in range(H):
                    pe.matmul(pt[1][:, h, :], mat["UI"][:, h, :], tok["VB"][:, h, :], start=True, stop=False)
                    last = pe.matmul(pt[1][:, h, :], feat["YS"][:, h, :], ident, start=False, stop=True)
                done(x, "pe", last)
                await_stage(pe, x, "act", "vn")
                for h in range(H):
                    pe.matmul(pf[2][:, h, :], tok["VN"][:, h, :], mat["ATT"][:, h, :], start=True, stop=False)
                    for b in range(DEC_B):
                        last = pe.matmul(pf[2][:, h, b * DEC_T:(b + 1) * DEC_T], S0[:, b, h, :],
                                         feat["QD"][:, h, b * DEC_T:(b + 1) * DEC_T], start=False, stop=(b == DEC_B - 1))
                done(x, "pe", last)
                for b in range(DEC_B):
                    pe.wait_ge(s_kdm[b % 2], b // 2 + 1)
                    if b >= 2:
                        pe.wait_ge(s_sns, b - 1)
                    for h in range(H):
                        last = pe.matmul(BK[4 + b % 2][:, h * DH:(h + 1) * DH], KDM[b % 2][0:NS, h * DH:(h + 1) * DH], tok["VN"][:, h, :],
                                         start=True, stop=True)
                    last.then_inc(s_sps, 1)
                pe.wait_ge(s_sns, DEC_B)
                for h in range(H):
                    b = h % 2
                    pe.wait_ge(s_osq[b], h // 2 + 1)
                    if h >= 2:
                        pe.wait_ge(s_ort[b], h // 2)
                    for t0, n in TOKENS:
                        last = pe.matmul(PP[b][:, t0:t0 + n], C("ONES"), SQ[b][:, t0:t0 + n], start=True, stop=True)
                    last.then_inc(s_onp[b], 1)

            @block.scalar
            def _(act):
                own = Own(act, own_a, counts["act"])
                act.activation(EXPA, V("alog", 0, H), ACT.Exp).then_inc(s_gexp, 1)
                act.wait_ge(s_gabs, 1)
                own(act.activation(GT1, GT1, ACT.Exp, scale=-1.0))
                own(act.activation(BETA, smw[:, 0:NT + 1, 8:12], ACT.Sigmoid))
                own.settle()
                act.activation(GT1, GT1, ACT.Ln, bias=C("ONES")[:, 0:1]).then_inc(s_gexp, 1)
                act.wait_ge(s_cvs, 1)
                act.activation(QKV[:, :, SEQ:T], CVS.rearrange("p c b t -> p c (b t)"), ACT.Silu).then_inc(s_cvsa, 1)
                act.wait_ge(s_cvsa, 1)
                with act.Fori(0, 4) as i:
                    for b in range(3):
                        act.wait_ge(s_cv[b], i + 1)
                        chunk = bass.ds(i * 2 + b, 1) if b < 2 else bass.ds(i + 8, 1)
                        alone(act)
                        act.activation(QKV[:, chunk, 0:SEQ].rearrange("p o t -> p (o t)"), CV[b], ACT.Silu).then_inc(s_cva[b], 1)
                        if b < 2:
                            alone(act)
                            act.wait_ge(s_nmp[b], i)
                            act.wait_ge(s_cva[b], i + 1)
                            act.activation(SQ[b], QKV[:, chunk, :].rearrange("p o t -> p (o t)"), ACT.Square).then_inc(s_sqa[b], 1)
                    for b in range(2):
                        act.wait_ge(s_nme[b], i)
                        act.wait_ge(s_nmp[b], i + 1)
                        act.activation(RT[b], PP[b][:, 0:T], ACT.Ln, bias=eps).then_inc(s_nrt[b], 1)
                    for b in range(2):
                        act.wait_ge(s_qkn[b], i)
                        act.wait_ge(s_nrt[b], i + 1)
                        act.activation(NR[b], RT[b], ACT.Exp, scale=-0.5).then_inc(s_nme[b], 1)

                def loads(x, i, cols, cols_v):
                    _, _, _, feat, _, _, _, _ = shapes(x)
                    alone(act)
                    done(x, "act", act.activation(feat["KC"], cols, ACT.Copy))
                    done(x, "act", act.activation(feat["VC"], cols_v, ACT.Copy))

                def exponents(x, i):
                    n, mat, tok, feat, bank, pm, pt, pf = shapes(x)
                    sm = SMALL[x]
                    await_stage(act, x, "dve", "cols", i)
                    done(x, "act", act.activation(sm["EX"][0:n, :], sm["GC"][0:n, :], ACT.Exp))
                    await_stage(act, x, "dve", "gd", i)
                    done(x, "act", act.activation(sm["GD"][0:n, H:2 * H], sm["GD"][0:n, 0:H], ACT.Exp))
                    await_stage(act, x, "dve", "min", i)
                    done(x, "act", act.activation(mat["GM"], mat["D"], ACT.Exp))
                    await_stage(act, x, "dve", "sub", i)
                    done(x, "act", act.activation(feat["R"], pf[1], ACT.Exp))

                def copy_out(x, i, stage, dst, src, scale=1.0):
                    await_stage(act, x, "pe", stage, i)
                    if stage == "o":
                        alone(act)
                    done(x, "act", act.activation(dst, src, ACT.Copy, scale=scale))

                act.wait_ge(s_cva[2], 4)
                act.wait_ge(s_coa, 16)
                for b in range(2):
                    act.wait_ge(s_qkn[b], 4)
                with act.Fori(0, NT // 2) as i:
                    for x in range(2):
                        act.wait_ge(DONE[1]["pe"], i * len(STAGES[1]["pe"]))
                        act.wait_ge(DONE[x]["dve"], i * len(STAGES[x]["dve"]))
                        tile = bass.ds(i * 2 * P + x * P, P)
                        loads(x, i, QKV[:, H:2 * H, tile], QKV[:, 2 * H:3 * H, tile])
                    for x in range(2):
                        exponents(x, i)
                    for x in range(2):
                        _, mat, _, feat, _, pm, _, pf = shapes(x)
                        copy_out(x, i, "t0", mat["TI"], pm[1])
                    for lev in range(1, LEV[0] + 1):
                        for x in range(2):
                            _, mat, _, _, _, pm, _, _ = shapes(x)
                            copy_out(x, i, f"y{lev}", mat["YS"], pm[0])
                    for x in range(2):
                        _, _, _, feat, _, _, _, pf = shapes(x)
                        copy_out(x, i, "nw", feat["NW"], pf[3], -1.0)
                    for x in range(2):
                        _, _, tok, feat, _, _, pt, pf = shapes(x)
                        copy_out(x, i, "vn", tok["VN"], pt[0])
                        copy_out(x, i, "o", OA[:, :, bass.ds(i * 2 * P + x * P, P)], pf[1])
                x = 2
                for y in range(2):
                    act.wait_ge(DONE[y]["pe"], 4 * len(STAGES[y]["pe"]))
                    act.wait_ge(DONE[y]["dve"], 4 * len(STAGES[y]["dve"]))
                _, mat, tok, feat, _, pm, pt, pf = shapes(x)
                loads(x, 0, QKV[:, H:2 * H, SEQ:T], QKV[:, 2 * H:3 * H, SEQ:T])
                exponents(x, 0)
                act.wait_ge(s_elp, 1)
                act.activation(ELS, BK[7][:, 0:DEC_B * H], ACT.Exp).then_inc(s_els, 1)
                copy_out(x, 0, "t0", mat["TI"], pm[1])
                for lev in (1, 2):
                    copy_out(x, 0, f"y{lev}", mat["YS"], pm[0])
                copy_out(x, 0, "nw", feat["NW"], pf[3], -1.0)
                copy_out(x, 0, "ws", feat["YS"], pf[0])
                copy_out(x, 0, "vn", tok["VN"], pt[1])
                copy_out(x, 0, "o", OA[:, :, SEQ:T], pf[2])
                await_stage(act, x, "act", "o")
                act.wait_ge(s_sns, DEC_B)
                for h in range(H):
                    b = h % 2
                    if h >= 2:
                        act.wait_ge(s_onp[b], h // 2)
                    act.activation(SQ[b], OA[:, h, :], ACT.Square).then_inc(s_osq[b], 1)
                    act.wait_ge(s_z[b], 16 * (h // 2 + 1))
                    act.activation(NR[b], NR[b], ACT.Silu).then_inc(s_zs[b], 1)
                    if h >= 2:
                        act.wait_ge(s_on[b], h // 2)
                    act.wait_ge(s_onp[b], h // 2 + 1)
                    act.activation(RT[b], PP[b][:, 0:T], ACT.Ln, scale=1.0 / DH, bias=eps).then_inc(s_ort[b], 1)
                    act.wait_ge(s_ort[b], h // 2 + 1)
                    act.activation(RN[b], RT[b], ACT.Exp, scale=-0.5).then_inc(s_one[b], 1)

            @block.vector
            def _(dve):
                own = Own(dve, own_v, counts["dve"])
                own(dve.tensor_tensor(G, smw[:, 0:NT + 1, 12:16], V("dtb", 0, H).unsqueeze(1).to_broadcast([P, NT + 1, H]), ALU.add))
                own.settle()
                dve.scalar_tensor_tensor(out=GT1, in0=G, scalar=-1.0, in1=G, op0=ALU.mult, op1=ALU.max).then_inc(s_gabs, 1)
                dve.wait_ge(s_gabs, 1)
                own(dve.tensor_scalar(G, G, 0.0, None, ALU.max))
                for b in range(3):
                    own(dve.memset(CI[b][:, 0:3], 0.0))
                dve.wait_ge(s_gexp, 2)
                own.settle()
                own(dve.tensor_tensor(G, G, GT1, ALU.add))
                own.settle()
                own(dve.scalar_tensor_tensor(out=G, in0=G, scalar=-1.0, in1=EXPA.unsqueeze(1).to_broadcast([P, NT + 1, H]),
                                             op0=ALU.mult, op1=ALU.mult))
                dve.wait_ge(s_si, 32)
                own(dve.tensor_copy(CIS.rearrange("p c b t -> p (c b) t")[:, :, 3:11], SIN.rearrange("p c (b t) -> p (c b) t", t=DEC_T)))
                own(dve.tensor_copy(CIS.rearrange("p c b t -> p (c b) t")[:, :, 0:3], SAS.rearrange("p c (b t) -> p (c b) t", t=3)))
                own.settle()
                own(dve.tensor_copy(COAS[:, :, 3:27].rearrange("p c (b t) -> p c b t", t=3), CIS[:, :, :, 8:11]))
                taps = V("wa", 0, 4 * A_CH).rearrange("p (c j) -> p c j", j=4)
                for j in range(4):
                    w = taps[:, :, j:j + 1].unsqueeze(3).to_broadcast([P, A_CH, DEC_B, DEC_T])
                    own(dve.tensor_tensor(CVT if j else CVS, CIS[:, :, :, j:j + DEC_T], w, ALU.mult))
                    if j:
                        own.settle()
                        own(dve.tensor_tensor(CVS, CVS, CVT, ALU.add))
                        own.settle()
                own(dve.memset(state, 0.0))
                last = dve.tensor_copy(GBJ[0:NS, :].rearrange("p (b h) -> p b h", h=H), C("BEQ", NS)[:, 0:DEC_B].unsqueeze(2).to_broadcast([NS, DEC_B, H]))
                last.then_inc(s_cvs, 1)
                dve.wait_ge(s_cvs, 1)
                gbj = GBJ[0:NS, :].rearrange("p (b h) -> p b h", h=H)
                dve.tensor_tensor(gbj, gbj, G[0:NS, NT, :].unsqueeze(1).to_broadcast([NS, DEC_B, H]), ALU.mult).then_inc(s_gbj, 1)
                n0 = own.n
                with dve.Fori(0, 4) as i:
                    for b in range(3):
                        dve.wait_ge(s_ci[b], i * 16 + 16)
                        dve.wait_ge(s_cva[b], i)
                        for j in range(4):
                            col = (i * 8 + (4 * b + j)) if b < 2 else (i * 4 + (32 + j))
                            w = vec[:, bass.ds(col + VEC["wa"], 1)]
                            if j == 0:
                                dve.tensor_scalar(CV[b], CI[b][:, 0:SEQ], w, None, ALU.mult).then_inc(own_v, 1)
                                continue
                            dve.wait_ge(own_v, i * 12 + (n0 + 4 * b + j))
                            dve.scalar_tensor_tensor(out=CV[b], in0=CI[b][:, j:j + SEQ], scalar=w, in1=CV[b],
                                                     op0=ALU.mult, op1=ALU.add).then_inc(own_v, 1)
                        chunk = bass.ds(i * 2 + b, 1) if b < 2 else bass.ds(i + 8, 1)
                        dve.tensor_scalar(COAS[:, chunk, 0:3].rearrange("p o t -> p (o t)"), CI[b][:, SEQ:SEQ + 3], 1.0, None, ALU.mult).then_inc(s_cv[b], 1)
                    for b in range(2):
                        dve.wait_ge(s_nme[b], i + 1)
                        q = QKV[:, bass.ds(i * 2 + b, 1), :].rearrange("p o t -> p (o t)")
                        dve.tensor_tensor(q, q, NR[b], ALU.mult).then_inc(s_qkn[b], 1)
                own.n = n0 + 48
                for b in range(2):
                    dve.wait_ge(s_qkn[b], 4)

                own.settle()

                def gate_columns(x, i, tile):
                    sm, n = SMALL[x], shapes(x)[0]
                    done(x, "dve", dve.tensor_scalar(sm["GB"][0:n, :].rearrange("p (k h) -> p k h", h=H),
                                                     GATES[0:n, :, tile, :].rearrange("p k o h -> p k (o h)"), 1.0, None, ALU.mult))

                def decays(x, i):
                    n, mat, tok, feat, bank, pm, pt, pf = shapes(x)
                    sm = SMALL[x]
                    await_stage(dve, x, "pe", "cols", i)
                    done(x, "dve", dve.tensor_copy(sm["GC"][0:n, :], bank[0][0:n, 0:2 * H]))
                    await_stage(dve, x, "dve", "cols", i)
                    done(x, "dve", dve.tensor_tensor(sm["GD"][0:n, 0:H], sm["GC"][0:n, H:2 * H], sm["GC"][0:n, 0:H], ALU.subtract))
                    await_stage(dve, x, "pe", "rows", i)
                    done(x, "dve", dve.tensor_tensor(mat["D"], pm[1][0:n], sm["GC"][0:n, 0:H].unsqueeze(2).to_broadcast([n, H, n]), ALU.subtract))
                    await_stage(dve, x, "dve", "sub", i)
                    done(x, "dve", dve.tensor_scalar(mat["D"], mat["D"], 0.0, None, ALU.min))
                    await_stage(dve, x, "pe", "beta", i)
                    done(x, "dve", dve.tensor_tensor(mat["BM"], pm[2], over_heads(C("ST" if x < 2 else "STS", n, n), n), ALU.mult))

                def couplings(x, i):
                    n, mat, tok, feat, bank, pm, pt, pf = shapes(x)
                    sm = SMALL[x]
                    await_stage(dve, x, "act", "ex", i)
                    done(x, "dve", dve.tensor_tensor(sm["BG"][0:n, 0:H], sm["GB"][0:n, H:2 * H], sm["EX"][0:n, 0:H], ALU.mult))
                    await_stage(dve, x, "act", "gm", i)
                    await_stage(dve, x, "dve", "st", i)
                    done(x, "dve", dve.tensor_tensor(mat["BM"], mat["BM"], mat["GM"], ALU.mult))
                    await_stage(dve, x, "pe", "kk", i)
                    await_stage(dve, x, "dve", "stg", i)
                    done(x, "dve", dve.tensor_tensor(mat["BM"], mat["BM"], pm[3], ALU.mult))

                def first_inverse(x, i):
                    n, mat, tok, feat, bank, pm, pt, pf = shapes(x)
                    await_stage(dve, x, "pool", "bl0", i)
                    done(x, "dve", dve.tensor_tensor(mat["UI"], over_heads(ident[0:n, 0:n], n), mat["BL0"], ALU.subtract))

                def attention(x, i, queries):
                    n, mat, tok, feat, bank, pm, pt, pf = shapes(x)
                    done(x, "dve", dve.tensor_tensor(mat["D"], mat["GM"], over_heads(C("UP" if x < 2 else "UPS", n, n), n), ALU.mult))
                    await_stage(dve, x, "pe", "qk", i)
                    await_stage(dve, x, "dve", "gu", i)
                    done(x, "dve", dve.scalar_tensor_tensor(out=mat["ATT"], in0=pm[0], scalar=DH ** -0.5, in1=mat["D"], op0=ALU.mult, op1=ALU.mult))
                    await_stage(dve, x, "act", "er", i)
                    done(x, "dve", dve.scalar_tensor_tensor(out=feat["QD"], in0=queries, scalar=DH ** -0.5, in1=feat["R"], op0=ALU.mult, op1=ALU.mult))

                def keys(x, i):
                    n, mat, tok, feat, bank, pm, pt, pf = shapes(x)
                    sm = SMALL[x]
                    await_stage(dve, x, "pe", "kt", i)
                    await_stage(dve, x, "dve", "bg", i)
                    done(x, "dve", dve.tensor_tensor(tok["KBG"], pt[3], over_dims(sm["BG"][0:n, 0:H], n), ALU.mult))
                    await_stage(dve, x, "act", "exd", i)
                    done(x, "dve", dve.tensor_tensor(tok["KDC"], pt[3], over_dims(sm["GD"][0:n, H:2 * H], n), ALU.mult))

                def values(x, i):
                    n, mat, tok, feat, bank, pm, pt, pf = shapes(x)
                    await_stage(dve, x, "pe", "vt", i)
                    done(x, "dve", dve.tensor_tensor(tok["VB"], pt[3], over_dims(SMALL[x]["GB"][0:n, H:2 * H], n), ALU.mult))

                def doubling(x, i, lev):
                    n, mat, tok, feat, bank, pm, pt, pf = shapes(x)
                    await_stage(dve, x, "pe", f"tu{lev}", i)
                    if lev < LEV[x]:
                        done(x, "dve", dve.tensor_tensor(mat["TI"], mat["TI"], pm[1], ALU.subtract))
                    done(x, "dve", dve.tensor_tensor(mat["UI"], mat["UI"], pm[2], ALU.subtract))

                with dve.Fori(0, NT // 2) as i:
                    for x in range(2):
                        for e in ("pe", "act"):
                            dve.wait_ge(DONE[x][e], i * len(STAGES[x][e]))
                        dve.wait_ge(DONE[x]["dve"], i * len(STAGES[x]["dve"]))
                    for x in range(2):
                        gate_columns(x, i, bass.ds(i * 2 + x, 1))
                    for x in range(2):
                        decays(x, i)
                    for x in range(2):
                        couplings(x, i)
                    for x in range(2):
                        first_inverse(x, i)
                    for x in range(2):
                        attention(x, i, QKV[:, 0:H, bass.ds(i * 2 * P + x * P, P)])
                    for x in range(2):
                        keys(x, i)
                    for x in range(2):
                        values(x, i)
                    for lev in range(1, LEV[0] + 1):
                        for x in range(2):
                            doubling(x, i, lev)
                    for x in range(2):
                        await_stage(dve, x, "pe", "s", i)
                        await_stage(dve, x, "pool", "sg", i)
                        done(x, "dve", dve.tensor_tensor(state, decayed, shapes(x)[6][2], ALU.add))
                x = 2
                n, mat, tok, feat, bank, pm, pt, pf = shapes(x)
                for y in range(2):
                    for e in ("pe", "act", "dve"):
                        dve.wait_ge(DONE[y][e], 4 * len(STAGES[y][e]))
                gate_columns(x, 0, slice(NT, NT + 1))
                decays(x, 0)
                couplings(x, 0)
                first_inverse(x, 0)
                attention(x, 0, QKV[:, 0:H, SEQ:T])
                keys(x, 0)
                values(x, 0)
                for lev in (1, 2):
                    doubling(x, 0, lev)
                await_stage(dve, x, "dve", "kd")
                for b in range(DEC_B + 2):
                    if b < DEC_B:
                        if b >= 2:
                            dve.wait_ge(s_sps, b - 1)
                        dve.tensor_scalar(KDM[b % 2][0:NS, :], at(TILE[x]["KDC"], HD)[0:NS, :], C("BEQ", NS)[:, b:b + 1], None,
                                          ALU.mult).then_inc(s_kdm[b % 2], 1)
                    if b >= 2:
                        k = b - 2
                        dve.wait_ge(s_sps, k + 1)
                        dve.wait_ge(s_s0d, k + 1)
                        dve.tensor_tensor(S0[:, k, :, :], S0[:, k, :, :], BK[4 + k % 2].rearrange("p (h e) -> p h e", h=H), ALU.add).then_inc(s_sns, 1)
                for h in range(H):
                    b = h % 2
                    dve.wait_ge(s_zs[b], h // 2 + 1)
                    own(dve.scalar_tensor_tensor(out=OA[:, h, :], in0=OA[:, h, :], scalar=V("gn"), in1=NR[b], op0=ALU.mult, op1=ALU.mult))
                    dve.wait_ge(s_one[b], h // 2 + 1)
                    own.settle()
                    dve.tensor_tensor(OA[:, h, :], OA[:, h, :], RN[b], ALU.mult).then_inc(s_on[b], 1)
                for b in range(2):
                    dve.wait_ge(s_on[b], 2)
                counts["dve"] = own.n

        end_phase()

        top[0] = work2
        QF = at(take(H * T), H * T).rearrange("p (h t) -> p h t", h=H)
        KF = at(take(H * T), H * T).rearrange("p (h t) -> p h t", h=H)
        bias_at, v_at = take(H * SEQ), take(NT * HD)
        BIAS = at(bias_at, H * SEQ).rearrange("p (h j) -> p h j", h=H)
        VT = at(v_at, NT * HD).rearrange("p (t n) -> p t n", n=HD)
        EQ = at(bias_at, N_BUCKETS * P).rearrange("p (m n) -> p m n", m=N_BUCKETS)
        EQR = at(v_at, N_BUCKETS * P).rearrange("p (m n) -> p m n", m=N_BUCKETS)
        VSN = at(take(HD), HD)
        VG = [at(take(4096), 4096).rearrange("p (n d) -> p n d", d=HD) for _ in range(2)]
        ISC2 = [at(take(8), 8, I32) for _ in range(2)]
        PDM2 = at(take(4), 4)
        LG = [at(take(REV), REV) for _ in range(2)]
        PTB = [at(take(SEQ), SEQ).rearrange("p (k n) -> p k n", n=P) for _ in range(2)]
        NM, RS = at(take(4), 4), at(take(4), 4)
        SPT = at(take(HD), HD)
        PNT = at(take(H * NS), H * NS)
        SRW = TOPK + DEC_T
        SR = at(take(H * SRW), H * SRW)[0:NS, :].rearrange("p (h k) -> p h k", h=H)
        HOT, TOES = at(take(REV), REV), [LG[0], at(take(REV), REV)]
        RELB = at(take(H), H)
        BKT, MNG, SBI = at(take(P), P), at(take(P), P), at(take(HD), HD)
        lo = slice(0, NS)
        NX = at(take(H * NS), H * NS)[lo, :].rearrange("p (h b t) -> p h b t", h=H, b=DEC_B)
        BN = at(take(H * 64), H * 64)[lo, :].rearrange("p (h t m) -> p h t m", h=H, t=DEC_T)
        BNR = at(take(H * DEC_T), H * DEC_T)[lo, :].rearrange("p (h t) -> p h t", h=H)
        DQ = at(take(DEC_T), DEC_T)[lo, :]
        SM4 = at(take(8), 8)[lo, :]
        assert top[0] <= ARENA, top[0]

        s_rel, s_qkf, s_toep, s_toc, s_toe = sem("bias_rows_in"), sem("q_k_in"), sem("bias_psum"), sem("bias_row"), sems("bias_row_stored", 2)
        s_bd, s_bt, s_kps, s_nd = sem("sample_bias"), sem("bias_and_values_in"), sem("k_stored"), sem("new_dots")
        s_lg2, s_srp, s_sx, s_se, s_sp = sem("sample_logits"), sem("sample_rows"), sem("sample_shifted"), sem("sample_exp"), sem("sample_probs")
        s_ptp, s_pt2, s_nv, s_nvc = sem("sample_probs_psum"), sem("sample_probs_by_key"), sem("new_values"), sem("new_values_out")
        s_vgi, s_vgu = sems("values_in", 2), sems("values_used", 2)
        s_lgp, s_lgr, s_mx, s_ex, s_pn = sem("logits_psum"), sem("logits_read"), sem("maximum"), sem("exp_done"), sem("probs")
        s_tp, s_tc, s_ov, s_oc = sem("probs_transposed"), sem("probs_by_key"), sem("out_psum"), sem("out_copied")
        STEPS = [(i, h) for i in range(NT) for h in range(H)]
        NU = len(STEPS)
        ASCALE = DH ** -0.5

        with nc.Block() as block:
            @block.sync
            def _(sp):
                sp.dma_start(HOT[0:N_BUCKETS, :], a["HOT"]).then_inc(s_rel, 16)
                sp.dma_start(RELB[0:N_BUCKETS, :], a["RELB"]).then_inc(s_rel, 16)
                sp.dma_start(QF, s["PR"][PR_Q:PR_Q + H].rearrange("c p t -> p c t")).then_inc(s_qkf, 16)
                sp.dma_start(KF, s["PR"][PR_K:PR_K + H].rearrange("c p t -> p c t")).then_inc(s_qkf, 16)
                for h in range(H):
                    sp.wait_ge(s_toc, h + 1)
                    sp.dma_start(s["TOE"][h], TOES[h % 2]).then_inc(s_toe[h % 2], 16)
                for b in range(2):
                    sp.wait_ge(s_toe[b], 16 * H // 2)
                sp.wait_ge(s_bd, 1)
                sp.dma_start(BIAS, bass.AP(s["TOE"].tensor, P - 1, [[REV - 1, P], [P * REV, H], [1, SEQ]])).then_inc(s_bt, 16)
                sp.dma_start(VT, o["VP"].rearrange("(t p) n -> p t n", p=P)).then_inc(s_bt, 16)
                sp.dma_start(VSN[0:NS, :], o["VS"]).then_inc(s_bt, 16)
                sp.wait_ge(s_qkf, 32)
                sp.dma_start(o["KP"].rearrange("h p t -> p h t"), KF[:, :, 0:SEQ]).then_inc(s_kps, 16)
                sp.wait_ge(s_kps, 16)

            @block.gpsimd
            def _(pool):
                own = Own(pool, own_g, counts["pool"])
                gather_rows(pool, own, VG, "CV", s_vgi, s_vgu, ISC2, PDM2)
                counts["pool"] = own.n

            @block.tensor
            def _(pe):
                pe.wait_ge(s_rel, 32)
                for h in range(H):
                    if h >= 2:
                        pe.wait_ge(s_toc, h - 1)
                    for t0, n in ((0, 512), (512, 512), (1024, P)):
                        last = pe.matmul(PP[h % 2][:, t0:t0 + n], RELB[0:N_BUCKETS, h:h + 1].to_broadcast([N_BUCKETS, P]),
                                         HOT[0:N_BUCKETS, t0:t0 + n], start=True, stop=True)
                    last.then_inc(s_toep, 1)
                pe.wait_ge(s_qkf, 32)
                pe.wait_ge(s_toc, H)
                for h in range(H):
                    last = pe.matmul(BK[3][0:NS, h * NS:(h + 1) * NS], QF[:, h, SEQ:T], KF[:, h, SEQ:T], start=True, stop=True)
                last.then_inc(s_nd, 1)
                pe.wait_ge(s_lg2, 1)
                by_head = lgs.rearrange("p (f q h) -> p f h q", f=2, h=H)
                for h in range(H):
                    for f in range(2):
                        last = pe.transpose(psum[0:NS, 2048 + h * TOPK + f * P:2048 + h * TOPK + (f + 1) * P], by_head[:, f, h, :], ident)
                last.then_inc(s_srp, 1)
                pe.wait_ge(s_sp, 1)
                for f in range(2):
                    for h in range(H):
                        c = (f * H + h) * NS
                        pe.transpose(BK[0][:, c:c + NS], SR[:, h, f * P:(f + 1) * P], ident[0:NS, 0:NS])
                for h in range(H):
                    last = pe.transpose(BK[1][0:NS, h * NS:(h + 1) * NS], NX[:, h].rearrange("p b t -> p (b t)"), ident[0:NS, 0:NS])
                last.then_inc(s_ptp, 1)
                pe.wait_ge(s_pt2, 1)
                pe.wait_ge(s_bt, 48)
                for h in range(H):
                    last = pe.matmul(BK[7][:, h * NS:(h + 1) * NS], VSN[0:NS, h * DH:(h + 1) * DH], PNT[0:NS, h * NS:(h + 1) * NS],
                                     start=True, stop=True)
                last.then_inc(s_nv, 1)

                def logits(u):
                    i, h = STEPS[u]
                    if u >= 2:
                        pe.wait_ge(s_lgr, u - 1)
                    L = P * (i + 1)
                    for k0 in range(0, L, 512):
                        n = min(512, L - k0)
                        c = 1024 * (u % 2) + k0
                        last = pe.matmul(psum[:, c:c + n], QF[:, h, i * P:(i + 1) * P], KF[:, h, k0:k0 + n], start=True, stop=True)
                    last.then_inc(s_lgp, 1)

                def to_keys(u):
                    pe.wait_ge(s_pn, u + 1)
                    if u:
                        pe.wait_ge(s_tc, u)
                    for k in range(STEPS[u][0] + 1):
                        last = pe.transpose(psum[:, 2048 + k * P:2048 + (k + 1) * P], LG[u % 2][:, k * P:(k + 1) * P], ident)
                    last.then_inc(s_tp, 1)

                def weighted_values(u):
                    i, h = STEPS[u]
                    pe.wait_ge(s_tc, u + 1)
                    if u:
                        pe.wait_ge(s_oc, u)
                    for k in range(i + 1):
                        last = pe.matmul(BK[6][:, 0:P], VT[:, k, h * DH:(h + 1) * DH], PTB[u % 2][:, k, :], start=(k == 0), stop=(k == i))
                    last.then_inc(s_ov, 1)

                def sample_values(g):
                    pe.wait_ge(s_vgi[g % 2], P * (g // 2 + 1))
                    for q in range(4):
                        for h in range(H):
                            for f in range(2):
                                c, w = h * NS + 4 * g + q, (f * H + h) * NS + 4 * g + q
                                last = pe.matmul(BK[7][:, c:c + 1], VG[g % 2][:, 2 * q + f, h * DH:(h + 1) * DH], SPT[:, w:w + 1],
                                                 start=(f == 0), stop=(f == 1))
                    last.then_inc(s_vgu[g % 2], 1)

                pe.wait_ge(s_nvc, 1)
                logits(0)
                for u in range(NU + 2):
                    if u + 1 < NU:
                        logits(u + 1)
                    if 1 <= u <= NU:
                        to_keys(u - 1)
                    if u >= 2:
                        weighted_values(u - 2)
                    if u % 2 and u < NU:
                        sample_values(u // 2)

            @block.scalar
            def _(act):
                for h in range(H):
                    act.wait_ge(s_toep, h + 1)
                    if h >= 2:
                        act.wait_ge(s_toe[h % 2], 16)
                    act.activation(TOES[h % 2], PP[h % 2][:, 0:REV], ACT.Copy).then_inc(s_toc, 1)
                act.wait_ge(s_sx, 1)
                act.activation(SR, SR, ACT.Exp).then_inc(s_se, 1)
                act.wait_ge(s_ptp, 1)
                act.activation(SPT, BK[0], ACT.Copy)
                act.activation(PNT[0:NS, :], BK[1][0:NS, 0:H * NS], ACT.Copy).then_inc(s_pt2, 1)
                act.wait_ge(s_nv, 1)
                act.activation(OB[:, :, SEQ:T], BK[7][:, 0:H * NS].rearrange("p (h q) -> p h q", h=H), ACT.Copy).then_inc(s_nvc, 1)
                for u in range(NU + 2):
                    if u < NU:
                        L = P * (STEPS[u][0] + 1)
                        act.wait_ge(s_mx, u + 1)
                        act.activation(LG[u % 2][:, 0:L], LG[u % 2][:, 0:L], ACT.Exp, bias=NM[:, 2 * (u % 2) + 1:2 * (u % 2) + 2],
                                       accum_out=RS[:, 2 * (u % 2):2 * (u % 2) + 1]).then_inc(s_ex, 1)
                    if 1 <= u <= NU:
                        v = u - 1
                        L = P * (STEPS[v][0] + 1)
                        if v >= 2:
                            act.wait_ge(s_ov, v - 1)
                        act.wait_ge(s_tp, v + 1)
                        act.activation(PTB[v % 2].rearrange("p k n -> p (k n)")[:, 0:L], psum[:, 2048:2048 + L], ACT.Copy).then_inc(s_tc, 1)
                    if u >= 2:
                        v = u - 2
                        i, h = STEPS[v]
                        act.wait_ge(s_ov, v + 1)
                        act.activation(OB[:, h, i * P:(i + 1) * P], BK[6][:, 0:P], ACT.Copy).then_inc(s_oc, 1)

            @block.vector
            def _(dve):
                own = Own(dve, own_v, counts["dve"])
                own(dve.memset(BKT, 0.0))
                n0 = own.n
                with dve.Fori(0, N_BUCKETS - 1) as m:
                    dve.wait_ge(own_v, m + n0)
                    dve.scalar_tensor_tensor(out=BKT, in0=dist_t, scalar=const[:, bass.ds(m + C_AT["THR"], 1)], in1=BKT,
                                             op0=ALU.is_ge, op1=ALU.add).then_inc(own_v, 1)
                own.n = n0 + N_BUCKETS - 1
                own.settle()
                buckets = C("THR")[:, N_BUCKETS:2 * N_BUCKETS]
                own(dve.tensor_tensor(EQ, BKT.unsqueeze(1).to_broadcast([P, N_BUCKETS, P]),
                                      buckets.unsqueeze(2).to_broadcast([P, N_BUCKETS, P]), ALU.is_equal))
                own(dve.tensor_scalar(MNG, dist_t, 0.0, NEG, ALU.is_lt, ALU.mult))
                own.settle()
                for h in range(H):
                    rb = V("rb", h * N_BUCKETS, N_BUCKETS).unsqueeze(2).to_broadcast([P, N_BUCKETS, P])
                    own(dve.tensor_tensor(EQR, EQ, rb, ALU.mult))
                    own.settle()
                    own(dve.tensor_reduce(SBI.rearrange("p (h n) -> p h n", h=H)[:, h, :], EQR.rearrange("p m n -> p n m"), AX.X, ALU.add))
                    own.settle()
                lgv = lgs.rearrange("p (n h) -> p n h", h=H)
                own(dve.scalar_tensor_tensor(out=lgv, in0=lgv, scalar=ASCALE, in1=SBI.rearrange("p (h n) -> p n h", h=H), op0=ALU.mult, op1=ALU.add))
                own.settle()
                dve.tensor_tensor(lgv, lgv, MNG.unsqueeze(2).to_broadcast([P, P, H]), ALU.add).then_inc(s_lg2, 1)
                dve.wait_ge(s_lg2, 1)
                dve.wait_ge(s_nd, 1)
                blk = C("BLK", NS, NS).rearrange("p (b t) -> p b t", b=DEC_B)
                own(dve.tensor_tensor(NX, BK[3][lo, 0:H * NS].rearrange("p (h b t) -> p h b t", h=H, b=DEC_B),
                                      blk.unsqueeze(1).to_broadcast([NS, H, DEC_B, DEC_T]), ALU.mult))
                own(dve.tensor_scalar(DQ, C("THR", NS)[:, N_BUCKETS:N_BUCKETS + DEC_T], -1.0, qpos, ALU.mult, ALU.add))
                own.settle()
                own(dve.tensor_scalar(DQ, DQ, float(-PAST), None, ALU.add))
                new_lg = SR[:, :, TOPK:SRW]
                own(dve.tensor_reduce(new_lg, NX.rearrange("p h b t -> p h t b"), AX.X, ALU.add))
                own.settle()
                own(dve.tensor_tensor(BN, DQ.unsqueeze(1).unsqueeze(3).to_broadcast([NS, H, DEC_T, DEC_T]),
                                      C("THR", NS)[:, N_BUCKETS:N_BUCKETS + DEC_T].unsqueeze(1).unsqueeze(1).to_broadcast([NS, H, DEC_T, DEC_T]), ALU.is_equal))
                own.settle()
                rbn = V("rb", 0, H * N_BUCKETS)[lo, :].rearrange("p (h m) -> p h m", h=H)[:, :, 0:DEC_T]
                own(dve.tensor_tensor(BN, BN, rbn.unsqueeze(2).to_broadcast([NS, H, DEC_T, DEC_T]), ALU.mult))
                own.settle()
                own(dve.tensor_reduce(BNR, BN, AX.X, ALU.add))
                own.settle()
                own(dve.scalar_tensor_tensor(out=new_lg, in0=new_lg, scalar=ASCALE, in1=BNR, op0=ALU.mult, op1=ALU.add))
                own.settle()
                own(dve.tensor_tensor(new_lg, new_lg, new_sel[lo, :].unsqueeze(1).to_broadcast([NS, H, DEC_T]), ALU.add))
                dve.wait_ge(s_srp, 1)
                own(dve.tensor_copy(SR[:, :, 0:TOPK], psum[lo, 2048:3072].rearrange("p (h k) -> p h k", h=H)))
                own.settle()
                own(dve.tensor_reduce(SM4[:, 0:H], SR, AX.X, ALU.max))
                own.settle()
                dve.tensor_tensor(SR, SR, SM4[:, 0:H].unsqueeze(2).to_broadcast([NS, H, SRW]), ALU.subtract).then_inc(s_sx, 1)
                dve.wait_ge(s_se, 1)
                own(dve.tensor_reduce(SM4[:, 0:H], SR, AX.X, ALU.add))
                own.settle()
                own(dve.reciprocal(SM4[:, H:2 * H], SM4[:, 0:H]))
                own.settle()
                own(dve.tensor_tensor(SR, SR, SM4[:, H:2 * H].unsqueeze(2).to_broadcast([NS, H, SRW]), ALU.mult))
                own.settle()
                dve.tensor_tensor(NX, SR[:, :, TOPK:SRW].unsqueeze(2).to_broadcast([NS, H, DEC_B, DEC_T]),
                                  blk.unsqueeze(1).to_broadcast([NS, H, DEC_B, DEC_T]), ALU.mult).then_inc(s_sp, 1)
                dve.tensor_copy(DQ, DQ).then_inc(s_bd, 1)

                def normalise(u):
                    L, b = P * (STEPS[u][0] + 1), u % 2
                    dve.wait_ge(s_ex, u + 1)
                    own(dve.reciprocal(RS[:, 2 * b + 1:2 * b + 2], RS[:, 2 * b:2 * b + 1]))
                    own.settle()
                    dve.tensor_scalar(LG[b][:, 0:L], LG[b][:, 0:L], RS[:, 2 * b + 1:2 * b + 2], None, ALU.mult).then_inc(s_pn, 1)

                dve.wait_ge(s_bt, 48)
                for u in range(NU + 1):
                    if u < NU:
                        i, h = STEPS[u]
                        L, b = P * (i + 1), u % 2
                        lg = LG[b][:, 0:L]
                        dve.wait_ge(s_lgp, u + 1)
                        if u >= 2:
                            dve.wait_ge(s_tp, u - 1)
                        dve.scalar_tensor_tensor(out=lg, in0=psum[:, 1024 * b:1024 * b + L], scalar=ASCALE, in1=BIAS[:, h, SEQ - L:SEQ],
                                                 op0=ALU.mult, op1=ALU.add).then_inc(s_lgr, 1)
                        dve.wait_ge(s_lgr, u + 1)
                        own(dve.tensor_tensor(lg, lg, mask[:, mask_at[i]:mask_at[i] + L], ALU.add))
                        own.settle()
                        own(dve.tensor_reduce(NM[:, 2 * b:2 * b + 1], lg, AX.X, ALU.max))
                        own.settle()
                        dve.tensor_scalar(NM[:, 2 * b + 1:2 * b + 2], NM[:, 2 * b:2 * b + 1], -1.0, None, ALU.mult).then_inc(s_mx, 1)
                    if u >= 1:
                        normalise(u - 1)
                for b in range(2):
                    dve.wait_ge(s_vgu[b], 8)
                own(dve.tensor_tensor(OB[:, :, SEQ:T], OB[:, :, SEQ:T], BK[7][:, 0:H * NS].rearrange("p (h q) -> p h q", h=H), ALU.add))
                own.settle()
                counts["dve"] = own.n

        end_phase()

        PADW = 2 + SEQ + DEC_B * (DEC_T + 2)
        OUTW = PADW - 2
        top[0] = work
        OA = at(take(H * T), H * T).rearrange("p (h t) -> p h t", t=T)
        OB = at(take(H * T), H * T).rearrange("p (h t) -> p h t", t=T)
        XN2 = at(work, KD * T).rearrange("p (k t) -> p k t", t=T)
        wpa, wpb = take(H * DM), take(H * DM)
        WP = [at(w, H * DM).rearrange("p (k n) -> p k n", n=DM) for w in (wpa, wpb)]
        MG = at(take(KD * T), KD * T).rearrange("p (k t) -> p k t", t=T)
        sg = take(4 * T)
        SG = [[at(sg + (2 * m + b) * T, T) for b in range(2)] for m in range(2)]
        WO = [at(take(4096), 4096).rearrange("p (k n) -> p k n", n=512), at(wpa, 4096).rearrange("p (k n) -> p k n", n=512)]
        SQ2 = [at(sg + b * T, T) for b in range(2)]
        SUM, RT2, RN2 = [at(wpb + k * T, T) for k in range(3)]
        top[0] = work2
        HH = at(take(FC * T), FC * T).rearrange("p (c t) -> p c t", t=T)
        wu = take(2 * 2048)
        WU = [at(wu + b * 2048, 2048).rearrange("p (k n) -> p k n", n=2 * P) for b in range(2)]
        tail = take(0)
        X1 = at(ARENA - KD * T, KD * T).rearrange("p (k t) -> p k t", t=T)
        PADS = [[at(take(PADW), PADW) for b in range(2)] for m in range(2)]
        CVG = [at(take(OUTW), OUTW) for b in range(2)]
        CVV = at(take(OUTW), OUTW)
        SFS = at(take(2 * FC * 2 * DEC_B), 2 * FC * 2 * DEC_B).rearrange("p (c t) -> p c t", t=2 * DEC_B)
        COFS = at(take(2 * FC * 18), 2 * FC * 18).rearrange("p (c t) -> p c t", t=18)
        STEP = at(take(8), 8)
        assert top[0] <= ARENA, top[0]
        WD = [at(work + b * FC * P, FC * P).rearrange("p (k n) -> p k n", n=P) for b in range(2)]
        SQ3 = [at(work + 2 * FC * P + b * T, T) for b in range(2)]
        SUM3, RT3, RN3 = [at(wu + k * T, T) for k in range(3)]
        X2 = X1
        assert 2 * FC * P + 2 * T <= 2 * H * T and 3 * T <= 4096

        def sample_of(pad):
            return pad[:, 2 + SEQ:PADW].rearrange("p (b t) -> p b t", b=DEC_B)

        def by_sample(out):
            return out[:, SEQ:SEQ + DEC_B * (DEC_T + 2)].rearrange("p (b t) -> p b t", b=DEC_B)[:, :, 2:2 + DEC_T]

        s_wp, s_sgi, s_mul, s_mg = sem("merge_weights_in"), sems("gates_in", 2), sem("gated"), sem("merged")
        s_wo, s_x1, s_x1s = sems("out_weights_in", 2), sem("x_again"), sem("x1_stored")
        s_f, s_e = sems("pp_full_", 2), sems("pp_free_", 2)
        s_q2, s_s2, s_r2, s_n2 = sem("squares2"), sem("squares_added2"), sem("root2"), sem("normed2")
        s_wu, s_sf, s_cg, s_cvv, s_sl, s_h = sems("up_weights_in", 2), sem("ffn_state_in"), sems("gate_conv", 2), sems("value_conv", 2), sems("gate_silu", 2), sem("hidden")
        s_cof, s_wd, s_x1r = sem("ffn_state_stored"), sems("down_weights_in", 2), sem("x1_again")
        s_q3, s_s3, s_r3, s_y, s_yo = sem("squares3"), sem("squares_added3"), sem("root3"), sem("y"), sem("y_stored")
        U_UP, U_DN = (KD + KD // 2 + 1, KD + KD // 2), (KD + KD // 2 + 1 + FC, KD + KD // 2 + FC)

        with nc.Block() as block:
            @block.sync
            def _(sp):
                for m, n in enumerate(("WPA", "WPB")):
                    sp.dma_start(WP[m], a[n]).then_inc(s_wp, 16)
                for c in range(KD):
                    b = c % 2
                    if c >= 2:
                        sp.wait_ge(s_mg, c - 1)
                    for m, first in ((0, PR_GA), (1, PR_GB)):
                        sp.dma_start(SG[m][b], s["PR"][first + c]).then_inc(s_sgi[b], 16)
                    if c == 1:
                        sp.dma_start(WO[0], a["WO"][0].rearrange("p (k n) -> p k n", n=512)).then_inc(s_wo[0], 16)
                        sp.dma_start(X1, a["X"]).then_inc(s_x1, 16)
                sp.wait_ge(s_f[0], KD)
                sp.dma_start(WO[1], a["WO"][1].rearrange("p (k n) -> p k n", n=512)).then_inc(s_wo[1], 16)
                for b in range(2):
                    sp.wait_ge(s_e[b], KD + KD // 2)
                sp.dma_start(s["X1"].rearrange("k p t -> p k t"), X1).then_inc(s_x1s, 16)
                with sp.Fori(0, FC // 2) as i:
                    for b in range(2):
                        sp.wait_ge(s_f[1], i * 2 + (U_UP[1] + b - 1))
                        sp.dma_start(WU[b], a["WUP"][bass.ds(i * 2 + b, 1), :, :].rearrange("o p n -> p (o n)")
                                     .rearrange("p (k n) -> p k n", n=2 * P)).then_inc(s_wu[b], 16)
                sp.wait_ge(s_f[1], U_DN[1])
                sp.wait_ge(s_h, FC)
                sp.dma_start(o["COF"], COFS).then_inc(s_cof, 16)
                with sp.Fori(0, KD // 2) as i:
                    for b in range(2):
                        sp.wait_ge(s_f[b], i + U_DN[b])
                        sp.dma_start(WD[b], a["WDN"][bass.ds(i * 2 + b, 1), :, :].rearrange("o p n -> p (o n)")
                                     .rearrange("p (k n) -> p k n", n=P)).then_inc(s_wd[b], 16)
                for c in range(KD):
                    sp.wait_ge(s_y, c + 1)
                    sp.dma_start(o["Y"][c], X2[:, c, :]).then_inc(s_yo, 16)
                sp.wait_ge(s_yo, 16 * KD)

            @block.gpsimd
            def _(pool):
                pool.wait_ge(s_x1s, 16)
                pool.wait_ge(s_n2, KD)
                pool.dma_start(SFS, a["SF"]).then_inc(s_sf, 16)
                pool.wait_ge(s_cof, 16)
                pool.dma_start(X2, s["X1"].rearrange("k p t -> p k t")).then_inc(s_x1r, 16)

            @block.tensor
            def _(pe):
                uses = [0, 0]

                def project(b, K, weights, rhs, used=None):
                    n = uses[b] if used is None else used
                    if used is not None or n:
                        pe.wait_ge(s_e[b], n)
                    for k in range(K):
                        for t0, n in TOKENS:
                            last = pe.matmul(PP[b][:, t0:t0 + n], weights(k), rhs(k)[:, t0:t0 + n], start=(k == 0), stop=(k == K - 1))
                    last.then_inc(s_f[b], 1)
                    uses[b] += 1

                pe.wait_ge(s_wp, 32)
                for c in range(KD):
                    for m, out in enumerate((OA, OB)):
                        project(m, H, lambda k: WP[m][:, k, c * P:(c + 1) * P], lambda k: out[:, k, :])
                pe.wait_ge(s_mg, KD)
                for c in range(KD):
                    if c % 4 == 0:
                        pe.wait_ge(s_wo[c // 4], 16)
                    project(c % 2, KD, lambda k: WO[c // 4][:, k, (c % 4) * P:(c % 4 + 1) * P], lambda k: MG[:, k, :])
                pe.wait_ge(s_s2, KD - 1)
                project(0, 1, lambda k: C("ONES"), lambda k: SUM)
                pe.wait_ge(s_n2, KD)
                with pe.Fori(0, FC // 2) as i:
                    for b in range(2):
                        pe.wait_ge(s_wu[b], i * 16 + 16)
                        for m in range(2):
                            project(m, KD, lambda k: WU[b][:, k, m * P:(m + 1) * P], lambda k: XN2[:, k, :], i * 2 + (U_UP[m] + b))
                pe.wait_ge(s_h, FC)
                with pe.Fori(0, KD // 2) as i:
                    for b in range(2):
                        pe.wait_ge(s_wd[b], i * 16 + 16)
                        project(b, FC, lambda k: WD[b][:, k, :], lambda k: HH[:, k, :], i + U_DN[b])
                uses[:] = [U_DN[0] + KD // 2, U_DN[1] + KD // 2]
                pe.wait_ge(s_s3, KD - 1)
                project(0, 1, lambda k: C("ONES"), lambda k: SUM3)

            @block.scalar
            def _(act):
                def squares(X, used, SQ, SUM, s_q, s_s, s_r, RT):
                    for c in range(KD):
                        act.wait_ge(s_e[c % 2], used[c % 2] + c // 2 + 1)
                        if c >= 3:
                            act.wait_ge(s_s, c - 2)
                        act.activation(SQ[c % 2] if c else SUM, X[:, c, :], ACT.Square).then_inc(s_q, 1)
                    act.wait_ge(s_f[0], used[0] + KD // 2 + 1)
                    act.activation(RT, PP[0][:, 0:T], ACT.Sqrt, scale=1.0 / DM, bias=eps).then_inc(s_r, 1)

                act.wait_ge(s_f[1], KD)
                squares(X1, (KD, KD), SQ2, SUM, s_q2, s_s2, s_r2, RT2)
                act.wait_ge(s_x1s, 16)
                act.wait_ge(s_sf, 16)
                with act.Fori(0, FC // 2) as i:
                    for b in range(2):
                        for m, s_c in enumerate((s_cg, s_cvv)):
                            act.wait_ge(s_c[b], i)
                            act.wait_ge(s_f[m], i * 2 + (U_UP[m] + b + 1))
                            act.activation(PADS[m][b][:, 2:2 + SEQ], PP[m][:, 0:SEQ], ACT.Copy)
                            act.activation(sample_of(PADS[m][b])[:, :, 2:2 + DEC_T], PP[m][:, SEQ:T].rearrange("p (b t) -> p b t", b=DEC_B),
                                           ACT.Copy).then_inc(s_e[m], 1)
                        alone(act)
                        act.wait_ge(s_cg[b], i + 1)
                        act.activation(CVG[b], CVG[b], ACT.Silu, bias=vec[:, bass.ds(i * 2 + (VEC["bf"] + b), 1)]).then_inc(s_sl[b], 1)
                squares(X2, U_DN, SQ3, SUM3, s_q3, s_s3, s_r3, RT3)

            @block.vector
            def _(dve):
                own = Own(dve, own_v, counts["dve"])

                def add_squares(c, SQ, SUM, s_q, s_s):
                    dve.wait_ge(s_q, c + 1)
                    if c > 1:
                        dve.wait_ge(s_s, c - 1)
                    dve.tensor_tensor(SUM, SUM, SQ[c % 2], ALU.add).then_inc(s_s, 1)

                for c in range(KD):
                    b = c % 2
                    dve.wait_ge(s_sgi[b], 32 * (c // 2 + 1))
                    for m in range(2):
                        dve.wait_ge(s_f[m], c + 1)
                        dve.tensor_tensor(SG[m][b], PP[m][:, 0:T], SG[m][b], ALU.mult).then_inc(s_e[m], 1)
                    for m in range(2):
                        dve.wait_ge(s_e[m], c + 1)
                    dve.tensor_tensor(MG[:, c, :], SG[0][b], SG[1][b], ALU.add).then_inc(s_mg, 1)
                dve.wait_ge(s_x1, 16)
                for c in range(KD):
                    dve.wait_ge(s_f[c % 2], KD + c // 2 + 1)
                    dve.tensor_tensor(X1[:, c, :], X1[:, c, :], PP[c % 2][:, 0:T], ALU.add).then_inc(s_e[c % 2], 1)
                    if c >= 2:
                        add_squares(c - 1, SQ2, SUM, s_q2, s_s2)
                add_squares(KD - 1, SQ2, SUM, s_q2, s_s2)
                dve.wait_ge(s_r2, 1)
                dve.reciprocal(RN2, RT2).then_inc(s_e[0], 1)
                dve.wait_ge(s_e[0], U_UP[0])
                for c in range(KD):
                    dve.scalar_tensor_tensor(out=XN2[:, c, :], in0=X1[:, c, :], scalar=V("g2", c), in1=RN2, op0=ALU.mult, op1=ALU.mult).then_inc(s_n2, 1)
                dve.wait_ge(s_x1s, 16)
                dve.wait_ge(s_n2, KD)
                dve.wait_ge(s_sf, 16)
                for m in range(2):
                    for b in range(2):
                        own(dve.memset(PADS[m][b][:, 0:2], 0.0))
                own.settle()
                n0 = own.n
                with dve.Fori(0, FC // 2) as i:
                    for b in range(2):
                        for m, s_c in enumerate((s_cg, s_cvv)):
                            pad, out = PADS[m][b], CVG[b] if m == 0 else CVV
                            chunk = bass.ds(i * 2 + (m * FC + b), 1)
                            k0 = n0 + 8 * b + 4 * m
                            if m == 1:
                                dve.wait_ge(s_h, i * 2 + b)
                            else:
                                dve.wait_ge(s_sl[b], i)
                            dve.wait_ge(own_v, i * 16 + k0)
                            dve.tensor_scalar(sample_of(pad)[:, :, 0:2], SFS[:, chunk, :].rearrange("p o (b t) -> p (o b) t", t=2), 1.0, None,
                                              ALU.mult).then_inc(own_v, 1)
                            dve.wait_ge(s_e[m], i * 2 + (U_UP[m] + b + 1))
                            dve.wait_ge(own_v, i * 16 + (k0 + 1))
                            dve.tensor_scalar(COFS[:, chunk, 2:18].rearrange("p o (b t) -> p (o b) t", t=2), sample_of(pad)[:, :, DEC_T:DEC_T + 2],
                                              1.0, None, ALU.mult)
                            dve.tensor_scalar(COFS[:, chunk, 0:2].rearrange("p o t -> p (o t)"), pad[:, SEQ:SEQ + 2], 1.0, None, ALU.mult)
                            for j in range(3):
                                w = vec[:, bass.ds(i * 6 + (VEC["wf"] + 3 * (m * FC + b) + j), 1)]
                                if j == 0:
                                    ins = dve.tensor_scalar(out, pad[:, 0:OUTW], w, None, ALU.mult)
                                else:
                                    dve.wait_ge(own_v, i * 16 + (k0 + 1 + j))
                                    ins = dve.scalar_tensor_tensor(out=out, in0=pad[:, j:j + OUTW], scalar=w, in1=out, op0=ALU.mult, op1=ALU.add)
                                ins.then_inc(s_c[b] if j == 2 else own_v, 1)
                            dve.wait_ge(s_c[b], i + 1)
                            dve.tensor_scalar(STEP, C("ONES")[:, 0:8], 1.0, None, ALU.mult).then_inc(own_v, 1)
                        dve.wait_ge(s_sl[b], i + 1)
                        chunk = bass.ds(i * 2 + b, 1)
                        bias = vec[:, bass.ds(i * 2 + (VEC["bf"] + FC + b), 1)]
                        dve.scalar_tensor_tensor(out=HH[:, chunk, 0:SEQ].rearrange("p o t -> p (o t)"), in0=CVV[:, 0:SEQ], scalar=bias,
                                                 in1=CVG[b][:, 0:SEQ], op0=ALU.add, op1=ALU.mult)
                        dve.scalar_tensor_tensor(out=HH[:, chunk, SEQ:T].rearrange("p o (b t) -> p (o b) t", t=DEC_T), in0=by_sample(CVV), scalar=bias,
                                                 in1=by_sample(CVG[b]), op0=ALU.add, op1=ALU.mult).then_inc(s_h, 1)
                own.n = n0 + 16 * (FC // 2)
                own.settle()
                dve.wait_ge(s_x1r, 16)
                for c in range(KD):
                    dve.wait_ge(s_f[c % 2], U_DN[c % 2] + c // 2 + 1)
                    dve.tensor_tensor(X2[:, c, :], X2[:, c, :], PP[c % 2][:, 0:T], ALU.add).then_inc(s_e[c % 2], 1)
                    if c >= 2:
                        add_squares(c - 1, SQ3, SUM3, s_q3, s_s3)
                add_squares(KD - 1, SQ3, SUM3, s_q3, s_s3)
                dve.wait_ge(s_r3, 1)
                own(dve.reciprocal(RN3, RT3))
                own.settle()
                for c in range(KD):
                    dve.scalar_tensor_tensor(out=X2[:, c, :], in0=X2[:, c, :], scalar=V("gf", c), in1=RN3, op0=ALU.mult, op1=ALU.mult).then_inc(s_y, 1)


def lay_out(i):
    f = {n: np.ascontiguousarray(np.asarray(v)) for n, v in i.items()}

    def rows(w):
        return w.reshape(-1, P, w.shape[1]).transpose(1, 0, 2)

    def groups(w, n):
        return w.reshape(-1, P, w.shape[1] // n, n).transpose(2, 1, 0, 3).reshape(w.shape[1] // n, P, -1)
    w_in = f["w_in"][0]
    o_qkva, o_small, o_z, o_qkvb = 0, 1536, 1544, 2056
    o_qi, o_ki, o_wi, o_g = 3592, 4104, 4168, 4176
    x = np.concatenate([f["x_prompt"].reshape(SEQ, DM), f["x_sample"].reshape(NS, DM)])
    const, comb, onehot = shape_constants()

    def cols(v, n):
        return v.reshape(n, P).T
    wf = f["conv_f_w"][0].reshape(3, 2 * FC, P).transpose(2, 1, 0).reshape(P, -1)
    wa = f["conv_a_w"][0].reshape(4, A_CH, P).transpose(2, 1, 0).reshape(P, -1)
    vec = np.concatenate([
        cols(f["norm1_g"][0], KD), cols(f["norm2_g"][0], KD), cols(f["final_g"], KD), f["norm_a_g"][0][:, None],
        wa, wf, cols(f["conv_f_b"][0], 2 * FC), np.broadcast_to(f["a_log"][0], (P, H)),
        np.broadcast_to(f["dt_bias"][0], (P, H)), np.broadcast_to(f["rel_bias"].T.reshape(-1), (P, H * N_BUCKETS))], axis=1)
    pt = f["page_table"]
    w_up = f["w_up"][0]
    pairs = np.stack([w_up[:, :FF].reshape(DM, FC, P), w_up[:, FF:].reshape(DM, FC, P)], axis=2).reshape(DM, 2 * FF)
    m = {
        "CONST": const, "VEC": vec, "COMB": comb, "HOT": onehot, "RELB": f["rel_bias"],
        "X": rows(x.T.copy()),
        "WIX": rows(np.concatenate([w_in[:, o_qi:o_qi + 512], w_in[:, o_ki:o_ki + 64], w_in[:, o_ki:o_ki + 64]], axis=1)),
        "WSM": rows(np.concatenate([w_in[:, o_wi:o_wi + 8], w_in[:, o_small:o_small + 8]], axis=1)),
        "WG": groups(np.concatenate([w_in[:, o_qkva:o_qkva + 1536], w_in[:, o_z:o_z + 512], w_in[:, o_qkvb:o_qkvb + 1536],
                                     w_in[:, o_g:o_g + 2048]], axis=1), 512),
        "CI": f["cache_idx_k"].reshape(CI_ROWS, 1024),
        "CK": f["cache_k"].reshape(CK_ROWS, 512), "CV": f["cache_v"].reshape(CK_ROWS, 512),
        "PTI": pt.reshape(4, P).T, "PTR": np.repeat(pt, DEC_T, axis=0),
        "WPA": rows(f["w_proj_a"][0]), "WPB": rows(f["w_proj_b"][0]), "WO": groups(f["w_out"][0], 512),
        "WUP": groups(pairs, 256), "WDN": groups(f["w_down"][0], P),
        "SA": f["state_a_conv"][0].reshape(DEC_B * 3, A_CH, P).transpose(2, 1, 0),
        "SF": f["state_ffn_conv"][0].reshape(DEC_B * 2, 2 * FC, P).transpose(2, 1, 0),
        "S0": f["state_a_rec"][0].transpose(2, 0, 1, 3),
    }
    return {n: np.ascontiguousarray(v) for n, v in m.items()}


OUTS = {
    "Y": (KD, P, T), "KP": (H, P, SEQ), "KS": (NS, 512), "VP": (SEQ, 512), "VS": (NS, 512), "KIDX": (DI, T),
    "COA": (P, A_CH, 3 + 3 * DEC_B), "REC": (P, H, DH), "RECS": (P, DEC_B, H, DH), "COF": (P, 2 * FC, 2 + 2 * DEC_B),
}
SCRATCH = {"PR": (PR_N, P, T), "X1": (KD, P, T), "QS": (NS, 512), "TOE": (H, P, REV)}


def build(nc, arrays):
    a = {n: nc.dram_tensor(f"in_{n}", v.shape, mybir.dt.from_np(v.dtype), kind="ExternalInput").ap() for n, v in arrays.items()}
    o = {n: nc.dram_tensor(f"out_{n}", shape, F32, kind="ExternalOutput").ap() for n, shape in OUTS.items()}
    s = {n: nc.dram_tensor(f"tmp_{n}", shape, F32, kind="Internal").ap() for n, shape in SCRATCH.items()}
    program(nc, a, o, s)


def kernel(**inputs):
    import concourse.bacc as bacc
    from concourse.bass_utils import run_bass_kernel_spmd
    arrays = lay_out(inputs)
    nc = bacc.Bacc("TRN2", target_bir_lowering=False, num_devices=1)
    build(nc, arrays)
    r = run_bass_kernel_spmd(nc, [{f"in_{n}": v for n, v in arrays.items()}], core_ids=[0]).results[0]
    g = {n: np.asarray(r[f"out_{n}"]) for n in OUTS}
    y = g["Y"].reshape(DM, T).T
    kp = g["KP"].reshape(512, SEQ).T
    ca = g["COA"].transpose(2, 1, 0).reshape(3 + 3 * DEC_B, -1)
    cf = g["COF"].transpose(2, 1, 0).reshape(2 + 2 * DEC_B, -1)
    ki = g["KIDX"].T
    out = (
        y[:SEQ].reshape(1, SEQ, DM), y[SEQ:].reshape(DEC_B, DEC_T, DM),
        kp.reshape(1, 1, SEQ, H, DH), g["VP"].reshape(1, 1, SEQ, H, DH), ki[:SEQ].reshape(1, 1, SEQ, DI),
        ca[:3].reshape(1, 1, 3, -1), g["REC"].transpose(1, 0, 2).reshape(1, 1, H, DH, DH), cf[:2].reshape(1, 1, 2, -1),
        g["KS"].reshape(1, DEC_B, DEC_T, H, DH), g["VS"].reshape(1, DEC_B, DEC_T, H, DH), ki[SEQ:].reshape(1, DEC_B, DEC_T, DI),
        ca[3:].reshape(1, DEC_B, 3, -1), g["RECS"].transpose(1, 2, 0, 3).reshape(1, DEC_B, H, DH, DH),
        cf[2:].reshape(1, DEC_B, 2, -1),
    )
    return tuple(np.ascontiguousarray(v) for v in out)
```

```python
from contextlib import ExitStack

import numpy as np
import concourse.bass as bass
from concourse import mybir

F32 = mybir.dt.float32
F32R = mybir.dt.float32r
BF16 = mybir.dt.bfloat16
I32 = mybir.dt.int32
U32 = mybir.dt.uint32
ALU = mybir.AluOpType
ACT = mybir.ActivationFunctionType
AX = mybir.AxisListType

P = 128
DM, SEQ, DEC_B, DEC_T = 1024, 1024, 8, 8
NS = DEC_B * DEC_T
T = SEQ + NS
KD = DM // P
H, DH = 4, 128
HI, DI = 8, 64
PAST, PAGE = 8192, 128
N_PAGES = PAST // PAGE
TOPK = 256
NT = SEQ // P
FF = 2816
FC = FF // P
EPS = 1e-6
N_BUCKETS, MAX_DIST = 32, 2048
CK_ROWS = 640 * PAGE
CI_ROWS = 640 * 8
ARENA = 53000
NEG, MARK = -1e30, -3e38
FAR = 1e6
TOKENS = [(0, 512), (512, 512), (1024, NS)]
A_CH = 3 * H
PR_Z, PR_Q, PR_K, PR_GA, PR_GB, PR_N = 12, 16, 20, 24, 32, 40
REV = SEQ + P
VEC = {}


def _vec_columns():
    at = 0
    for name, n in (("g1", KD), ("g2", KD), ("gf", KD), ("gn", 1), ("wa", 4 * A_CH), ("wf", 3 * 2 * FC),
                    ("bf", 2 * FC), ("alog", H), ("dtb", H), ("rb", H * N_BUCKETS)):
        VEC[name] = at
        at += n
    return at


N_VEC = _vec_columns()

CONSTS = ["IDN", "ONES", "UP", "UPS", "ST", "STS", "BLK", "CAU", "NEW", "L0", "L1", "L2", "L3", "L4", "L5", "L6",
          "THR", "BEQ", "IOT"]
C_AT = {n: i * P for i, n in enumerate(CONSTS)}
N_CONST = len(CONSTS) * P
BASE = N_CONST + N_VEC + 160 + 3 * 80 + 2304 + 2 * P + DEC_T + 512 + KD * T


def bucket_of(d):
    d = np.maximum(d, 0)
    half = N_BUCKETS // 2
    nf = np.maximum(d, half).astype(np.float64)
    large = half + (np.log(nf / half) / np.log(MAX_DIST / half) * (N_BUCKETS - half) + 1e-9).astype(np.int64)
    return np.where(d < half, d, np.minimum(large, N_BUCKETS - 1))


def shape_constants():
    j, i = np.meshgrid(np.arange(P), np.arange(P), indexing="ij")
    c = {n: np.zeros((P, P), np.float32) for n in CONSTS}
    c["IDN"] = (j == i)
    c["ONES"] = np.ones((P, P))
    c["UP"] = (j <= i)
    inb = (j < NS) & (i < NS) & (j // DEC_T == i // DEC_T)
    c["UPS"] = (j <= i) & inb
    c["ST"] = (j < i)
    c["STS"] = (j < i) & inb
    c["BLK"] = inb
    c["CAU"] = np.where(i <= j, 0.0, NEG)
    q = j - NS
    c["NEW"] = np.where((j >= NS) & (i < NS) & (q // DEC_T == i // DEC_T) & (i <= q), 0.0, NEG)
    for lev in range(7):
        s = 1 << lev
        c[f"L{lev}"] = (j // (2 * s) == i // (2 * s)) & ((i // s) % 2 == 1) & ((j // s) % 2 == 0)
    dist = np.arange(PAST + DEC_T)
    b = bucket_of(dist)
    thr = np.array([np.argmax(b >= m) for m in range(1, N_BUCKETS)] + [3e9])
    row = np.zeros(P)
    row[0:N_BUCKETS] = thr
    row[N_BUCKETS:2 * N_BUCKETS] = np.arange(N_BUCKETS)
    c["THR"] = np.broadcast_to(row, (P, P)).copy()
    p = np.arange(P)
    c["THR"][:, 64] = EPS
    c["THR"][:, 65] = 8192 + (p % DEC_T)
    c["THR"][:, 66] = DEC_T * ((p % NS) // DEC_T)
    c["THR"][:, 67] = p // NS
    c["IOT"] = i
    c["BEQ"][:NS, :DEC_B] = (p[:NS, None] // DEC_T == np.arange(DEC_B))
    c["BEQ"][:NS, 64:128] = (p[:NS, None] % DEC_T == (np.arange(64) % DEC_T))
    const = np.concatenate([np.asarray(c[n], np.float32) for n in CONSTS], axis=1)
    r = np.arange(P)
    col = np.arange(DEC_B * P)
    cb, cpar, cb2, ct = col // P, (col % P) // NS, (col % NS) // DEC_T, col % DEC_T
    comb = ((r[:, None] // NS == cpar) & (r[:, None] % DEC_T == ct) & (cb == cb2)).astype(np.float32)
    onehot = np.zeros((N_BUCKETS, REV), np.float32)
    y = np.arange(REV)
    onehot[bucket_of(SEQ - 1 - y), y] = 1.0
    return const, comb, onehot


def program(nc, a, o, s):
    with ExitStack() as ctx:
        def sb(name, n, dt=F32, parts=P):
            return ctx.enter_context(nc.sbuf_tensor(name, [parts, n], dt))

        def lasting(name):
            return ctx.enter_context(nc.semaphore(name))

        phase = []

        def sem(name):
            phase.append(nc.alloc_semaphore(name))
            return phase[-1]

        def end_phase():
            nc.all_engine_barrier()
            nc.clear_and_free_semaphores(phase)
            nc.all_engine_barrier()
            phase.clear()

        def sems(name, n):
            return [sem(f"{name}{k}") for k in range(n)]

        base = sb("base", BASE)
        early = ctx.enter_context(ExitStack())
        rest = early.enter_context(nc.sbuf_tensor("rest", [P, ARENA - BASE], F32))
        psum = ctx.enter_context(nc.psum_tensor("psum", [P, 4096], F32))

        def at(off, n, dt=F32):
            assert off + n <= BASE or off >= BASE, (off, n)
            v = base[:, off:off + n] if off < BASE else rest[:, off - BASE:off - BASE + n]
            return v if dt == F32 else v.bitcast(dt)

        PP = [psum[:, 0:1536], psum[:, 1536:3072]]
        BK = [psum[:, k * 512:(k + 1) * 512] for k in range(8)]

        top = [0]

        def take(n):
            top[0] += n
            return top[0] - n

        const = at(take(N_CONST), N_CONST)
        vec = at(take(N_VEC), N_VEC)

        def C(name, rows=P, cols=P):
            return const[0:rows, C_AT[name]:C_AT[name] + cols]

        def V(name, k=0, n=1):
            return vec[:, VEC[name] + k:VEC[name] + k + n]

        def column(k, rows=P):
            return const[0:rows, C_AT["THR"] + k:C_AT["THR"] + k + 1]
        eps, qpos, newat, parity = column(64), column(65, NS), column(66, NS), column(67)
        ident = C("IDN")
        smw = at(take(160), 160).rearrange("p (t c) -> p t c", c=16)
        wabs = at(take(80), 80).rearrange("p (t c) -> p t c", c=8)
        wsgn = at(take(80), 80).rearrange("p (t c) -> p t c", c=8)
        ws = at(take(80), 80).rearrange("p (t c) -> p t c", c=8)
        mask = at(take(2304), 2304, BF16)
        mask_at = [P * (i * (i + 1) // 2) for i in range(NT)]
        idx_cache = at(take(P), P, I32)
        new_sel = at(take(DEC_T), DEC_T)
        dist_t = at(take(P), P)
        lgs = at(take(512), 512)
        work = top[0]
        assert work + KD * T == BASE

        XN = at(take(KD * T), KD * T).rearrange("p (k t) -> p k t", t=T)
        QI = at(take(4 * T), 4 * T).rearrange("p (c t) -> p c t", t=T)
        KI = at(take(T), T)
        wb = take(4096)
        wb2 = take(KD * 640)
        WB = [at(w, 4096).rearrange("p (k n) -> p k n", n=512) for w in (wb, wb2)]
        WIX = at(wb2, KD * 640).rearrange("p (k n) -> p k n", n=640)
        WSM = at(take(KD * 16), KD * 16).rearrange("p (k n) -> p k n", n=16)
        stg = take(4 * T)
        STG = [at(stg + b * T, T) for b in range(4)]
        VST = [at(take(512), 512) for b in range(2)]
        z = take(KD * T)
        X = at(z, KD * T).rearrange("p (k t) -> p k t", t=T)
        SCW = PAST // 2 + NS
        SC = at(z, SCW)
        QB = at(z + SCW, 1024).rearrange("p (b n) -> p b n", n=P)
        CM = at(z + SCW + 1024, 1024).rearrange("p (b n) -> p b n", n=P)
        KT = [at(z + SCW + 2048 + b * 1024, 1024).rearrange("p (o n) -> p o n", n=P) for b in range(2)]
        assert SCW + 4096 <= KD * T
        RP = [at(z + b * 1024, 1024) for b in range(2)]
        WK = [at(z + 2048 + b * 1024, 1024) for b in range(2)]
        pg = take(4096)
        PG = [at(pg + b * 1024, 1024).rearrange("p (o n) -> p o n", n=P) for b in range(4)]
        names = ["LV", "LI", "BV", "BI", "LA", "LB", "KEY", "KPG", "KOF", "KNEW", "ACC", "LT1", "LT2", "LT3"]
        LST = {n: at(pg + k * TOPK, TOPK) for k, n in enumerate(names)}
        assert len(names) * TOPK <= 4096
        EQ4 = at(pg, 4 * TOPK)[0:NS, :].rearrange("p (k n) -> p k n", n=TOPK)
        kg2 = take(4096)
        RL = [at(kg2 + b * 512, 512) for b in range(2)]
        PTI = at(kg2 + 1024, 4, I32)
        PIX = at(kg2 + 1032, 32, I32)
        PIF = at(kg2 + 1064, 4)
        WLT = at(kg2 + 1072, P)
        WCOL = at(kg2 + 1200, 8)
        NK = at(kg2 + 1216, 512)
        PTR = at(kg2 + 1728, N_PAGES)
        PTRI = at(kg2 + 1792, N_PAGES, I32)
        KINT = at(kg2 + 1856, TOPK, I32)
        M8 = at(take(8), 8)
        MI8 = at(take(8), 8, U32)
        DMY = at(take(8), 8)
        KG = [at(z + 4096, 4096).rearrange("p (n d) -> p n d", d=512), at(kg2, 4096).rearrange("p (n d) -> p n d", d=512)]
        QBC = [at(pg + b * 2048, 2048) for b in range(2)]
        QKS = at(take(512), 512).rearrange("p (c t) -> p c t", t=NS)
        ISC = [at(take(8), 8, I32) for b in range(2)]
        PDM = at(take(4), 4)
        LG8 = at(take(32), 32)
        assert top[0] <= ARENA, top[0]

        own_a, own_v, own_g, s_const = lasting("own_act"), lasting("own_dve"), lasting("own_pool"), lasting("consts_in")
        s_wix, s_x = sem("idx_weights_in"), sems("x_in", 4)
        s_sq, s_sqmm, s_std, s_xn = sem("squares"), sem("squares_summed"), sem("deviation"), sem("normed")
        s_full, s_free = sems("pp_full", 2), sems("pp_free", 2)
        s_sm, s_smc, s_wl, s_wcolp, s_wcol = sem("small"), sem("small_out"), sem("wl"), sem("wcol_psum"), sem("wcol")
        s_kidx = sem("kidx_stored")
        s_cmd, s_cm, s_qb = sem("comb_in"), sem("comb"), sem("qb")
        s_pt, s_pix, s_pg = sem("page_table_in"), sem("page_rows"), sems("pages_in", 4)
        s_ktp, s_kte, s_dot, s_dotp = sem("kt_psum"), sems("kt_out", 2), sems("dots_done", 2), sems("dots_psum", 2)
        s_rle, s_cmb, s_sce = sems("relu_out", 2), sems("combined", 2), sem("scores_out")
        s_nk, s_nke = sem("new_scores_psum"), sem("new_scores_out")
        s_load, _, s_sto = sems("weights_in", 2), None, sems("stored", 4)
        s_vps, s_vst, s_vo = sem("v_psum"), sems("v_staged", 2), sems("v_stored", 2)
        s_qks, s_qkp, s_qke, s_qso = sem("qk_sample_in"), sem("qk_sample_psum"), sem("qk_sample_out"), sem("qk_sample_stored")
        s_ptr, s_lists, s_ltp, s_idx = sem("page_rows_in"), sem("lists"), sem("lists_psum"), sem("indices")
        s_lg, s_rpe, s_rpu = sem("prompt_dots"), sems("prompt_relu", 2), sems("prompt_relu_used", 2)
        s_kgi, s_kgm, s_kgu = sems("keys_in", 2), sems("keys_times_queries", 2), sems("keys_summed", 2)
        s_qbc = sems("queries_in", 2)
        N_A = 6
        s_gp, s_gat = sem("gates_psum"), sem("gates_out")
        GATES_FIRST = 4
        BESIDE = {3: "kgkg", 5: "kgkgkgkgkk", 7: "kgkgkgkgkkggkk"}
        assert "".join(BESIDE.values()).count("g") == 16 - GATES_FIRST and "".join(BESIDE.values()).count("k") == 16
        U0 = 3

        class Own:

            def __init__(self, eng, s, n=0):
                self.eng, self.s, self.n = eng, s, n

            def __call__(self, ins):
                ins.then_inc(self.s, 1)
                self.n = self.n + 1
                return ins

            def settle(self):
                self.eng.wait_ge(self.s, self.n)

        def gather_rows(pool, own, ring, cache, s_in, s_u, isc, pdm, beside=None, then=None):
            own(pool.memset(pdm, 0.0))
            for b in range(2):
                own(pool.memset(ring[b], 0.0))
            n0 = own.n

            def carry(k):
                pool.wait_ge(own_g, i * 6 + (n0 + k))
                pool.tensor_tensor(pdm[:, 2:4], pdm[:, 0:2], pdm[:, 0:2], ALU.add).then_inc(own_g, 1)

            with pool.Fori(0, 8) as i:
                for b in range(2):
                    pool.wait_ge(s_u[b], i)
                    carry(3 * b)
                    pool.tensor_copy(isc[b], idx_cache[:, bass.ds(i * 16 + 8 * b, 8)]).then_inc(own_g, 1)
                    carry(3 * b + 2)
                    if beside:
                        beside(i, b)
                    for n in range(8):
                        pool.indirect_dma_start(out=ring[b][:, n, :], out_offset=None, in_=a[cache],
                                                in_offset=bass.IndirectOffsetOnAxis(ap=isc[b][:, n:n + 1], axis=0),
                                                bounds_check=CK_ROWS - 1, oob_is_err=False).then_inc(s_in[b], 16)
                if then:
                    for b in range(2):
                        then(i, b)
            own.n = n0 + 48

        def alone(eng):
            eng.wait_ge(s_const, 32)

        counts = {}

        with nc.Block() as block:
            @block.sync
            def _(sp):
                for q in range(4):
                    sp.dma_start(X[:, 2 * q:2 * q + 2, :], a["X"][:, 2 * q:2 * q + 2, :]).then_inc(s_x[q], 16)
                sp.dma_start(WIX, a["WIX"]).then_inc(s_wix, 16)
                sp.dma_start(WSM, a["WSM"]).then_inc(s_wix, 16)
                sp.dma_start(WB[0], a["WG"][0]).then_inc(s_load[0], 16)
                sp.wait_ge(s_xn, KD)
                sp.dma_start(CM, a["COMB"]).then_inc(s_cmd, 16)
                sp.wait_ge(s_free[1], 3)
                sp.dma_start(o["KIDX"], KI[0:DI, :]).then_inc(s_kidx, 16)
                sp.wait_ge(s_sm, 1)
                sp.dma_start(WB[1], a["WG"][1]).then_inc(s_load[1], 16)
                with sp.Fori(0, N_A // 2) as i:
                    for b in range(2):
                        for c in range(4):
                            sp.wait_ge(s_free[c % 2], i * 4 + (U0 + 2 * b + c // 2 + 1))
                            sp.dma_start(s["PR"][bass.ds(i * 8 + (4 * b + c), 1), :, :].rearrange("o p n -> p (o n)"),
                                         STG[c]).then_inc(s_sto[c], 16)
                        sp.wait_ge(s_full[1], i * 4 + (U0 + 2 * b + 2))
                        sp.dma_start(WB[b], a["WG"][bass.ds(i * 2 + (b + 2), 1), :, :].rearrange("o p n -> p (o n)")
                                     .rearrange("p (k n) -> p k n", n=512)).then_inc(s_load[b], 16)
                for c in range(4):
                    sp.wait_ge(s_sto[c], 16 * N_A)
                sp.dma_start(QKS, s["PR"][PR_Q:PR_Q + 8, :, SEQ:T].rearrange("c p t -> p c t")).then_inc(s_qks, 16)
                for t in range(NT + 1):
                    sp.wait_ge(s_vst[t % 2], t // 2 + 1)
                    dst = o["VP"][t * P:(t + 1) * P, :] if t < NT else o["VS"]
                    rows = P if t < NT else NS
                    sp.dma_start(dst, VST[t % 2][0:rows, :]).then_inc(s_vo[t % 2], 16)
                sp.wait_ge(s_vps, NT + 1)
                sp.dma_start(WB[0], a["WG"][8].rearrange("p (k n) -> p k n", n=512)).then_inc(s_load[0], 16)
                for b, dst in ((0, s["QS"]), (1, o["KS"])):
                    sp.wait_ge(s_qke, b + 1)
                    sp.dma_start(dst, VST[b][0:NS, :]).then_inc(s_qso, 16)
                sp.wait_ge(s_sce, 8)
                sp.dma_start(PTRI[0:NS, :], a["PTR"]).then_inc(s_ptr, 16)
                for g in range(4):
                    for c in range(4):
                        sp.wait_ge(s_gat, 4 * g + c + 1)
                        sp.dma_start(s["PR"][PR_GA + 4 * g + c], STG[c]).then_inc(s_sto[c], 16)
                    if g < 2:
                        b = (g + 1) % 2
                        sp.dma_start(WB[b], a["WG"][9 + g].rearrange("p (k n) -> p k n", n=512)).then_inc(s_load[b], 16)
                sp.wait_ge(s_kidx, 16)
                for b in range(2):
                    sp.wait_ge(s_vo[b], 16 * (5 - b))
                for c in range(4):
                    sp.wait_ge(s_sto[c], 16 * (N_A + 4))

            @block.gpsimd
            def _(pool):
                own = Own(pool, own_g)
                pool.dma_start(PTI, a["PTI"]).then_inc(s_pt, 16)
                pool.wait_ge(s_pix, 1)
                for j in range(8):
                    for g in range(4):
                        if j:
                            pool.wait_ge(s_ktp, 2 * (4 * (j - 1) + g) + 2)
                        n = g * 8 + j
                        pool.indirect_dma_start(
                            out=PG[g].rearrange("p o n -> p (o n)"), out_offset=None, in_=a["CI"],
                            in_offset=bass.IndirectOffsetOnAxis(ap=PIX[:, n:n + 1], axis=0),
                            bounds_check=CI_ROWS - 1, oob_is_err=False).then_inc(s_pg[g], 16)
                pool.wait_ge(s_idx, 1)

                def times_queries(i, b):
                    pool.wait_ge(s_qbc[b], i * 16 + 16)
                    pool.wait_ge(s_kgi[b], i * P + P)
                    kv = KG[b].rearrange("p (q f) d -> p q f d", f=2)
                    pool.tensor_tensor(kv, kv, QBC[b].rearrange("p (q d) -> p q d", d=512).unsqueeze(2)
                                       .to_broadcast([P, 4, 2, 512]), ALU.mult).then_inc(s_kgm[b], 1)

                def load_queries(i, b):
                    pool.dma_start(QBC[b], s["QS"][bass.ds(i * 8 + 4 * b, 4), :].rearrange("q n -> (q n)")
                                   .partition_broadcast(P)).then_inc(s_qbc[b], 16)
                pool.wait_ge(s_qso, 32)
                gather_rows(pool, own, KG, "CK", s_kgi, s_kgu, ISC, PDM, load_queries, times_queries)
                counts["pool"] = own.n

            @block.tensor
            def _(pe):
                pe.wait_ge(s_const, 32)
                uses = [0, 0]

                def project(b, K, weights, rhs, used=None):
                    n = uses[b] if used is None else used
                    if used is not None or n:
                        pe.wait_ge(s_free[b], n)
                    for k in range(K):
                        for t0, n in TOKENS:
                            last = pe.matmul(PP[b][:, t0:t0 + n], weights(k), rhs(k)[:, t0:t0 + n],
                                             start=(k == 0), stop=(k == K - 1))
                    last.then_inc(s_full[b], 1)
                    uses[b] += 1

                for k in range(KD):
                    pe.wait_ge(s_sq, k + 1)
                    for t0, n in TOKENS:
                        last = pe.matmul(PP[0][:, t0:t0 + n], C("ONES"), STG[k % 2][:, t0:t0 + n], start=(k == 0), stop=(k == KD - 1))
                    last.then_inc(s_sqmm if k < KD - 1 else s_full[0], 1)
                uses[0] = 1
                pe.wait_ge(s_wix, 32)
                pe.wait_ge(s_xn, KD)
                for c in range(5):
                    project((c + 1) % 2, KD, lambda k: WIX[:, k, c * P:(c + 1) * P], lambda k: XN[:, k, :])
                for t in range(NT + 2):
                    t0, n = (t * P, P) if t < NT else (SEQ, NS) if t == NT else (T - P, P)
                    for k in range(KD):
                        last = pe.matmul(BK[6][0:n, t * 16:(t + 1) * 16], XN[:, k, t0:t0 + n], WSM[:, k, :],
                                         start=(k == 0), stop=(k == KD - 1))
                last.then_inc(s_sm, 1)
                pe.wait_ge(s_wl, 1)
                pe.matmul(BK[7][:, 0:DEC_B], WLT[0:NS, :], C("BEQ", NS, DEC_B), start=True, stop=True).then_inc(s_wcolp, 1)

                pe.wait_ge(s_qb, 1)
                pe.wait_ge(s_cm, 1)
                for b in range(2):
                    pe.wait_ge(s_free[b], uses[b])

                def transpose_keys(j, g):
                    pe.wait_ge(s_pg[g], j * 16 + 16)
                    for hh in range(2):
                        pe.wait_ge(s_kte[hh], j * 4 + g)
                        for q in range(4):
                            last = pe.transpose(BK[hh][:, q * P:(q + 1) * P], PG[g][:, 4 * hh + q, :], ident)
                        last.then_inc(s_ktp, 1)

                def scores(j, final):
                    for g in range(4):
                        for hh in range(2):
                            pe.wait_ge(s_kte[hh], j * 4 + (g + 1))
                        for bb in range(2):
                            pe.wait_ge(s_rle[bb], j * 4 + g)
                            last = pe.matmul(BK[2 + bb], QB[:, 2 * g + bb, :],
                                             KT[g % 2][:, :, bb * N_PAGES:(bb + 1) * N_PAGES], start=True, stop=True)
                            last.then_inc(s_dotp[bb], 1)
                        if g < 3:
                            transpose_keys(j, g + 1)
                        elif not final:
                            transpose_keys(j + 1, 0)
                        for bb in range(2):
                            pe.wait_ge(s_rle[bb], j * 4 + (g + 1))
                            if g == bb == 0:
                                pe.wait_ge(s_sce, j)
                            last = pe.matmul(BK[4], CM[:, 2 * g + bb, :], RL[bb], start=(g == bb == 0), stop=(g == 3 and bb == 1))
                            last.then_inc(s_cmb[bb], 1)

                transpose_keys(0, 0)
                with pe.Fori(0, 7) as j:
                    scores(j, False)
                scores(7, True)
                for h in range(HI):
                    r = slice(DI * (h % 2), DI * (h % 2) + DI)
                    last = pe.matmul(BK[(5, 3)[h % 2]][:, h // 2 * NS:(h // 2 + 1) * NS], QI[r, h // 2, T - P:T], KI[r, SEQ:T],
                                     start=True, stop=True)
                last.then_inc(s_nk, 1)
                pe.wait_ge(s_nke, 2)
                pe.wait_ge(s_sce, 8)

                base = list(uses)
                with pe.Fori(0, N_A // 2) as i:
                    for b in range(2):
                        pe.wait_ge(s_load[b], i * 16 + 16)
                        for c in range(4):
                            project(c % 2, KD, lambda k: WB[b][:, k, c * P:(c + 1) * P], lambda k: XN[:, k, :],
                                    i * 4 + (base[c % 2] + 2 * b + c // 2))
                uses[:] = [base[0] + 2 * N_A, base[1] + 2 * N_A]
                pe.wait_ge(s_load[0], 64)
                pe.wait_ge(s_smc, 1)
                for t in range(NT + 1):
                    n = P if t < NT else NS
                    if t >= 2:
                        pe.wait_ge(s_vst[t % 2], t // 2)
                    else:
                        pe.wait_ge(s_wcol, 1)
                    for k in range(KD):
                        last = pe.matmul(BK[6 + t % 2][0:n, :], XN[:, k, t * P:t * P + n], WB[0][:, k, :],
                                         start=(k == 0), stop=(k == KD - 1))
                    last.then_inc(s_vps, 1)
                pe.wait_ge(s_qks, 16)
                for b in range(2):
                    pe.wait_ge(s_vst[b], 5 - b)
                    for h in range(H):
                        last = pe.transpose(BK[6 + b][0:NS, h * P:(h + 1) * P], QKS[:, 4 * b + h, :], ident)
                    last.then_inc(s_qkp, 1)

                def gate_chunk(g):
                    w, c = (g // 4 + 1) % 2, g % 4
                    if c == 0:
                        pe.wait_ge(s_load[w], 16 * (g // 8) + (64 if w else 80))
                    if g:
                        pe.wait_ge(s_gat, g)
                    for k in range(KD):
                        for t0, n in TOKENS:
                            last = pe.matmul(psum[:, 2048 + t0:2048 + t0 + n], WB[w][:, k, c * P:(c + 1) * P], XN[:, k, t0:t0 + n],
                                             start=(k == 0), stop=(k == KD - 1))
                    last.then_inc(s_gp, 1)

                pe.wait_ge(s_qke, 2)
                for b in range(2):
                    pe.wait_ge(s_free[b], uses[b])
                for g in range(GATES_FIRST):
                    gate_chunk(g)
                pe.wait_ge(s_gat, GATES_FIRST)
                pe.wait_ge(s_lists, 1)
                for n, name in enumerate(("LT1", "LT3")):
                    for hh in range(2):
                        last = pe.transpose(BK[6][:, (2 * n + hh) * NS:(2 * n + hh + 1) * NS],
                                            LST[name][0:NS, hh * P:(hh + 1) * P], ident[0:NS, 0:NS])
                last.then_inc(s_ltp, 1)
                u, g = 0, GATES_FIRST
                for i in range(2, NT):
                    L = P * (i + 1)
                    for h in range(HI):
                        r = slice(DI * (h % 2), DI * (h % 2) + DI)
                        if u >= 2:
                            pe.wait_ge(s_rpe[u % 2], u // 2)
                        for k0 in range(0, L, 512):
                            n = min(512, L - k0)
                            last = pe.matmul(psum[:, 1024 * (u % 2) + k0:1024 * (u % 2) + k0 + n],
                                             QI[r, h // 2, i * P:(i + 1) * P], KI[r, k0:k0 + n], start=True, stop=True)
                        last.then_inc(s_lg, 1)
                        u += 1
                    for _ in range(BESIDE.get(i, "").count("g")):
                        gate_chunk(g)
                        g += 1

            @block.scalar
            def _(act):
                own = Own(act, own_a)
                act.dma_start(const, a["CONST"]).then_inc(s_const, 16)
                act.dma_start(vec, a["VEC"]).then_inc(s_const, 16)
                for k in range(KD):
                    act.wait_ge(s_x[k // 2], 16)
                    if k >= 2:
                        act.wait_ge(s_sqmm, k - 1)
                    act.activation(STG[k % 2], X[:, k, :], ACT.Square).then_inc(s_sq, 1)
                act.wait_ge(s_full[0], 1)
                act.wait_ge(s_const, 32)
                own(act.activation(STG[2], PP[0][:, 0:T], ACT.Ln, scale=1.0 / DM, bias=eps))
                own.settle()
                act.activation(STG[3], STG[2], ACT.Exp, scale=-0.5).then_inc(s_free[0], 1)
                for c in range(5):
                    b = (c + 1) % 2
                    act.wait_ge(s_full[b], (c + 1) // 2 + 1)
                    act.activation(QI[:, c, :] if c < 4 else KI, PP[b][:, 0:T], ACT.Copy).then_inc(s_free[b], 1)
                act.wait_ge(s_sm, 1)
                act.activation(smw[:, 0:NT, :], BK[6][:, 0:NT * 16].rearrange("p (t c) -> p t c", c=16), ACT.Copy)
                act.activation(smw[0:NS, NT, :], BK[6][0:NS, NT * 16:(NT + 1) * 16], ACT.Copy)
                act.activation(smw[:, NT + 1, :], BK[6][:, (NT + 1) * 16:(NT + 2) * 16], ACT.Copy).then_inc(s_smc, 1)
                with act.Fori(0, 8) as j:
                    for g in range(4):
                        for bb in range(2):
                            act.wait_ge(s_cmb[bb], j * 4 + g)
                            act.wait_ge(s_dotp[bb], j * 4 + (g + 1))
                            act.activation(RL[bb], BK[2 + bb], ACT.Relu).then_inc(s_rle[bb], 1)
                with act.Fori(0, N_A // 2) as i:
                    for b in range(2):
                        for c in range(4):
                            act.wait_ge(s_sto[c], i * 32 + 16 * b)
                            act.wait_ge(s_full[c % 2], i * 4 + (U0 + 2 * b + c // 2 + 1))
                            act.activation(STG[c], PP[c % 2][:, 0:T], ACT.Copy).then_inc(s_free[c % 2], 1)
                for t in range(NT + 1):
                    n = P if t < NT else NS
                    if t >= 2:
                        act.wait_ge(s_vo[t % 2], 16 * (t // 2))
                    act.wait_ge(s_vps, t + 1)
                    act.activation(VST[t % 2][0:n, :], BK[6 + t % 2][0:n, :], ACT.Copy).then_inc(s_vst[t % 2], 1)
                for b in range(2):
                    act.wait_ge(s_vo[b], 16 * (5 - b))
                    act.wait_ge(s_qkp, b + 1)
                    act.activation(VST[b][0:NS, :], BK[6 + b][0:NS, :], ACT.Copy).then_inc(s_qke, 1)
                def gate_out(g):
                    act.wait_ge(s_sto[g % 4], 16 * (N_A + g // 4))
                    act.wait_ge(s_gp, g + 1)
                    act.activation(STG[g % 4], psum[:, 2048:2048 + T], ACT.Sigmoid).then_inc(s_gat, 1)

                for g in range(GATES_FIRST):
                    gate_out(g)
                u, g, kg = 0, GATES_FIRST, 0
                for i in range(2, NT):
                    L = P * (i + 1)
                    for h in range(HI):
                        if u >= 2:
                            act.wait_ge(s_rpu[u % 2], u // 2)
                        act.wait_ge(s_lg, u + 1)
                        act.activation(RP[u % 2][:, 0:L], psum[:, 1024 * (u % 2):1024 * (u % 2) + L], ACT.Relu,
                                       scale=wabs[:, i, h:h + 1]).then_inc(s_rpe[u % 2], 1)
                        u += 1
                    for what in BESIDE.get(i, ""):
                        if what == "g":
                            gate_out(g)
                            g += 1
                            continue
                        b = kg % 2
                        act.wait_ge(s_kgm[b], kg // 2 + 1)
                        for n in range(8):
                            for h in range(H):
                                part = KG[b][:, n, h * DH:(h + 1) * DH]
                                at_col = (n % 2) * TOPK + (4 * kg + n // 2) * H + h
                                last = act.activation(part, part, ACT.Copy, accum_out=lgs[:, at_col:at_col + 1])
                        last.then_inc(s_kgu[b], 1)
                        kg += 1
                counts["act"] = own.n

            @block.vector
            def _(dve):
                own = Own(dve, own_v)
                own(dve.memset(smw, 0.0))
                own(dve.memset(mask[:, 0:mask_at[2]], 0.0))
                dve.wait_ge(s_pt, 16)
                own(dve.tensor_scalar(PIF, PTI, 8.0, None, ALU.mult))
                own.settle()
                for j in range(8):
                    last = dve.tensor_scalar(PIX.rearrange("p (g j) -> p g j", j=8)[:, :, j], PIF, float(j), None, ALU.add)
                last.then_inc(s_pix, 1)
                dve.wait_ge(s_free[0], 1)
                dve.wait_ge(s_const, 32)
                for k in range(KD):
                    dve.scalar_tensor_tensor(out=XN[:, k, :], in0=X[:, k, :], scalar=V("g1", k), in1=STG[3],
                                             op0=ALU.mult, op1=ALU.mult).then_inc(s_xn, 1)
                for i in range(2):
                    dve.tensor_copy(mask[:, mask_at[i] + i * P:mask_at[i] + (i + 1) * P], C("CAU"))
                dve.wait_ge(s_xn, KD)
                own(dve.memset(QB, 0.0))
                own(dve.memset(SC[0:NS, PAST // 2:SCW], NEG))
                for b in range(2):
                    dve.wait_ge(s_free[b], U0)
                own.settle()
                for h in range(HI):
                    src = QI[DI * (h % 2):DI * (h % 2) + DI, h // 2, SEQ:T].rearrange("p (b t) -> p b t", t=DEC_T)
                    for par in range(2):
                        c0 = par * NS + h * DEC_T
                        last = dve.tensor_copy(QB[par * DI:par * DI + DI, :, c0:c0 + DEC_T], src)
                last.then_inc(s_qb, 1)
                dve.wait_ge(s_smc, 1)
                own(dve.tensor_scalar(ws, smw[:, :, 0:HI], HI ** -0.5, DI ** -0.5, ALU.mult, ALU.mult))
                own.settle()
                own(dve.scalar_tensor_tensor(out=wabs, in0=ws, scalar=-1.0, in1=ws, op0=ALU.mult, op1=ALU.max))
                own(dve.tensor_scalar(wsgn, ws, 0.0, 2.0, ALU.is_ge, ALU.mult))
                for par in range(2):
                    last = dve.tensor_tensor(WLT[0:NS, par * NS:(par + 1) * NS].rearrange("p (h t) -> p h t", t=DEC_T),
                                             ws[0:NS, NT, :].unsqueeze(2).to_broadcast([NS, HI, DEC_T]),
                                             C("BEQ", NS)[:, 64:128].rearrange("p (h t) -> p h t", t=DEC_T), ALU.mult)
                last.then_inc(s_wl, 1)
                own.settle()
                own(dve.tensor_scalar(wsgn, wsgn, -1.0, None, ALU.add))
                dve.wait_ge(s_wcolp, 1)
                dve.tensor_copy(WCOL, BK[7][:, 0:DEC_B]).then_inc(s_wcol, 1)
                dve.wait_ge(s_wcol, 1)
                dve.wait_ge(s_cmd, 16)
                for b in range(DEC_B):
                    last = dve.tensor_scalar(CM[:, b, :], CM[:, b, :], WCOL[:, b:b + 1], None, ALU.mult)
                last.then_inc(s_cm, 1)
                with dve.Fori(0, 8) as j:
                    for g in range(4):
                        for hh in range(2):
                            dve.wait_ge(s_ktp, j * 8 + (2 * g + hh + 1))
                            dve.tensor_copy(KT[g % 2][:, 4 * hh:4 * hh + 4, :],
                                            BK[hh].rearrange("p (o n) -> p o n", n=P)).then_inc(s_kte[hh], 1)
                    dve.wait_ge(s_cmb[1], j * 4 + 4)
                    dve.tensor_scalar(SC[:, 0:PAST // 2].rearrange("p (g o) -> p g o", o=64)[:, :, bass.ds(j * 8, 8)],
                                      BK[4].rearrange("p (o g) -> p g o", o=8), 1.0, None, ALU.mult).then_inc(s_sce, 1)
                dve.wait_ge(s_nk, 1)
                up = slice(NS, P)
                nkv = NK[up, :].rearrange("p (h k) -> p h k", k=NS)
                for f, bank in ((0, 5), (1, 3)):
                    dve.tensor_scalar(NK[up, :].rearrange("p (q f k) -> p q f k", f=2, k=NS)[:, :, f, :],
                                      BK[bank][up, 0:HI // 2 * NS].rearrange("p (q k) -> p q k", k=NS), 0.0, None, ALU.max).then_inc(s_nke, 1)
                dve.wait_ge(s_nke, 2)
                own(dve.tensor_tensor(nkv, nkv, ws[up, NT + 1, :].unsqueeze(2).to_broadcast([NS, HI, NS]), ALU.mult))
                own.settle()
                own(dve.tensor_reduce(SC[up, PAST // 2:SCW], nkv.rearrange("p h k -> p k h"), AX.X, ALU.add))
                own.settle()
                own(dve.tensor_tensor(SC[up, PAST // 2:SCW], SC[up, PAST // 2:SCW], C("NEW")[up, 0:NS], ALU.add))
                own.settle()

                n0 = own.n
                with dve.Fori(0, TOPK // 8) as r:
                    own.n = r * 5 + n0
                    own(dve.max(M8, SC))
                    own.settle()
                    own(dve.tensor_scalar(LST["LV"][:, bass.ds(r * 8, 8)], M8, 1.0, None, ALU.mult))
                    own(dve.max_index(MI8, M8, SC))
                    own(dve.match_replace(SC, M8, SC, MARK))
                    own.settle()
                    own(dve.tensor_scalar(LST["LI"][:, bass.ds(r * 8, 8)], MI8, 1.0, None, ALU.mult))
                own.n = n0 + 5 * TOPK // 8
                own.settle()
                L = LST
                lo = slice(0, NS)
                own(dve.tensor_scalar(L["LA"], L["LI"], float(1 - PAST // 2), 0.0, ALU.add, ALU.max))
                own(dve.tensor_scalar(L["LB"], L["LI"], 2.0, parity, ALU.mult, ALU.add))
                own.settle()
                own(dve.tensor_tensor(L["LI"], L["LB"], L["LA"], ALU.subtract))
                own.settle()
                own(dve.tensor_copy(L["BV"][lo, :], L["LV"][up, ::-1]))
                own(dve.tensor_copy(L["BI"][lo, :], L["LI"][up, ::-1]))
                own.settle()
                own(dve.tensor_tensor(L["LA"][lo, :], L["LV"][lo, :], L["BV"][lo, :], ALU.is_gt))
                own(dve.tensor_tensor(L["LB"][lo, :], L["LV"][lo, :], L["BV"][lo, :], ALU.is_equal))
                own(dve.tensor_tensor(L["KEY"][lo, :], L["LI"][lo, :], L["BI"][lo, :], ALU.is_lt))
                own.settle()
                own(dve.tensor_tensor(L["LB"][lo, :], L["LB"][lo, :], L["KEY"][lo, :], ALU.mult))
                own(dve.tensor_tensor(L["LT1"][lo, :], L["LI"][lo, :], L["BI"][lo, :], ALU.subtract))
                own.settle()
                own(dve.tensor_tensor(L["LA"][lo, :], L["LA"][lo, :], L["LB"][lo, :], ALU.add))
                own.settle()
                own(dve.tensor_tensor(L["LT1"][lo, :], L["LT1"][lo, :], L["LA"][lo, :], ALU.mult))
                own.settle()
                own(dve.tensor_tensor(L["KEY"][lo, :], L["LT1"][lo, :], L["BI"][lo, :], ALU.add))
                own.settle()
                own(dve.tensor_scalar(L["KNEW"][lo, :], L["KEY"][lo, :], float(PAST), None, ALU.is_ge))
                own(dve.tensor_copy(KINT[lo, :], L["KEY"][lo, :]))
                dve.wait_ge(s_ptr, 16)
                own(dve.tensor_copy(PTR[lo, :], PTRI[lo, :]))
                own(dve.memset(L["ACC"][lo, :], 0.0))
                own(dve.memset(L["BV"][lo, :], 0.0))
                own.settle()
                kpi, koi = L["LA"][lo, :].bitcast(I32), L["LB"][lo, :].bitcast(I32)
                own(dve.tensor_scalar(kpi, KINT[lo, :], 7, None, ALU.arith_shift_right))
                own(dve.tensor_scalar(koi, KINT[lo, :], PAGE - 1, None, ALU.bitwise_and))
                own.settle()
                own(dve.tensor_copy(L["KPG"][lo, :], kpi))
                own(dve.tensor_copy(L["KOF"][lo, :], koi))
                own.settle()
                n0 = own.n
                with dve.Fori(0, N_PAGES // 2) as r:
                    own.n = r * 4 + n0
                    for k in range(2):
                        dve.wait_ge(own_v, r * 4 + (n0 - 1 + k))
                        own(dve.tensor_scalar(L["LT2" if k else "LT1"][lo, :], L["KPG"][lo, :], C("IOT", NS)[:, bass.ds(r * 2 + k, 1)],
                                              PTR[lo, bass.ds(r * 2 + k, 1)], ALU.is_equal, ALU.mult))
                    own.n = r * 4 + (n0 + 1)
                    for k in range(2):
                        dve.wait_ge(own_v, r * 4 + (n0 + 1 + k))
                        acc = L["BV" if k else "ACC"][lo, :]
                        dve.tensor_tensor(acc, acc, L["LT2" if k else "LT1"][lo, :], ALU.add).then_inc(own_v, 1)
                own.n = n0 + 2 * N_PAGES
                own.settle()
                own(dve.tensor_tensor(L["ACC"][lo, :], L["ACC"][lo, :], L["BV"][lo, :], ALU.add))
                own.settle()
                own(dve.scalar_tensor_tensor(out=L["LT1"][lo, :], in0=L["ACC"][lo, :], scalar=float(PAGE), in1=L["KOF"][lo, :], op0=ALU.mult, op1=ALU.add))
                own(dve.scalar_tensor_tensor(out=L["LT3"][lo, :], in0=L["KNEW"][lo, :], scalar=-100.0, in1=L["KEY"][lo, :], op0=ALU.mult, op1=ALU.subtract))
                own(dve.tensor_scalar(L["LT2"][lo, :], L["KEY"][lo, :], newat, float(-PAST), ALU.subtract, ALU.add))
                own.settle()
                own(dve.scalar_tensor_tensor(out=L["LT1"][lo, :], in0=L["KNEW"][lo, :], scalar=FAR, in1=L["LT1"][lo, :], op0=ALU.mult, op1=ALU.add))
                dve.tensor_scalar(L["LT3"][lo, :], L["LT3"][lo, :], qpos, None, ALU.add).then_inc(s_lists, 1)
                for k0 in (0, 4):
                    own(dve.tensor_tensor(EQ4, L["LT2"][lo, :].unsqueeze(1).to_broadcast([NS, 4, TOPK]),
                                          C("THR", NS)[:, N_BUCKETS + k0:N_BUCKETS + k0 + 4].unsqueeze(2).to_broadcast([NS, 4, TOPK]), ALU.is_equal))
                    own.settle()
                    own(dve.tensor_reduce(new_sel[lo, k0:k0 + 4], EQ4, AX.X, ALU.add))
                    own.settle()
                own(dve.tensor_scalar(new_sel[lo, :], new_sel[lo, :], -1.0, -NEG, ALU.add, ALU.mult))
                dve.wait_ge(s_ltp, 1)
                own(dve.tensor_copy(idx_cache.rearrange("p (q f) -> p f q", f=2), BK[6][:, 0:P].rearrange("p (f q) -> p f q", f=2)))
                dve.tensor_copy(dist_t, BK[6][:, P:2 * P]).then_inc(s_idx, 1)

                u = 0
                for i in range(2, NT):
                    W = WK[i % 2][:, 0:P * (i + 1)]
                    for h in range(HI):
                        dve.wait_ge(s_rpe[u % 2], u // 2 + 1)
                        src, sg = RP[u % 2][:, 0:P * (i + 1)], wsgn[:, i, h:h + 1]
                        if h == 0:
                            ins = dve.tensor_scalar(W, src, sg, None, ALU.mult)
                        else:
                            dve.wait_ge(s_rpu[(u - 1) % 2], (u - 1) // 2 + 1)
                            ins = dve.scalar_tensor_tensor(out=W, in0=src, scalar=sg, in1=W, op0=ALU.mult, op1=ALU.add)
                        ins.then_inc(s_rpu[u % 2], 1)
                        u += 1
                    dve.wait_ge(s_rpu[(u - 1) % 2], (u - 1) // 2 + 1)
                    D = WK[i % 2][:, P * i:P * (i + 1)]
                    own(dve.tensor_tensor(D, D, C("CAU"), ALU.add))
                    if i % 2 == 0:
                        continue
                    own.settle()
                    n0 = own.n
                    pair = [(M8, WK[0][:, 0:P * i]), (MI8.bitcast(F32), WK[1][:, 0:P * (i + 1)])]
                    def after(r, k, n):
                        dve.wait_ge(own_v, r * 8 + (n0 + n))
                        own(dve.tensor_scalar(DMY[:, 2 * k:2 * k + 2], C("ONES")[:, 0:2], 1.0, None, ALU.mult))

                    with dve.Fori(0, TOPK // 8) as r:
                        for k, (m8, W) in enumerate(pair):
                            after(r, k, 2 * k - 2)
                            own(dve.max(m8, W))
                        for k, (m8, W) in enumerate(pair):
                            after(r, 2 + k, 2 * k + 2)
                            own(dve.match_replace(W, m8, W, MARK))
                    own.n = n0 + TOPK
                    own.settle()
                    for k, (m8, W) in enumerate(pair):
                        t = i - 1 + k
                        own(dve.tensor_scalar(mask[:, mask_at[t]:mask_at[t] + P * (t + 1)], W, 0.5 * MARK, NEG, ALU.is_gt, ALU.mult))
                    own.settle()
                counts["dve"] = own.n

        end_phase()
        HD = H * DH
        ASCALE = DH ** -0.5
        CW = T + 3
        NSC = DEC_B * (DEC_T + 3)
        OA = at(work, H * T).rearrange("p (h t) -> p h t", t=T)
        OB = at(work + H * T, H * T).rearrange("p (h t) -> p h t", t=T)
        top[0] = work + 2 * H * T
        work2 = top[0]
        QKV = at(take(A_CH * T), A_CH * T).rearrange("p (c t) -> p c t", t=T)
        S0 = at(take(DEC_B * HD), DEC_B * HD).rearrange("p (b h e) -> p b h e", b=DEC_B, h=H)
        GATES = at(take(2 * (NT + 1) * H), 2 * (NT + 1) * H).rearrange("p (k t h) -> p k t h", k=2, h=H)
        G, BETA = GATES[:, 0, :, :], GATES[:, 1, :, :]
        BKT, MNG, SBI = [at(work + H * T + c, n) for c, n in ((0, P), (P, P), (2 * P, HD))]
        GT1 = at(take((NT + 1) * H), (NT + 1) * H).rearrange("p (t h) -> p t h", h=H)
        EXPA = at(take(H), H)
        z2 = top[0]
        CI = [at(take(CW), CW) for _ in range(3)]
        CV = [at(take(SEQ), SEQ) for _ in range(3)]
        SQ = [at(take(T), T) for _ in range(2)]
        NR = [at(take(T), T) for _ in range(2)]
        RT = [at(take(T), T) for _ in range(2)]
        SIN = at(take(A_CH * NS), A_CH * NS).rearrange("p (c t) -> p c t", t=NS)
        SAS = at(take(A_CH * 3 * DEC_B), A_CH * 3 * DEC_B).rearrange("p (c t) -> p c t", t=3 * DEC_B)
        CIS = at(take(A_CH * NSC), A_CH * NSC).rearrange("p (c b t) -> p c b t", c=A_CH, b=DEC_B)
        CVS = at(take(A_CH * NS), A_CH * NS).rearrange("p (c b t) -> p c b t", c=A_CH, b=DEC_B)
        CVT = at(take(A_CH * NS), A_CH * NS).rearrange("p (c b t) -> p c b t", c=A_CH, b=DEC_B)
        COAS = at(take(A_CH * 27), A_CH * 27).rearrange("p (c t) -> p c t", t=27)
        assert top[0] <= ARENA, top[0]
        top[0] = z2
        BUFS = ["KC", "VC", "R", "D", "GM", "ATT", "BM", "BL0", "BL1", "TI", "UI", "YS", "KBG", "KDC", "VB", "NW", "QD", "VN"]
        TILE = [{n: take(HD) for n in BUFS} for _ in range(2)]
        TILE.append(TILE[0])
        SMALL = [{n: at(take(8), 8) for n in ("GB", "GC", "EX", "GD", "BG")} for _ in range(2)]
        SMALL.append(SMALL[0])
        ST = [at(take(HD), HD) for _ in range(2)]
        OSQ, OZ, ORT, ORN = [[at(TILE[0]["KC"] + (2 * n + b) * T, T) for b in range(2)] for n in range(4)]
        assert 8 * T <= len(BUFS) * HD
        EQ = at(TILE[1]["KC"], N_BUCKETS * P).rearrange("p (m n) -> p m n", m=N_BUCKETS)
        EQR = at(TILE[1]["KC"] + N_BUCKETS * P, N_BUCKETS * P).rearrange("p (m n) -> p m n", m=N_BUCKETS)
        assert 2 * N_BUCKETS * P <= len(BUFS) * HD
        GBJ = at(take(DEC_B * H), DEC_B * H)
        ELS = at(take(DEC_B * H), DEC_B * H)
        KDM = [at(take(HD), HD) for _ in range(2)]
        assert top[0] <= ARENA, top[0]

        s_ci, s_cv, s_cva = sems("conv_in", 3), sems("conv_done", 3), sems("conv_silu", 3)
        s_si, s_cvs, s_cvsa, s_coa = sem("sample_conv_in"), sem("sample_conv"), sem("sample_silu"), sem("conv_state_stored")
        s_bkt, s_eq, s_eqr, s_eqd = sem("buckets"), sem("buckets_one_hot"), sem("buckets_biased"), sem("bias_summed")
        s_qkn = sems("qk_normed", 2)
        s_nrt, s_ort = sems("norm_root", 2), sems("out_norm_root", 2)
        s_sqa, s_nmp, s_nme = sems("conv_squares", 2), sems("norm_psum", 2), sems("norm_out", 2)
        s_gexp, s_gabs, s_gate, s_s0 = sem("decay_rate"), sem("gate_abs"), sem("gates"), sem("sample_state_in")
        LEV = [6, 6, 2]

        def stages(lev):
            mid = [(f"y{k}", f"tu{k}") for k in range(1, lev + 1)]
            return {
                "pe": ["cols", "rows", "beta", "kk", "qk", "kt", "t0", "y1", "vt"] +
                      [n for p in mid for n in p][1:] + ["nw"] + (["ws"] if lev < 6 else []) + ["vn", "o", "s"],
                "dve": ["gb", "cols", "gd", "sub", "min", "st", "bg", "stg", "bm", "u0", "gu", "att", "qd", "kbg", "kd", "vb"] +
                       [n for k in range(1, lev) for n in (f"t{k}", f"u{k}")] + [f"u{lev}", "s"],
                "act": ["kc", "vc", "ex", "exd", "gm", "er", "t0"] + [f"y{k}" for k in range(1, lev + 1)] + ["nw"] +
                       (["ws"] if lev < 6 else []) + ["vn", "o"],
                "pool": [f"bl{k}" for k in range(lev + 1)] + (["sg"] if lev == 6 else []),
            }
        STAGES = [stages(lev) for lev in LEV]
        DONE = [{e: sem(f"tile{x}_{e}") for e in ("pe", "dve", "act", "pool")} for x in range(3)]

        def await_stage(eng, x, who, stage, i=0):
            st = STAGES[x][who]
            eng.wait_ge(DONE[x][who], i * len(st) + (st.index(stage) + 1))

        def done(x, who, ins):
            ins.then_inc(DONE[x][who], 1)

        def shapes(x):
            n = P if x < 2 else NS
            B = {k: at(v, HD) for k, v in TILE[x].items()}
            mat = {k: v[0:n, 0:H * n].rearrange("p (h i) -> p h i", h=H) for k, v in B.items()}
            tok = {k: v[0:n, :].rearrange("p (h d) -> p h d", h=H) for k, v in B.items()}
            feat = {k: v[:, 0:H * n].rearrange("p (h i) -> p h i", h=H) for k, v in B.items()}
            bank = [BK[(4 * x if x < 2 else 0) + k] for k in range(4)]
            pm = [b[0:n, 0:H * n].rearrange("p (h i) -> p h i", h=H) for b in bank]
            pt = [b[0:n, :].rearrange("p (h d) -> p h d", h=H) for b in bank]
            pf = [b[:, 0:H * n].rearrange("p (h i) -> p h i", h=H) for b in bank]
            return n, mat, tok, feat, bank, pm, pt, pf

        def over_heads(m, n):
            return m.unsqueeze(1).to_broadcast([n, H, n])

        def over_dims(col, n):
            return col.unsqueeze(2).to_broadcast([n, H, DH])
        state = ST[0].rearrange("p (h e) -> p h e", h=H)
        decayed = ST[1].rearrange("p (h e) -> p h e", h=H)
        s_kdm, s_kdu, s_sps, s_sns = sems("keys_by_batch", 2), sems("keys_by_batch_used", 2), sem("states_psum"), sem("states_new")
        s_gbj, s_els, s_elp, s_s0d = sem("decay_by_batch"), sem("decay_exp"), sem("decay_psum"), sem("states_decayed")
        s_rec, s_z, s_zs = sem("states_stored"), sems("z_in", 2), sems("z_silu", 2)
        s_osq, s_onp, s_one = sems("out_squares", 2), sems("out_norm_psum", 2), sems("out_norm", 2)
        s_on = sems("out_normed", 2)

        with nc.Block() as block:
            @block.sync
            def _(sp):
                sp.dma_start(SIN, s["PR"][0:A_CH, :, SEQ:T].rearrange("c p t -> p c t")).then_inc(s_si, 16)
                sp.dma_start(SAS, a["SA"]).then_inc(s_si, 16)
                with sp.Fori(0, 4) as i:
                    for b in range(3):
                        chunk = bass.ds(i * 2 + b, 1) if b < 2 else bass.ds(i + 8, 1)
                        sp.wait_ge(s_cv[b], i)
                        sp.dma_start(CI[b][:, 3:CW], s["PR"][chunk, :, :].rearrange("o p n -> p (o n)")).then_inc(s_ci[b], 16)
                sp.dma_start(S0, a["S0"]).then_inc(s_s0, 16)
                for b in range(3):
                    sp.wait_ge(s_cv[b], 4)
                sp.wait_ge(s_cvs, 1)
                sp.dma_start(o["COA"], COAS).then_inc(s_coa, 16)
                await_stage(sp, 1, "dve", "s", 3)
                sp.dma_start(o["REC"], state).then_inc(s_rec, 16)
                sp.wait_ge(s_sns, DEC_B)
                sp.dma_start(o["RECS"], S0).then_inc(s_rec, 16)
                for h in range(H):
                    if h >= 2:
                        sp.wait_ge(s_on[h % 2], h // 2)
                    sp.dma_start(OZ[h % 2], s["PR"][PR_Z + h]).then_inc(s_z[h % 2], 16)
                sp.wait_ge(s_rec, 32)

            @block.gpsimd
            def _(pool):
                own = Own(pool, own_g, counts["pool"])

                def blocks_of_level(x, lev, i):
                    n, mat, _, _, _, _, _, _ = shapes(x)
                    await_stage(pool, x, "dve", "bm", i)
                    if lev == 2:
                        await_stage(pool, x, "dve", "u0", i)
                    elif lev > 2:
                        await_stage(pool, x, "pe", f"y{lev - 2}", i)
                    done(x, "pool", pool.tensor_tensor(mat[f"BL{lev % 2}"], mat["BM"], over_heads(C(f"L{lev}", n, n), n), ALU.mult))

                pool.wait_ge(s_coa, 16)
                with pool.Fori(0, NT // 2) as i:
                    for lev in range(LEV[0] + 1):
                        for x in range(2):
                            blocks_of_level(x, lev, i)
                    for x in range(2):
                        if x == 0:
                            pool.wait_ge(DONE[1]["dve"], i * len(STAGES[1]["dve"]))
                        else:
                            await_stage(pool, 0, "dve", "s", i)
                        await_stage(pool, x, "act", "ex", i)
                        done(x, "pool", pool.tensor_tensor(decayed, state, over_dims(SMALL[x]["EX"][:, 4:8], P), ALU.mult))
                for lev in range(LEV[2] + 1):
                    blocks_of_level(2, lev, 0)
                pool.wait_ge(s_eq, 1)

                def biased(h):
                    if h:
                        pool.wait_ge(s_eqd, h)
                    pool.tensor_tensor(EQR, EQ, V("rb", h * N_BUCKETS, N_BUCKETS).unsqueeze(2).to_broadcast([P, N_BUCKETS, P]),
                                       ALU.mult).then_inc(s_eqr, 1)
                biased(0)
                biased(1)
                pool.wait_ge(s_els, 1)
                await_stage(pool, 2, "pe", "o")
                for b in range(DEC_B):
                    ins = pool.tensor_tensor(S0[:, b, :, :], S0[:, b, :, :], over_dims(ELS[:, H * b:H * b + H], P), ALU.mult)
                    ins.then_inc(s_s0d, 1)
                biased(2)
                biased(3)
                counts["pool"] = own.n

            @block.tensor
            def _(pe):
                with pe.Fori(0, 4) as i:
                    for b in range(2):
                        pe.wait_ge(s_sqa[b], i + 1)
                        pe.wait_ge(s_nrt[b], i)
                        for t0, n in TOKENS:
                            last = pe.matmul(PP[b][:, t0:t0 + n], C("ONES"), SQ[b][:, t0:t0 + n], start=True, stop=True)
                        last.then_inc(s_nmp[b], 1)
                for b in range(2):
                    pe.wait_ge(s_nme[b], 4)

                def gates(x, i):
                    n, mat, tok, feat, bank, pm, pt, pf = shapes(x)
                    g = SMALL[x]["GB"][0:n, 0:H]
                    up, last_of = (C("UP"), C("ONES")) if x < 2 else (C("UPS", n, n), C("BLK", n, n))
                    await_stage(pe, x, "dve", "gb", i)
                    pe.matmul(bank[0][0:n, 0:H], up, g, start=True, stop=True)
                    done(x, "pe", pe.matmul(bank[0][0:n, H:2 * H], last_of, g, start=True, stop=True))
                    for h in range(H):
                        last = pe.matmul(pf[1][:, h, :], SMALL[x]["GB"][0:n, h:h + 1].to_broadcast([n, P]), up, start=True, stop=True)
                    done(x, "pe", last)
                    for h in range(H):
                        last = pe.matmul(pm[2][:, h, :], SMALL[x]["GB"][0:n, H + h:H + h + 1].to_broadcast([n, n]), ident[0:n, 0:n],
                                         start=True, stop=True)
                    done(x, "pe", last)
                    await_stage(pe, x, "act", "kc", i)
                    for h in range(H):
                        last = pe.matmul(pm[3][:, h, :], feat["KC"][:, h, :], feat["KC"][:, h, :], start=True, stop=True)
                    done(x, "pe", last)

                def attention(x, i, queries):
                    n, mat, tok, feat, bank, pm, pt, pf = shapes(x)
                    await_stage(pe, x, "dve", "cols", i)
                    for h in range(H):
                        last = pe.matmul(pm[0][:, h, :], feat["KC"][:, h, :], queries(h), start=True, stop=True)
                    done(x, "pe", last)

                def to_tokens(x, i, src, until):
                    n, mat, tok, feat, bank, pm, pt, pf = shapes(x)
                    await_stage(pe, x, "dve", until, i)
                    if src == "VC":
                        await_stage(pe, x, "act", "vc", i)
                    for h in range(H):
                        last = pe.transpose(pt[3][:, h, :], feat[src][:, h, :], ident)
                    done(x, "pe", last)

                def first_inverse(x, i):
                    n, mat, tok, feat, bank, pm, pt, pf = shapes(x)
                    await_stage(pe, x, "dve", "u0", i)
                    await_stage(pe, x, "act", "er", i)
                    for h in range(H):
                        last = pe.transpose(pm[1][:, h, :], mat["UI"][:, h, :], ident[0:n, 0:n])
                    done(x, "pe", last)

                def level_y(x, i, lev):
                    n, mat, tok, feat, bank, pm, pt, pf = shapes(x)
                    await_stage(pe, x, "pool", f"bl{lev}", i)
                    if lev == 1:
                        await_stage(pe, x, "act", "t0", i)
                        await_stage(pe, x, "dve", "att", i)
                    else:
                        await_stage(pe, x, "dve", f"t{lev - 1}", i)
                        await_stage(pe, x, "act", f"y{lev - 1}", i)
                    for h in range(H):
                        last = pe.matmul(pm[0][:, h, :], mat[f"BL{lev % 2}"][:, h, :], mat["TI"][:, h, :], start=True, stop=True)
                    done(x, "pe", last)

                def level_tu(x, i, lev):
                    n, mat, tok, feat, bank, pm, pt, pf = shapes(x)
                    await_stage(pe, x, "act", f"y{lev}", i)
                    if lev == 1:
                        await_stage(pe, x, "dve", "st", i)
                    else:
                        await_stage(pe, x, "dve", f"u{lev - 1}", i)
                    if lev < LEV[x]:
                        for h in range(H):
                            pe.matmul(pm[1][:, h, :], mat["UI"][:, h, :], mat["YS"][:, h, :], start=True, stop=True)
                    for h in range(H):
                        last = pe.matmul(pm[2][:, h, :], mat["YS"][:, h, :], mat["UI"][:, h, :], start=True, stop=True)
                    done(x, "pe", last)

                def key_part(x, i):
                    n, mat, tok, feat, bank, pm, pt, pf = shapes(x)
                    await_stage(pe, x, "dve", f"u{LEV[x]}", i)
                    for h in range(H):
                        last = pe.matmul(pf[3][:, h, :], tok["KBG"][:, h, :], mat["UI"][:, h, :], start=True, stop=True)
                    done(x, "pe", last)

                with pe.Fori(0, NT // 2) as i:
                    for x in range(2):
                        for e in ("act", "dve"):
                            pe.wait_ge(DONE[x][e], i * len(STAGES[x][e]))
                    for x in range(2):
                        gates(x, i)
                    for x in range(2):
                        attention(x, i, lambda h: QKV[:, h, bass.ds(i * 2 * P + x * P, P)])
                    for x in range(2):
                        to_tokens(x, i, "KC", "bm")
                    for x in range(2):
                        first_inverse(x, i)
                    for x in range(2):
                        level_y(x, i, 1)
                    for x in range(2):
                        to_tokens(x, i, "VC", "kd")
                    for x in range(2):
                        level_tu(x, i, 1)
                    for lev in range(2, LEV[0] + 1):
                        for x in range(2):
                            level_y(x, i, lev)
                        for x in range(2):
                            level_tu(x, i, lev)
                    for x in range(2):
                        key_part(x, i)
                    for x in range(2):
                        n, mat, tok, feat, bank, pm, pt, pf = shapes(x)
                        if x == 0:
                            pe.wait_ge(DONE[1]["dve"], i * len(STAGES[1]["dve"]))
                        else:
                            await_stage(pe, 0, "dve", "s", i)
                        await_stage(pe, x, "act", "nw", i)
                        for h in range(H):
                            pe.matmul(pt[0][:, h, :], mat["UI"][:, h, :], tok["VB"][:, h, :], start=True, stop=False)
                            last = pe.matmul(pt[0][:, h, :], feat["NW"][:, h, :], state[:, h, :], start=False, stop=True)
                        done(x, "pe", last)
                        await_stage(pe, x, "act", "vn", i)
                        await_stage(pe, x, "dve", "u6", i)
                        for h in range(H):
                            pe.matmul(pf[1][:, h, :], state[:, h, :], feat["QD"][:, h, :], start=True, stop=False)
                            last = pe.matmul(pf[1][:, h, :], tok["VN"][:, h, :], mat["ATT"][:, h, :], start=False, stop=True)
                        done(x, "pe", last)
                        for h in range(H):
                            last = pe.matmul(pt[2][:, h, :], tok["KDC"][:, h, :], tok["VN"][:, h, :], start=True, stop=True)
                        done(x, "pe", last)

                for x in range(2):
                    for e in ("act", "dve"):
                        pe.wait_ge(DONE[x][e], 4 * len(STAGES[x][e]))
                x = 2
                n, mat, tok, feat, bank, pm, pt, pf = shapes(x)
                gates(x, 0)
                pe.wait_ge(s_gbj, 1)
                pe.matmul(BK[7][:, 0:DEC_B * H], C("ONES", NS, P), GBJ[0:NS, :], start=True, stop=True).then_inc(s_elp, 1)
                attention(x, 0, lambda h: QKV[:, h, SEQ:T])
                to_tokens(x, 0, "KC", "bm")
                first_inverse(x, 0)
                level_y(x, 0, 1)
                to_tokens(x, 0, "VC", "kd")
                level_tu(x, 0, 1)
                level_y(x, 0, 2)
                level_tu(x, 0, 2)
                key_part(x, 0)
                pe.wait_ge(s_s0, 16)
                await_stage(pe, x, "act", "nw")
                for h in range(H):
                    for b in range(DEC_B):
                        last = pe.matmul(pf[0][:, h, b * DEC_T:(b + 1) * DEC_T], S0[:, b, h, :],
                                         feat["NW"][:, h, b * DEC_T:(b + 1) * DEC_T], start=True, stop=True)
                done(x, "pe", last)
                await_stage(pe, x, "act", "ws")
                await_stage(pe, x, "dve", "t1")
                for h in range(H):
                    pe.matmul(pt[1][:, h, :], mat["UI"][:, h, :], tok["VB"][:, h, :], start=True, stop=False)
                    last = pe.matmul(pt[1][:, h, :], feat["YS"][:, h, :], ident, start=False, stop=True)
                done(x, "pe", last)
                await_stage(pe, x, "act", "vn")
                for h in range(H):
                    pe.matmul(pf[2][:, h, :], tok["VN"][:, h, :], mat["ATT"][:, h, :], start=True, stop=False)
                    for b in range(DEC_B):
                        last = pe.matmul(pf[2][:, h, b * DEC_T:(b + 1) * DEC_T], S0[:, b, h, :],
                                         feat["QD"][:, h, b * DEC_T:(b + 1) * DEC_T], start=False, stop=(b == DEC_B - 1))
                done(x, "pe", last)
                for b in range(DEC_B):
                    pe.wait_ge(s_kdm[b % 2], b // 2 + 1)
                    if b >= 2:
                        pe.wait_ge(s_sns, b - 1)
                    for h in range(H):
                        last = pe.matmul(BK[4 + b % 2][:, h * DH:(h + 1) * DH], KDM[b % 2][0:NS, h * DH:(h + 1) * DH], tok["VN"][:, h, :],
                                         start=True, stop=True)
                    last.then_inc(s_sps, 1)
                pe.wait_ge(s_sns, DEC_B)
                for h in range(H):
                    b = h % 2
                    pe.wait_ge(s_osq[b], h // 2 + 1)
                    if h >= 2:
                        pe.wait_ge(s_ort[b], h // 2)
                    for t0, n in TOKENS:
                        last = pe.matmul(PP[b][:, t0:t0 + n], C("ONES"), OSQ[b][:, t0:t0 + n], start=True, stop=True)
                    last.then_inc(s_onp[b], 1)

            @block.scalar
            def _(act):
                own = Own(act, own_a, counts["act"])
                act.activation(EXPA, V("alog", 0, H), ACT.Exp).then_inc(s_gexp, 1)
                act.wait_ge(s_gabs, 1)
                own(act.activation(GT1, GT1, ACT.Exp, scale=-1.0))
                own(act.activation(BETA, smw[:, 0:NT + 1, 8:12], ACT.Sigmoid))
                own.settle()
                act.activation(GT1, GT1, ACT.Ln, bias=C("ONES")[:, 0:1]).then_inc(s_gexp, 1)
                counts["act"] = own.n
                act.wait_ge(s_cvs, 1)
                act.activation(QKV[:, :, SEQ:T], CVS.rearrange("p c b t -> p c (b t)"), ACT.Silu).then_inc(s_cvsa, 1)
                act.wait_ge(s_cvsa, 1)
                with act.Fori(0, 4) as i:
                    for b in range(3):
                        act.wait_ge(s_cv[b], i + 1)
                        chunk = bass.ds(i * 2 + b, 1) if b < 2 else bass.ds(i + 8, 1)
                        alone(act)
                        act.activation(QKV[:, chunk, 0:SEQ].rearrange("p o t -> p (o t)"), CV[b], ACT.Silu).then_inc(s_cva[b], 1)
                        if b < 2:
                            alone(act)
                            act.wait_ge(s_nmp[b], i)
                            act.wait_ge(s_cva[b], i + 1)
                            act.activation(SQ[b], QKV[:, chunk, :].rearrange("p o t -> p (o t)"), ACT.Square).then_inc(s_sqa[b], 1)
                    for b in range(2):
                        act.wait_ge(s_nme[b], i)
                        act.wait_ge(s_nmp[b], i + 1)
                        act.activation(RT[b], PP[b][:, 0:T], ACT.Ln, bias=eps).then_inc(s_nrt[b], 1)
                    for b in range(2):
                        act.wait_ge(s_qkn[b], i)
                        act.wait_ge(s_nrt[b], i + 1)
                        act.activation(NR[b], RT[b], ACT.Exp, scale=-0.5).then_inc(s_nme[b], 1)

                def loads(x, i, cols, cols_v):
                    _, _, _, feat, _, _, _, _ = shapes(x)
                    alone(act)
                    done(x, "act", act.activation(feat["KC"], cols, ACT.Copy))
                    done(x, "act", act.activation(feat["VC"], cols_v, ACT.Copy))

                def exponents(x, i):
                    n, mat, tok, feat, bank, pm, pt, pf = shapes(x)
                    sm = SMALL[x]
                    await_stage(act, x, "dve", "cols", i)
                    done(x, "act", act.activation(sm["EX"][0:n, :], sm["GC"][0:n, :], ACT.Exp))
                    await_stage(act, x, "dve", "gd", i)
                    done(x, "act", act.activation(sm["GD"][0:n, H:2 * H], sm["GD"][0:n, 0:H], ACT.Exp))
                    await_stage(act, x, "dve", "min", i)
                    done(x, "act", act.activation(mat["GM"], mat["D"], ACT.Exp))
                    await_stage(act, x, "dve", "sub", i)
                    done(x, "act", act.activation(feat["R"], pf[1], ACT.Exp))

                def copy_out(x, i, stage, dst, src, scale=1.0):
                    await_stage(act, x, "pe", stage, i)
                    if stage == "o":
                        alone(act)
                    done(x, "act", act.activation(dst, src, ACT.Copy, scale=scale))

                act.wait_ge(s_cva[2], 4)
                act.wait_ge(s_coa, 16)
                for b in range(2):
                    act.wait_ge(s_qkn[b], 4)
                with act.Fori(0, NT // 2) as i:
                    for x in range(2):
                        act.wait_ge(DONE[1]["pe"], i * len(STAGES[1]["pe"]))
                        act.wait_ge(DONE[x]["dve"], i * len(STAGES[x]["dve"]))
                        tile = bass.ds(i * 2 * P + x * P, P)
                        loads(x, i, QKV[:, H:2 * H, tile], QKV[:, 2 * H:3 * H, tile])
                    for x in range(2):
                        exponents(x, i)
                    for x in range(2):
                        _, mat, _, feat, _, pm, _, pf = shapes(x)
                        copy_out(x, i, "t0", mat["TI"], pm[1])
                    for lev in range(1, LEV[0] + 1):
                        for x in range(2):
                            _, mat, _, _, _, pm, _, _ = shapes(x)
                            copy_out(x, i, f"y{lev}", mat["YS"], pm[0])
                    for x in range(2):
                        _, _, _, feat, _, _, _, pf = shapes(x)
                        copy_out(x, i, "nw", feat["NW"], pf[3], -1.0)
                    for x in range(2):
                        _, _, tok, feat, _, _, pt, pf = shapes(x)
                        copy_out(x, i, "vn", tok["VN"], pt[0])
                        copy_out(x, i, "o", OA[:, :, bass.ds(i * 2 * P + x * P, P)], pf[1])
                x = 2
                for y in range(2):
                    act.wait_ge(DONE[y]["pe"], 4 * len(STAGES[y]["pe"]))
                    act.wait_ge(DONE[y]["dve"], 4 * len(STAGES[y]["dve"]))
                _, mat, tok, feat, _, pm, pt, pf = shapes(x)
                loads(x, 0, QKV[:, H:2 * H, SEQ:T], QKV[:, 2 * H:3 * H, SEQ:T])
                exponents(x, 0)
                act.wait_ge(s_elp, 1)
                act.activation(ELS, BK[7][:, 0:DEC_B * H], ACT.Exp).then_inc(s_els, 1)
                copy_out(x, 0, "t0", mat["TI"], pm[1])
                for lev in (1, 2):
                    copy_out(x, 0, f"y{lev}", mat["YS"], pm[0])
                copy_out(x, 0, "nw", feat["NW"], pf[3], -1.0)
                copy_out(x, 0, "ws", feat["YS"], pf[0])
                copy_out(x, 0, "vn", tok["VN"], pt[1])
                copy_out(x, 0, "o", OA[:, :, SEQ:T], pf[2])
                await_stage(act, x, "act", "o")
                act.wait_ge(s_sns, DEC_B)
                for h in range(H):
                    b = h % 2
                    if h >= 2:
                        act.wait_ge(s_onp[b], h // 2)
                    act.activation(OSQ[b], OA[:, h, :], ACT.Square).then_inc(s_osq[b], 1)
                    act.wait_ge(s_z[b], 16 * (h // 2 + 1))
                    act.activation(OZ[b], OZ[b], ACT.Silu).then_inc(s_zs[b], 1)
                    if h >= 2:
                        act.wait_ge(s_on[b], h // 2)
                    act.wait_ge(s_onp[b], h // 2 + 1)
                    act.activation(ORT[b], PP[b][:, 0:T], ACT.Ln, scale=1.0 / DH, bias=eps).then_inc(s_ort[b], 1)
                    act.wait_ge(s_ort[b], h // 2 + 1)
                    act.activation(ORN[b], ORT[b], ACT.Exp, scale=-0.5).then_inc(s_one[b], 1)

            @block.vector
            def _(dve):
                own = Own(dve, own_v, counts["dve"])
                own(dve.tensor_tensor(G, smw[:, 0:NT + 1, 12:16], V("dtb", 0, H).unsqueeze(1).to_broadcast([P, NT + 1, H]), ALU.add))
                own.settle()
                dve.scalar_tensor_tensor(out=GT1, in0=G, scalar=-1.0, in1=G, op0=ALU.mult, op1=ALU.max).then_inc(s_gabs, 1)
                dve.wait_ge(s_gabs, 1)
                own(dve.tensor_scalar(G, G, 0.0, None, ALU.max))
                for b in range(3):
                    own(dve.memset(CI[b][:, 0:3], 0.0))
                dve.wait_ge(s_gexp, 2)
                own.settle()
                own(dve.tensor_tensor(G, G, GT1, ALU.add))
                own.settle()
                own(dve.scalar_tensor_tensor(out=G, in0=G, scalar=-1.0, in1=EXPA.unsqueeze(1).to_broadcast([P, NT + 1, H]),
                                             op0=ALU.mult, op1=ALU.mult))
                own(dve.memset(BKT, 0.0))
                n0 = own.n
                with dve.Fori(0, N_BUCKETS - 1) as m:
                    dve.wait_ge(own_v, m + n0)
                    dve.scalar_tensor_tensor(out=BKT, in0=dist_t, scalar=const[:, bass.ds(m + C_AT["THR"], 1)], in1=BKT,
                                             op0=ALU.is_ge, op1=ALU.add).then_inc(own_v, 1)
                own.n = n0 + N_BUCKETS - 1
                dve.tensor_scalar(MNG, dist_t, 0.0, NEG, ALU.is_lt, ALU.mult).then_inc(s_bkt, 1)
                dve.wait_ge(s_si, 32)
                own(dve.tensor_copy(CIS.rearrange("p c b t -> p (c b) t")[:, :, 3:11], SIN.rearrange("p c (b t) -> p (c b) t", t=DEC_T)))
                own(dve.tensor_copy(CIS.rearrange("p c b t -> p (c b) t")[:, :, 0:3], SAS.rearrange("p c (b t) -> p (c b) t", t=3)))
                own.settle()
                own(dve.tensor_copy(COAS[:, :, 3:27].rearrange("p c (b t) -> p c b t", t=3), CIS[:, :, :, 8:11]))
                taps = V("wa", 0, 4 * A_CH).rearrange("p (c j) -> p c j", j=4)
                for j in range(4):
                    w = taps[:, :, j:j + 1].unsqueeze(3).to_broadcast([P, A_CH, DEC_B, DEC_T])
                    own(dve.tensor_tensor(CVT if j else CVS, CIS[:, :, :, j:j + DEC_T], w, ALU.mult))
                    if j:
                        own.settle()
                        own(dve.tensor_tensor(CVS, CVS, CVT, ALU.add))
                        own.settle()
                own(dve.memset(state, 0.0))
                last = dve.tensor_copy(GBJ[0:NS, :].rearrange("p (b h) -> p b h", h=H), C("BEQ", NS)[:, 0:DEC_B].unsqueeze(2).to_broadcast([NS, DEC_B, H]))
                last.then_inc(s_cvs, 1)
                dve.wait_ge(s_cvs, 1)
                gbj = GBJ[0:NS, :].rearrange("p (b h) -> p b h", h=H)
                dve.tensor_tensor(gbj, gbj, G[0:NS, NT, :].unsqueeze(1).to_broadcast([NS, DEC_B, H]), ALU.mult).then_inc(s_gbj, 1)
                n0 = own.n

                def conv(i):
                    for b in range(3):
                        dve.wait_ge(s_ci[b], i * 16 + 16)
                        dve.wait_ge(s_cva[b], i)
                        for j in range(4):
                            col = (i * 8 + (4 * b + j)) if b < 2 else (i * 4 + (32 + j))
                            w = vec[:, bass.ds(col + VEC["wa"], 1)]
                            if j == 0:
                                dve.tensor_scalar(CV[b], CI[b][:, 0:SEQ], w, None, ALU.mult).then_inc(own_v, 1)
                                continue
                            dve.wait_ge(own_v, i * 12 + (n0 + 4 * b + j))
                            dve.scalar_tensor_tensor(out=CV[b], in0=CI[b][:, j:j + SEQ], scalar=w, in1=CV[b],
                                                     op0=ALU.mult, op1=ALU.add).then_inc(own_v, 1)
                        chunk = bass.ds(i * 2 + b, 1) if b < 2 else bass.ds(i + 8, 1)
                        dve.tensor_scalar(COAS[:, chunk, 0:3].rearrange("p o t -> p (o t)"), CI[b][:, SEQ:SEQ + 3], 1.0, None, ALU.mult).then_inc(s_cv[b], 1)

                def normalise(i):
                    for b in range(2):
                        dve.wait_ge(s_nme[b], i + 1)
                        q = QKV[:, bass.ds(i * 2 + b, 1), :].rearrange("p o t -> p (o t)")
                        dve.tensor_tensor(q, q, NR[b], ALU.mult).then_inc(s_qkn[b], 1)

                conv(0)
                with dve.Fori(1, 4) as i:
                    conv(i)
                    normalise(i - 1)
                normalise(3)
                own.n = n0 + 48
                for b in range(2):
                    dve.wait_ge(s_qkn[b], 4)

                own.settle()

                def gate_columns(x, i, tile):
                    sm, n = SMALL[x], shapes(x)[0]
                    done(x, "dve", dve.tensor_scalar(sm["GB"][0:n, :].rearrange("p (k h) -> p k h", h=H),
                                                     GATES[0:n, :, tile, :].rearrange("p k o h -> p k (o h)"), 1.0, None, ALU.mult))

                def decays(x, i):
                    n, mat, tok, feat, bank, pm, pt, pf = shapes(x)
                    sm = SMALL[x]
                    await_stage(dve, x, "pe", "cols", i)
                    done(x, "dve", dve.tensor_copy(sm["GC"][0:n, :], bank[0][0:n, 0:2 * H]))
                    await_stage(dve, x, "dve", "cols", i)
                    done(x, "dve", dve.tensor_tensor(sm["GD"][0:n, 0:H], sm["GC"][0:n, H:2 * H], sm["GC"][0:n, 0:H], ALU.subtract))
                    await_stage(dve, x, "pe", "rows", i)
                    done(x, "dve", dve.tensor_tensor(mat["D"], pm[1][0:n], sm["GC"][0:n, 0:H].unsqueeze(2).to_broadcast([n, H, n]), ALU.subtract))
                    await_stage(dve, x, "dve", "sub", i)
                    done(x, "dve", dve.tensor_scalar(mat["D"], mat["D"], 0.0, None, ALU.min))
                    await_stage(dve, x, "pe", "beta", i)
                    done(x, "dve", dve.tensor_tensor(mat["BM"], pm[2], over_heads(C("ST" if x < 2 else "STS", n, n), n), ALU.mult))

                def couplings(x, i):
                    n, mat, tok, feat, bank, pm, pt, pf = shapes(x)
                    sm = SMALL[x]
                    await_stage(dve, x, "act", "ex", i)
                    done(x, "dve", dve.tensor_tensor(sm["BG"][0:n, 0:H], sm["GB"][0:n, H:2 * H], sm["EX"][0:n, 0:H], ALU.mult))
                    await_stage(dve, x, "act", "gm", i)
                    await_stage(dve, x, "dve", "st", i)
                    done(x, "dve", dve.tensor_tensor(mat["BM"], mat["BM"], mat["GM"], ALU.mult))
                    await_stage(dve, x, "pe", "kk", i)
                    await_stage(dve, x, "dve", "stg", i)
                    done(x, "dve", dve.tensor_tensor(mat["BM"], mat["BM"], pm[3], ALU.mult))

                def first_inverse(x, i):
                    n, mat, tok, feat, bank, pm, pt, pf = shapes(x)
                    await_stage(dve, x, "pool", "bl0", i)
                    done(x, "dve", dve.tensor_tensor(mat["UI"], over_heads(ident[0:n, 0:n], n), mat["BL0"], ALU.subtract))

                def attention(x, i, queries):
                    n, mat, tok, feat, bank, pm, pt, pf = shapes(x)
                    done(x, "dve", dve.tensor_tensor(mat["D"], mat["GM"], over_heads(C("UP" if x < 2 else "UPS", n, n), n), ALU.mult))
                    await_stage(dve, x, "pe", "qk", i)
                    await_stage(dve, x, "dve", "gu", i)
                    done(x, "dve", dve.scalar_tensor_tensor(out=mat["ATT"], in0=pm[0], scalar=DH ** -0.5, in1=mat["D"], op0=ALU.mult, op1=ALU.mult))
                    await_stage(dve, x, "act", "er", i)
                    done(x, "dve", dve.scalar_tensor_tensor(out=feat["QD"], in0=queries, scalar=DH ** -0.5, in1=feat["R"], op0=ALU.mult, op1=ALU.mult))

                def keys(x, i):
                    n, mat, tok, feat, bank, pm, pt, pf = shapes(x)
                    sm = SMALL[x]
                    await_stage(dve, x, "pe", "kt", i)
                    await_stage(dve, x, "dve", "bg", i)
                    done(x, "dve", dve.tensor_tensor(tok["KBG"], pt[3], over_dims(sm["BG"][0:n, 0:H], n), ALU.mult))
                    await_stage(dve, x, "act", "exd", i)
                    done(x, "dve", dve.tensor_tensor(tok["KDC"], pt[3], over_dims(sm["GD"][0:n, H:2 * H], n), ALU.mult))

                def values(x, i):
                    n, mat, tok, feat, bank, pm, pt, pf = shapes(x)
                    await_stage(dve, x, "pe", "vt", i)
                    done(x, "dve", dve.tensor_tensor(tok["VB"], pt[3], over_dims(SMALL[x]["GB"][0:n, H:2 * H], n), ALU.mult))

                def doubling(x, i, lev):
                    n, mat, tok, feat, bank, pm, pt, pf = shapes(x)
                    await_stage(dve, x, "pe", f"tu{lev}", i)
                    if lev < LEV[x]:
                        done(x, "dve", dve.tensor_tensor(mat["TI"], mat["TI"], pm[1], ALU.subtract))
                    done(x, "dve", dve.tensor_tensor(mat["UI"], mat["UI"], pm[2], ALU.subtract))

                with dve.Fori(0, NT // 2) as i:
                    for x in range(2):
                        for e in ("pe", "act"):
                            dve.wait_ge(DONE[x][e], i * len(STAGES[x][e]))
                        dve.wait_ge(DONE[x]["dve"], i * len(STAGES[x]["dve"]))
                    for x in range(2):
                        gate_columns(x, i, bass.ds(i * 2 + x, 1))
                    for x in range(2):
                        decays(x, i)
                    for x in range(2):
                        couplings(x, i)
                    for x in range(2):
                        first_inverse(x, i)
                    for x in range(2):
                        attention(x, i, QKV[:, 0:H, bass.ds(i * 2 * P + x * P, P)])
                    for x in range(2):
                        keys(x, i)
                    for x in range(2):
                        values(x, i)
                    for lev in range(1, LEV[0] + 1):
                        for x in range(2):
                            doubling(x, i, lev)
                    for x in range(2):
                        await_stage(dve, x, "pe", "s", i)
                        await_stage(dve, x, "pool", "sg", i)
                        done(x, "dve", dve.tensor_tensor(state, decayed, shapes(x)[6][2], ALU.add))
                x = 2
                n, mat, tok, feat, bank, pm, pt, pf = shapes(x)
                for y in range(2):
                    for e in ("pe", "act", "dve"):
                        dve.wait_ge(DONE[y][e], 4 * len(STAGES[y][e]))
                gate_columns(x, 0, slice(NT, NT + 1))
                decays(x, 0)
                couplings(x, 0)
                first_inverse(x, 0)
                attention(x, 0, QKV[:, 0:H, SEQ:T])
                keys(x, 0)
                values(x, 0)
                dve.wait_ge(s_bkt, 1)
                dve.tensor_tensor(EQ, BKT.unsqueeze(1).to_broadcast([P, N_BUCKETS, P]),
                                  C("THR")[:, N_BUCKETS:2 * N_BUCKETS].unsqueeze(2).to_broadcast([P, N_BUCKETS, P]), ALU.is_equal).then_inc(s_eq, 1)

                def sum_bias(h):
                    dve.wait_ge(s_eqr, h + 1)
                    dve.tensor_reduce(SBI.rearrange("p (h n) -> p h n", h=H)[:, h, :], EQR.rearrange("p m n -> p n m"), AX.X,
                                      ALU.add).then_inc(s_eqd, 1)
                doubling(x, 0, 1)
                doubling(x, 0, 2)
                sum_bias(0)
                sum_bias(1)
                await_stage(dve, x, "dve", "kd")
                for b in range(DEC_B + 2):
                    if b < DEC_B:
                        if b >= 2:
                            dve.wait_ge(s_sps, b - 1)
                        dve.tensor_scalar(KDM[b % 2][0:NS, :], at(TILE[x]["KDC"], HD)[0:NS, :], C("BEQ", NS)[:, b:b + 1], None,
                                          ALU.mult).then_inc(s_kdm[b % 2], 1)
                    if b >= 2:
                        k = b - 2
                        dve.wait_ge(s_sps, k + 1)
                        dve.wait_ge(s_s0d, k + 1)
                        dve.tensor_tensor(S0[:, k, :, :], S0[:, k, :, :], BK[4 + k % 2].rearrange("p (h e) -> p h e", h=H), ALU.add).then_inc(s_sns, 1)
                for h in range(H):
                    b = h % 2
                    dve.wait_ge(s_zs[b], h // 2 + 1)
                    own(dve.scalar_tensor_tensor(out=OA[:, h, :], in0=OA[:, h, :], scalar=V("gn"), in1=OZ[b], op0=ALU.mult, op1=ALU.mult))
                    dve.wait_ge(s_one[b], h // 2 + 1)
                    own.settle()
                    dve.tensor_tensor(OA[:, h, :], OA[:, h, :], ORN[b], ALU.mult).then_inc(s_on[b], 1)
                    if h in (0, 1):
                        sum_bias(h + 2)
                dve.wait_ge(s_eqd, H)
                lgv = lgs.rearrange("p (n h) -> p n h", h=H)
                own(dve.scalar_tensor_tensor(out=lgv, in0=lgv, scalar=ASCALE, in1=SBI.rearrange("p (h n) -> p n h", h=H), op0=ALU.mult, op1=ALU.add))
                own.settle()
                own(dve.tensor_tensor(lgv, lgv, MNG.unsqueeze(2).to_broadcast([P, P, H]), ALU.add))
                for b in range(2):
                    dve.wait_ge(s_on[b], 2)
                counts["dve"] = own.n

        end_phase()

        top[0] = work2
        QF = at(take(H * T), H * T).rearrange("p (h t) -> p h t", h=H)
        KF = at(take(H * T), H * T).rearrange("p (h t) -> p h t", h=H)
        bias_at, v_at = take(H * SEQ), take(NT * HD)
        BIAS = at(bias_at, H * SEQ).rearrange("p (h j) -> p h j", h=H)
        VT = at(v_at, NT * HD).rearrange("p (t n) -> p t n", n=HD)
        VSN = at(take(HD), HD)
        VG = [at(take(4096), 4096).rearrange("p (n d) -> p n d", d=HD) for _ in range(2)]
        ISC2 = [at(take(8), 8, I32) for _ in range(2)]
        PDM2 = at(take(4), 4)
        LG = [at(take(REV), REV) for _ in range(3)]
        PTB = [at(take(SEQ), SEQ).rearrange("p (k n) -> p k n", n=P) for _ in range(2)]
        NM, RS = at(take(6), 6), at(take(6), 6)
        SPT = at(take(HD), HD)
        PNT = at(take(H * NS), H * NS)
        SRW = TOPK + DEC_T
        SR = at(take(H * SRW), H * SRW)[0:NS, :].rearrange("p (h k) -> p h k", h=H)
        TOES, HOT = LG[0:2], LG[2]
        RELB = at(take(H), H)
        lo = slice(0, NS)
        NX = at(take(H * NS), H * NS)[lo, :].rearrange("p (h b t) -> p h b t", h=H, b=DEC_B)
        BN = at(take(H * 64), H * 64)[lo, :].rearrange("p (h t m) -> p h t m", h=H, t=DEC_T)
        BNR = at(take(H * DEC_T), H * DEC_T)[lo, :].rearrange("p (h t) -> p h t", h=H)
        DQ = at(take(DEC_T), DEC_T)[lo, :]
        SM4 = at(take(8), 8)[lo, :]
        assert top[0] <= ARENA, top[0]


        s_rel, s_qkf, s_toep, s_toc, s_toe = sem("bias_rows_in"), sem("q_k_in"), sem("bias_psum"), sem("bias_row"), sems("bias_row_stored", 2)
        s_bt, s_kps, s_nd = sem("bias_and_values_in"), sem("k_stored"), sem("new_dots")
        s_srp, s_sx, s_se, s_sp = sem("sample_rows"), sem("sample_shifted"), sem("sample_exp"), sem("sample_probs")
        s_ptp, s_pt2, s_nv, s_nvc = sem("sample_probs_psum"), sem("sample_probs_by_key"), sem("new_values"), sem("new_values_out")
        s_vgi, s_vgu = sems("values_in", 2), sems("values_used", 2)
        s_lgp, s_lgr, s_mx, s_ex, s_pn = sem("logits_psum"), sem("logits_read"), sem("maximum"), sem("exp_done"), sem("probs")
        s_tp, s_tc, s_ov, s_oc = sem("probs_transposed"), sem("probs_by_key"), sem("out_psum"), sem("out_copied")
        STEPS = [(i, h) for i in range(NT) for h in range(H)]
        NU = len(STEPS)

        with nc.Block() as block:
            @block.sync
            def _(sp):
                sp.dma_start(HOT[0:N_BUCKETS, :], a["HOT"]).then_inc(s_rel, 16)
                sp.dma_start(RELB[0:N_BUCKETS, :], a["RELB"]).then_inc(s_rel, 16)
                sp.dma_start(QF, s["PR"][PR_Q:PR_Q + H].rearrange("c p t -> p c t")).then_inc(s_qkf, 16)
                sp.dma_start(KF, s["PR"][PR_K:PR_K + H].rearrange("c p t -> p c t")).then_inc(s_qkf, 16)
                sp.dma_start(VT, o["VP"].rearrange("(t p) n -> p t n", p=P)).then_inc(s_bt, 16)
                sp.dma_start(VSN[0:NS, :], o["VS"]).then_inc(s_bt, 16)
                for h in range(H):
                    sp.wait_ge(s_toc, h + 1)
                    sp.dma_start(s["TOE"][h], TOES[h % 2]).then_inc(s_toe[h % 2], 16)
                for b in range(2):
                    sp.wait_ge(s_toe[b], 16 * H // 2)
                sp.dma_start(BIAS, bass.AP(s["TOE"].tensor, P - 1, [[REV - 1, P], [P * REV, H], [1, SEQ]])).then_inc(s_bt, 16)
                sp.wait_ge(s_qkf, 32)
                sp.dma_start(o["KP"].rearrange("h p t -> p h t"), KF[:, :, 0:SEQ]).then_inc(s_kps, 16)
                sp.wait_ge(s_kps, 16)

            @block.gpsimd
            def _(pool):
                own = Own(pool, own_g, counts["pool"])
                gather_rows(pool, own, VG, "CV", s_vgi, s_vgu, ISC2, PDM2)
                counts["pool"] = own.n

            @block.tensor
            def _(pe):
                pe.wait_ge(s_rel, 32)
                for h in range(H):
                    if h >= 2:
                        pe.wait_ge(s_toc, h - 1)
                    for t0, n in ((0, 512), (512, 512), (1024, P)):
                        last = pe.matmul(PP[h % 2][:, t0:t0 + n], RELB[0:N_BUCKETS, h:h + 1].to_broadcast([N_BUCKETS, P]),
                                         HOT[0:N_BUCKETS, t0:t0 + n], start=True, stop=True)
                    last.then_inc(s_toep, 1)
                pe.wait_ge(s_qkf, 32)
                pe.wait_ge(s_toc, H)
                for h in range(H):
                    last = pe.matmul(BK[3][0:NS, h * NS:(h + 1) * NS], QF[:, h, SEQ:T], KF[:, h, SEQ:T], start=True, stop=True)
                last.then_inc(s_nd, 1)
                by_head = lgs.rearrange("p (f q h) -> p f h q", f=2, h=H)
                for h in range(H):
                    for f in range(2):
                        last = pe.transpose(psum[0:NS, 2048 + h * TOPK + f * P:2048 + h * TOPK + (f + 1) * P], by_head[:, f, h, :], ident)
                last.then_inc(s_srp, 1)
                pe.wait_ge(s_sp, 1)
                for f in range(2):
                    for h in range(H):
                        c = (f * H + h) * NS
                        pe.transpose(BK[0][:, c:c + NS], SR[:, h, f * P:(f + 1) * P], ident[0:NS, 0:NS])
                for h in range(H):
                    last = pe.transpose(BK[1][0:NS, h * NS:(h + 1) * NS], NX[:, h].rearrange("p b t -> p (b t)"), ident[0:NS, 0:NS])
                last.then_inc(s_ptp, 1)
                pe.wait_ge(s_pt2, 1)
                pe.wait_ge(s_bt, 48)
                for h in range(H):
                    last = pe.matmul(BK[7][:, h * NS:(h + 1) * NS], VSN[0:NS, h * DH:(h + 1) * DH], PNT[0:NS, h * NS:(h + 1) * NS],
                                     start=True, stop=True)
                last.then_inc(s_nv, 1)

                def logits(u):
                    i, h = STEPS[u]
                    if u >= 2:
                        pe.wait_ge(s_lgr, u - 1)
                    L = P * (i + 1)
                    for k0 in range(0, L, 512):
                        n = min(512, L - k0)
                        c = 1024 * (u % 2) + k0
                        last = pe.matmul(psum[:, c:c + n], QF[:, h, i * P:(i + 1) * P], KF[:, h, k0:k0 + n], start=True, stop=True)
                    last.then_inc(s_lgp, 1)

                def to_keys(u):
                    pe.wait_ge(s_pn, u + 1)
                    if u:
                        pe.wait_ge(s_tc, u)
                    for k in range(STEPS[u][0] + 1):
                        last = pe.transpose(psum[:, 2048 + k * P:2048 + (k + 1) * P], LG[u % 3][:, k * P:(k + 1) * P], ident)
                    last.then_inc(s_tp, 1)

                def weighted_values(u):
                    i, h = STEPS[u]
                    pe.wait_ge(s_tc, u + 1)
                    if u:
                        pe.wait_ge(s_oc, u)
                    for k in range(i + 1):
                        last = pe.matmul(BK[6][:, 0:P], VT[:, k, h * DH:(h + 1) * DH], PTB[u % 2][:, k, :], start=(k == 0), stop=(k == i))
                    last.then_inc(s_ov, 1)

                def sample_values(u):
                    g = u // 2
                    if u % 2 == 0:
                        pe.wait_ge(s_vgi[g % 2], P * (g // 2 + 1))
                    for q in (2 * (u % 2), 2 * (u % 2) + 1):
                        for h in range(H):
                            for f in range(2):
                                c, w = h * NS + 4 * g + q, (f * H + h) * NS + 4 * g + q
                                last = pe.matmul(BK[7][:, c:c + 1], VG[g % 2][:, 2 * q + f, h * DH:(h + 1) * DH], SPT[:, w:w + 1],
                                                 start=(f == 0), stop=(f == 1))
                    if u % 2:
                        last.then_inc(s_vgu[g % 2], 1)

                pe.wait_ge(s_nvc, 1)
                logits(0)
                for u in range(NU + 2):
                    if u + 1 < NU:
                        logits(u + 1)
                    if 1 <= u <= NU:
                        to_keys(u - 1)
                    if u >= 2:
                        weighted_values(u - 2)
                    if u < NU:
                        sample_values(u)

            @block.scalar
            def _(act):
                for h in range(H):
                    act.wait_ge(s_toep, h + 1)
                    if h >= 2:
                        act.wait_ge(s_toe[h % 2], 16)
                    act.activation(TOES[h % 2], PP[h % 2][:, 0:REV], ACT.Copy).then_inc(s_toc, 1)
                act.wait_ge(s_sx, 1)
                act.activation(SR, SR, ACT.Exp).then_inc(s_se, 1)
                act.wait_ge(s_ptp, 1)
                act.activation(SPT, BK[0], ACT.Copy)
                act.activation(PNT[0:NS, :], BK[1][0:NS, 0:H * NS], ACT.Copy).then_inc(s_pt2, 1)
                act.wait_ge(s_nv, 1)
                act.activation(OB[:, :, SEQ:T], BK[7][:, 0:H * NS].rearrange("p (h q) -> p h q", h=H), ACT.Copy).then_inc(s_nvc, 1)
                for u in range(NU + 2):
                    if u < NU:
                        L = P * (STEPS[u][0] + 1)
                        act.wait_ge(s_mx, u + 1)
                        b = u % 3
                        act.activation(LG[b][:, 0:L], LG[b][:, 0:L], ACT.Exp, bias=NM[:, 2 * b + 1:2 * b + 2],
                                       accum_out=RS[:, 2 * b:2 * b + 1]).then_inc(s_ex, 1)
                    if 1 <= u <= NU:
                        v = u - 1
                        L = P * (STEPS[v][0] + 1)
                        if v >= 2:
                            act.wait_ge(s_ov, v - 1)
                        act.wait_ge(s_tp, v + 1)
                        act.activation(PTB[v % 2].rearrange("p k n -> p (k n)")[:, 0:L], psum[:, 2048:2048 + L], ACT.Copy).then_inc(s_tc, 1)
                    if u >= 2:
                        v = u - 2
                        i, h = STEPS[v]
                        act.wait_ge(s_ov, v + 1)
                        act.activation(OB[:, h, i * P:(i + 1) * P], BK[6][:, 0:P], ACT.Copy).then_inc(s_oc, 1)

            @block.vector
            def _(dve):
                own = Own(dve, own_v, counts["dve"])
                dve.wait_ge(s_nd, 1)
                blk = C("BLK", NS, NS).rearrange("p (b t) -> p b t", b=DEC_B)
                own(dve.tensor_tensor(NX, BK[3][lo, 0:H * NS].rearrange("p (h b t) -> p h b t", h=H, b=DEC_B),
                                      blk.unsqueeze(1).to_broadcast([NS, H, DEC_B, DEC_T]), ALU.mult))
                own(dve.tensor_scalar(DQ, C("THR", NS)[:, N_BUCKETS:N_BUCKETS + DEC_T], -1.0, qpos, ALU.mult, ALU.add))
                own.settle()
                own(dve.tensor_scalar(DQ, DQ, float(-PAST), None, ALU.add))
                new_lg = SR[:, :, TOPK:SRW]
                own(dve.tensor_reduce(new_lg, NX.rearrange("p h b t -> p h t b"), AX.X, ALU.add))
                own.settle()
                own(dve.tensor_tensor(BN, DQ.unsqueeze(1).unsqueeze(3).to_broadcast([NS, H, DEC_T, DEC_T]),
                                      C("THR", NS)[:, N_BUCKETS:N_BUCKETS + DEC_T].unsqueeze(1).unsqueeze(1).to_broadcast([NS, H, DEC_T, DEC_T]), ALU.is_equal))
                own.settle()
                rbn = V("rb", 0, H * N_BUCKETS)[lo, :].rearrange("p (h m) -> p h m", h=H)[:, :, 0:DEC_T]
                own(dve.tensor_tensor(BN, BN, rbn.unsqueeze(2).to_broadcast([NS, H, DEC_T, DEC_T]), ALU.mult))
                own.settle()
                own(dve.tensor_reduce(BNR, BN, AX.X, ALU.add))
                own.settle()
                own(dve.scalar_tensor_tensor(out=new_lg, in0=new_lg, scalar=ASCALE, in1=BNR, op0=ALU.mult, op1=ALU.add))
                own.settle()
                own(dve.tensor_tensor(new_lg, new_lg, new_sel[lo, :].unsqueeze(1).to_broadcast([NS, H, DEC_T]), ALU.add))
                dve.wait_ge(s_srp, 1)
                own(dve.tensor_copy(SR[:, :, 0:TOPK], psum[lo, 2048:3072].rearrange("p (h k) -> p h k", h=H)))
                own.settle()
                own(dve.tensor_reduce(SM4[:, 0:H], SR, AX.X, ALU.max))
                own.settle()
                dve.tensor_tensor(SR, SR, SM4[:, 0:H].unsqueeze(2).to_broadcast([NS, H, SRW]), ALU.subtract).then_inc(s_sx, 1)
                dve.wait_ge(s_se, 1)
                own(dve.tensor_reduce(SM4[:, 0:H], SR, AX.X, ALU.add))
                own.settle()
                own(dve.reciprocal(SM4[:, H:2 * H], SM4[:, 0:H]))
                own.settle()
                own(dve.tensor_tensor(SR, SR, SM4[:, H:2 * H].unsqueeze(2).to_broadcast([NS, H, SRW]), ALU.mult))
                own.settle()
                dve.tensor_tensor(NX, SR[:, :, TOPK:SRW].unsqueeze(2).to_broadcast([NS, H, DEC_B, DEC_T]),
                                  blk.unsqueeze(1).to_broadcast([NS, H, DEC_B, DEC_T]), ALU.mult).then_inc(s_sp, 1)

                def normalise(u):
                    L, b = P * (STEPS[u][0] + 1), u % 3
                    dve.wait_ge(s_ex, u + 1)
                    own(dve.reciprocal(RS[:, 2 * b + 1:2 * b + 2], RS[:, 2 * b:2 * b + 1]))
                    own.settle()
                    dve.tensor_scalar(LG[b][:, 0:L], LG[b][:, 0:L], RS[:, 2 * b + 1:2 * b + 2], None, ALU.mult).then_inc(s_pn, 1)

                dve.wait_ge(s_bt, 48)
                for u in range(NU + 1):
                    if u < NU:
                        i, h = STEPS[u]
                        L, b = P * (i + 1), u % 3
                        lg = LG[b][:, 0:L]
                        dve.wait_ge(s_lgp, u + 1)
                        if u >= 3:
                            dve.wait_ge(s_tp, u - 2)
                        dve.scalar_tensor_tensor(out=lg, in0=psum[:, 1024 * (u % 2):1024 * (u % 2) + L], scalar=ASCALE, in1=BIAS[:, h, SEQ - L:SEQ],
                                                 op0=ALU.mult, op1=ALU.add).then_inc(s_lgr, 1)
                        dve.wait_ge(s_lgr, u + 1)
                        own(dve.tensor_tensor(lg, lg, mask[:, mask_at[i]:mask_at[i] + L], ALU.add))
                        own.settle()
                        own(dve.tensor_reduce(NM[:, 2 * b:2 * b + 1], lg, AX.X, ALU.max))
                        own.settle()
                        dve.tensor_scalar(NM[:, 2 * b + 1:2 * b + 2], NM[:, 2 * b:2 * b + 1], -1.0, None, ALU.mult).then_inc(s_mx, 1)
                    if u >= 1:
                        normalise(u - 1)
                for b in range(2):
                    dve.wait_ge(s_vgu[b], 8)
                own(dve.tensor_tensor(OB[:, :, SEQ:T], OB[:, :, SEQ:T], BK[7][:, 0:H * NS].rearrange("p (h q) -> p h q", h=H), ALU.add))
                own.settle()
                counts["dve"] = own.n

        end_phase()

        early.close()

        spare = N_CONST + N_VEC
        X1 = at(work, KD * T).rearrange("p (k t) -> p k t", t=T)
        RN2, RT2, SUM = [at(spare + k * T, T) for k in range(3)]
        assert spare + 3 * T <= work

        TG = T // 4
        QUARTERS = [(g * TG, g * 512) for g in range(4)]
        PB = [psum[:, 2048 * b:2048 * (b + 1)] for b in range(2)]
        PBV = [p.rearrange("p (g n) -> p g n", n=512)[:, :, 0:TG] for p in PB]

        def quarters(x):
            return x.rearrange("p (g n) -> p g n", n=TG)

        class Space:

            def __init__(self, owner, name, n, dt=F32):
                self.all = owner.enter_context(nc.sbuf_tensor(name, [P, n], dt))
                self.at, self.n = 0, n

            def take(self, n):
                self.at += n
                assert self.at <= self.n, (self.at, self.n)
                return self.all[:, self.at - n:self.at]

        def norm_of_squares(act, full, used, done):
            act.wait_ge(full, used)
            own = Own(act, own_a, counts["act"])
            own(act.activation(quarters(RT2), PBV[0], ACT.Ln, scale=1.0 / DM, bias=eps))
            own.settle()
            counts["act"] = own.n
            act.activation(RN2, RT2, ACT.Exp, scale=-0.5).then_inc(done, 1)

        with ExitStack() as stage:
            mem = Space(stage, "merge", 2 * H * DM + KD * T + 4 * T + 4096)
            WP = [mem.take(H * DM).rearrange("p (k n) -> p k n", n=DM) for _ in range(2)]
            MG = mem.take(KD * T).rearrange("p (k t) -> p k t", t=T)
            SG = [[mem.take(T) for b in range(2)] for m in range(2)]
            WO = [mem.take(4096).rearrange("p (k n) -> p k n", n=512), WP[0].rearrange("p k n -> p (k n)").rearrange("p (k n) -> p k n", n=512)]
            SQ2 = SG[0]
            s_wp, s_sgi, s_mg = sem("merge_weights_in"), sems("gates_in", 2), sem("merged")
            s_wo, s_x1 = sems("out_weights_in", 2), sems("x_again", 4)
            s_f, s_e = sems("merge_full", 2), sems("merge_free", 2)
            s_q2, s_s2, s_r2 = sem("squares2"), sem("squares_added2"), sem("norm2")

            with nc.Block() as block:
                @block.sync
                def _(sp):
                    for m, n in enumerate(("WPA", "WPB")):
                        sp.dma_start(WP[m], a[n]).then_inc(s_wp, 16)
                    for c in range(KD):
                        b = c % 2
                        if c >= 2:
                            sp.wait_ge(s_mg, c - 1)
                        for m, first in ((0, PR_GA), (1, PR_GB)):
                            sp.dma_start(SG[m][b], s["PR"][first + c]).then_inc(s_sgi[b], 16)
                        if c == 1:
                            sp.dma_start(WO[0], a["WO"][0].rearrange("p (k n) -> p k n", n=512)).then_inc(s_wo[0], 16)
                    for m in range(2):
                        sp.wait_ge(s_f[m], KD)
                    for q in range(4):
                        sp.dma_start(X1[:, 2 * q:2 * q + 2, :], a["X"][:, 2 * q:2 * q + 2, :]).then_inc(s_x1[q], 16)
                        if q == 1:
                            sp.dma_start(WO[1], a["WO"][1].rearrange("p (k n) -> p k n", n=512)).then_inc(s_wo[1], 16)

                @block.tensor
                def _(pe):
                    uses = [0, 0]

                    def project(b, K, weights, rhs):
                        if uses[b]:
                            pe.wait_ge(s_e[b], uses[b])
                        for k in range(K):
                            for t0, c0 in QUARTERS:
                                last = pe.matmul(PB[b][:, c0:c0 + TG], weights(k), rhs(k)[:, t0:t0 + TG], start=(k == 0), stop=(k == K - 1))
                        last.then_inc(s_f[b], 1)
                        uses[b] += 1

                    pe.wait_ge(s_wp, 32)
                    for c in range(KD):
                        for m, out in enumerate((OA, OB)):
                            project(m, H, lambda k: WP[m][:, k, c * P:(c + 1) * P], lambda k: out[:, k, :])
                    pe.wait_ge(s_mg, KD)
                    for c in range(KD):
                        if c % 4 == 0:
                            pe.wait_ge(s_wo[c // 4], 16)
                        project(c % 2, KD, lambda k: WO[c // 4][:, k, (c % 4) * P:(c % 4 + 1) * P], lambda k: MG[:, k, :])
                    pe.wait_ge(s_s2, KD)
                    project(0, 1, lambda k: C("ONES"), lambda k: SUM)

                @block.scalar
                def _(act):
                    for c in range(KD):
                        act.wait_ge(s_e[c % 2], KD + c // 2 + 1)
                        if c >= 2:
                            act.wait_ge(s_s2, c - 1)
                        act.activation(SQ2[c % 2], X1[:, c, :], ACT.Square).then_inc(s_q2, 1)
                    norm_of_squares(act, s_f[0], KD + KD // 2 + 1, s_r2)

                @block.vector
                def _(dve):
                    own = Own(dve, own_v, counts["dve"])
                    for c in range(KD):
                        b = c % 2
                        dve.wait_ge(s_sgi[b], 32 * (c // 2 + 1))
                        for m in range(2):
                            dve.wait_ge(s_f[m], c + 1)
                            dve.tensor_tensor(quarters(SG[m][b]), PBV[m], quarters(SG[m][b]), ALU.mult).then_inc(s_e[m], 1)
                        for m in range(2):
                            dve.wait_ge(s_e[m], c + 1)
                        dve.tensor_tensor(MG[:, c, :], SG[0][b], SG[1][b], ALU.add).then_inc(s_mg, 1)
                    own(dve.memset(SUM, 0.0))
                    own.settle()

                    def add_squares(c):
                        dve.wait_ge(s_q2, c + 1)
                        if c:
                            dve.wait_ge(s_s2, c)
                        dve.tensor_tensor(SUM, SUM, SQ2[c % 2], ALU.add).then_inc(s_s2, 1)
                    for c in range(KD):
                        dve.wait_ge(s_x1[c // 2], 16)
                        dve.wait_ge(s_f[c % 2], KD + c // 2 + 1)
                        dve.tensor_tensor(quarters(X1[:, c, :]), quarters(X1[:, c, :]), PBV[c % 2], ALU.add).then_inc(s_e[c % 2], 1)
                        if c:
                            add_squares(c - 1)
                    add_squares(KD - 1)
                    counts["dve"] = own.n

            end_phase()

        PADW = 2 + SEQ + DEC_B * (DEC_T + 2)
        OUTW = PADW - 2
        PASSES = ((0, 0), (0, 1), (1, 0))

        def sample_of(pad):
            return pad[:, 2 + SEQ:PADW].rearrange("p (b t) -> p b t", b=DEC_B)

        def by_sample(out):
            return out[:, SEQ:SEQ + DEC_B * (DEC_T + 2)].rearrange("p (b t) -> p b t", b=DEC_B)[:, :, 2:2 + DEC_T]

        with ExitStack() as stage:
            mem = Space(stage, "up", 2048 + 4 * PADW + 3 * OUTW + 2 * FC * (2 * DEC_B + 18) + 8)
            parts = Space(stage, "up_parts", 2 * KD * T + 8192, F32R)
            XP = [parts.take(KD * T).rearrange("p (k t) -> p k t", t=T) for _ in range(2)]
            WUP = [[parts.take(2048).rearrange("p (k n) -> p k n", n=2 * P) for _ in range(2)] for _ in range(2)]
            WU = [mem.take(1024).rearrange("p (k n) -> p k n", n=2 * P) for _ in range(2)]
            PADS = [[mem.take(PADW) for b in range(2)] for m in range(2)]
            CVG = [mem.take(OUTW) for b in range(2)]
            CVV = mem.take(OUTW)
            SFS = mem.take(2 * FC * 2 * DEC_B).rearrange("p (c t) -> p c t", t=2 * DEC_B)
            COFS = mem.take(2 * FC * 18).rearrange("p (c t) -> p c t", t=18)
            STEP = mem.take(8)
            NX1 = [c[:, 0:T] for c in CVG]
            HS = [RT2, SUM]
            s_xt, s_xh, s_xl = sem("normed2"), sem("token_high"), sem("token_low")
            s_wu, s_wh, s_wl = sems("up_weights_in", 2), sems("up_weights_high", 2), sems("up_weights_low", 2)
            s_f, s_e = sems("up_full", 2), sems("up_free", 2)
            s_sf, s_cg, s_cvv, s_sl, s_h, s_ho = sem("ffn_state_in"), sems("gate_conv", 2), sems("value_conv", 2), sems("gate_silu", 2), sems("hidden", 2), sems("hidden_stored", 2)
            s_cof = sem("ffn_state_stored")

            with nc.Block() as block:
                @block.sync
                def _(sp):
                    with sp.Fori(0, FC) as i:
                        for half in range(2):
                            sp.wait_ge(s_wl[half], i)
                            sp.dma_start(WU[half], a["WUP"][bass.ds(i, 1), :, 1024 * half:1024 * (half + 1)].rearrange("o p n -> p (o n)")
                                         .rearrange("p (k n) -> p k n", n=2 * P)).then_inc(s_wu[half], 16)

                @block.gpsimd
                def _(pool):
                    pool.dma_start(SFS, a["SF"]).then_inc(s_sf, 16)
                    with pool.Fori(0, FC // 2) as i:
                        for b in range(2):
                            pool.wait_ge(s_h[b], i + 1)
                            alone(pool)
                            pool.dma_start(s["H"][bass.ds(i * 2 + b, 1), :, :].rearrange("o p n -> p (o n)"), HS[b]).then_inc(s_ho[b], 16)
                    for b in range(2):
                        pool.wait_ge(s_h[b], FC // 2)
                    pool.dma_start(o["COF"], COFS).then_inc(s_cof, 16)
                    pool.wait_ge(s_cof, 16)
                    for b in range(2):
                        pool.wait_ge(s_ho[b], 16 * (FC // 2))

                @block.tensor
                def _(pe):
                    pe.wait_ge(s_xl, KD)
                    with pe.Fori(0, FC // 2) as i:
                        for b in range(2):
                            for half in range(2):
                                pe.wait_ge(s_wl[half], i * 2 + (b + 1))
                            for m in range(2):
                                pe.wait_ge(s_e[m], i * 2 + b)
                                for k in range(KD):
                                    for n, (wp, xp) in enumerate(PASSES):
                                        for t0, c0 in QUARTERS:
                                            last = pe.matmul(PB[m][:, c0:c0 + TG], WUP[wp][b][:, k, m * P:(m + 1) * P], XP[xp][:, k, t0:t0 + TG],
                                                             start=(k == 0 and n == 0), stop=(k == KD - 1 and n == 2))
                                last.then_inc(s_f[m], 1)

                @block.scalar
                def _(act):
                    for k in range(KD):
                        act.wait_ge(s_xt, k + 1)
                        act.activation(XP[0][:, k, :], NX1[k % 2], ACT.Copy).then_inc(s_xh, 1)

                    def high_weights(b, chunk):
                        for half in range(2):
                            act.wait_ge(s_wu[half], chunk * 16 + 16)
                            act.activation(WUP[0][b][:, 4 * half:4 * half + 4, :], WU[half], ACT.Copy).then_inc(s_wh[half], 1)

                    def chunk_out(i, b, more):
                        for m, s_c in enumerate((s_cg, s_cvv)):
                            act.wait_ge(s_c[b], i)
                            act.wait_ge(s_f[m], i * 2 + (b + 1))
                            act.activation(PADS[m][b][:, 2:2 + 3 * TG].rearrange("p (g n) -> p g n", n=TG), PBV[m][:, 0:3, :], ACT.Copy)
                            act.activation(PADS[m][b][:, 2 + 3 * TG:2 + SEQ], PBV[m][:, 3, 0:SEQ - 3 * TG], ACT.Copy)
                            act.activation(sample_of(PADS[m][b])[:, :, 2:2 + DEC_T],
                                           PBV[m][:, 3, SEQ - 3 * TG:TG].rearrange("p (b t) -> p b t", b=DEC_B),
                                           ACT.Copy).then_inc(s_e[m], 1)
                        if more:
                            high_weights(b, i * 2 + (b + 2))
                        alone(act)
                        act.wait_ge(s_cg[b], i + 1)
                        alone(act)
                        act.activation(CVG[b], CVG[b], ACT.Silu, bias=vec[:, bass.ds(i * 2 + (VEC["bf"] + b), 1)]).then_inc(s_sl[b], 1)
                    high_weights(0, 0)
                    high_weights(1, 1)
                    act.wait_ge(s_sf, 16)
                    with act.Fori(0, FC // 2 - 1) as i:
                        for b in range(2):
                            chunk_out(i, b, True)
                    for b in range(2):
                        chunk_out(FC // 2 - 1, b, False)

                @block.vector
                def _(dve):
                    own = Own(dve, own_v, counts["dve"])
                    for m in range(2):
                        for b in range(2):
                            own(dve.memset(PADS[m][b][:, 0:2], 0.0))

                    def low_tokens(k):
                        dve.wait_ge(s_xh, k + 1)
                        dve.tensor_tensor(XP[1][:, k, :], NX1[k % 2], XP[0][:, k, :], ALU.subtract).then_inc(s_xl, 1)

                    def low_weights(b, chunk):
                        for half in range(2):
                            dve.wait_ge(s_wh[half], chunk + 1)
                            part = slice(4 * half, 4 * half + 4)
                            dve.tensor_tensor(WUP[1][b][:, part, :], WU[half], WUP[0][b][:, part, :], ALU.subtract).then_inc(s_wl[half], 1)

                    for k in range(KD):
                        if k >= 2:
                            dve.wait_ge(s_xl, k - 1)
                        dve.scalar_tensor_tensor(out=NX1[k % 2], in0=X1[:, k, :], scalar=V("g2", k), in1=RN2, op0=ALU.mult, op1=ALU.mult).then_inc(s_xt, 1)
                        if k:
                            low_tokens(k - 1)
                    low_tokens(KD - 1)
                    low_weights(0, 0)
                    low_weights(1, 1)
                    dve.wait_ge(s_xl, KD)
                    dve.wait_ge(s_sf, 16)
                    own.settle()
                    n0 = own.n

                    def chunk_conv(i, b, more):
                        for m, s_c in enumerate((s_cg, s_cvv)):
                            pad, out = PADS[m][b], CVG[b] if m == 0 else CVV
                            chunk = bass.ds(i * 2 + (m * FC + b), 1)
                            k0 = n0 + 8 * b + 4 * m
                            if m == 0:
                                dve.wait_ge(s_h[b], i)
                            else:
                                dve.wait_ge(s_h[1 - b], i + b)
                            dve.wait_ge(own_v, i * 16 + k0)
                            dve.tensor_scalar(sample_of(pad)[:, :, 0:2], SFS[:, chunk, :].rearrange("p o (b t) -> p (o b) t", t=2), 1.0, None,
                                              ALU.mult).then_inc(own_v, 1)
                            dve.wait_ge(s_e[m], i * 2 + (b + 1))
                            dve.wait_ge(own_v, i * 16 + (k0 + 1))
                            dve.tensor_scalar(COFS[:, chunk, 2:18].rearrange("p o (b t) -> p (o b) t", t=2), sample_of(pad)[:, :, DEC_T:DEC_T + 2],
                                              1.0, None, ALU.mult)
                            dve.tensor_scalar(COFS[:, chunk, 0:2].rearrange("p o t -> p (o t)"), pad[:, SEQ:SEQ + 2], 1.0, None, ALU.mult)
                            for j in range(3):
                                w = vec[:, bass.ds(i * 6 + (VEC["wf"] + 3 * (m * FC + b) + j), 1)]
                                if j == 0:
                                    ins = dve.tensor_scalar(out, pad[:, 0:OUTW], w, None, ALU.mult)
                                else:
                                    dve.wait_ge(own_v, i * 16 + (k0 + 1 + j))
                                    ins = dve.scalar_tensor_tensor(out=out, in0=pad[:, j:j + OUTW], scalar=w, in1=out, op0=ALU.mult, op1=ALU.add)
                                ins.then_inc(s_c[b] if j == 2 else own_v, 1)
                            dve.wait_ge(s_c[b], i + 1)
                            dve.tensor_scalar(STEP[:, 0:4], C("ONES")[:, 0:4], 1.0, None, ALU.mult).then_inc(own_v, 1)
                        if more:
                            low_weights(b, i * 2 + (b + 2))
                        dve.wait_ge(s_sl[b], i + 1)
                        dve.wait_ge(s_ho[b], i * 16)
                        bias = vec[:, bass.ds(i * 2 + (VEC["bf"] + FC + b), 1)]
                        dve.scalar_tensor_tensor(out=HS[b][:, 0:SEQ], in0=CVV[:, 0:SEQ], scalar=bias, in1=CVG[b][:, 0:SEQ], op0=ALU.add, op1=ALU.mult)
                        dve.scalar_tensor_tensor(out=HS[b][:, SEQ:T].rearrange("p (b t) -> p b t", t=DEC_T), in0=by_sample(CVV), scalar=bias,
                                                 in1=by_sample(CVG[b]), op0=ALU.add, op1=ALU.mult).then_inc(s_h[b], 1)

                    with dve.Fori(0, FC // 2 - 1) as i:
                        for b in range(2):
                            chunk_conv(i, b, True)
                    for b in range(2):
                        chunk_conv(FC // 2 - 1, b, False)
                    own.n = n0 + 16 * (FC // 2)
                    counts["dve"] = own.n

            end_phase()

        ROUNDS, HALF = KD // 2, FC // 2
        with ExitStack() as stage:
            mem = Space(stage, "down", FC * T + 2 * HALF * 2 * P + 2 * T)
            parts = Space(stage, "down_parts", 4 * T + 8 * P, F32R)
            HH = mem.take(FC * T).rearrange("p (c t) -> p c t", t=T)
            WD = [mem.take(HALF * 2 * P).rearrange("p (k n) -> p k n", n=2 * P) for _ in range(2)]
            SQ2 = [mem.take(T) for _ in range(2)]
            HP = [[parts.take(T) for _ in range(2)] for _ in range(2)]
            WDP = [[parts.take(2 * P) for _ in range(2)] for _ in range(2)]
            FIRST = [0, 2, 6, 12, 17, FC]
            s_hi, s_wd = sems("hidden_in", 5), sems("down_weights_in", 2)
            s_hh, s_hl, s_wh, s_wl, s_used = sems("hidden_high", 2), sems("hidden_low", 2), sems("down_high", 2), sems("down_low", 2), sems("parts_used", 2)
            s_f, s_e = sems("down_full", 2), sems("down_free", 2)
            s_q, s_s, s_r, s_y, s_yo = sems("squares3", 2), sems("squares_added3", 2), sem("norm3"), sem("y"), sem("y_stored")

            with nc.Block() as block:
                @block.sync
                def _(sp):
                    for half in range(2):
                        sp.dma_start(WD[half], a["WDN"][half].rearrange("p (k n) -> p k n", n=2 * P)).then_inc(s_wd[half], 16)
                        for n in ((0, 1, 2), (3, 4))[half]:
                            c0, c1 = FIRST[n], FIRST[n + 1]
                            sp.dma_start(HH[:, c0:c1, :], s["H"][c0:c1].rearrange("c p t -> p c t")).then_inc(s_hi[n], 16)
                    with sp.Fori(0, ROUNDS - 1) as r:
                        for half in range(2):
                            k = HALF * (half + 1) - 1
                            sp.wait_ge(s_wl[k % 2], r * HALF + (k // 2 + 1))
                            sp.dma_start(WD[half], a["WDN"][bass.ds(r * 2 + (half + 2), 1), :, :].rearrange("o p n -> p (o n)")
                                         .rearrange("p (k n) -> p k n", n=2 * P)).then_inc(s_wd[half], 16)
                    for c in range(KD):
                        sp.wait_ge(s_y, c + 1)
                        sp.dma_start(o["Y"][c], X1[:, c, :]).then_inc(s_yo, 16)
                    sp.wait_ge(s_yo, 16 * KD)

                @block.gpsimd
                def _(pool):
                    with pool.Fori(0, ROUNDS) as r:
                        for k in range(FC):
                            b = k % 2
                            pool.wait_ge(s_wh[b], r * HALF + (k // 2 + 1))
                            pool.tensor_tensor(WDP[1][b], WD[k // HALF][:, k % HALF, :], WDP[0][b], ALU.subtract).then_inc(s_wl[b], 1)

                @block.tensor
                def _(pe):
                    with pe.Fori(0, ROUNDS) as r:
                        for k in range(FC):
                            b = k % 2
                            pe.wait_ge(s_hl[b], r * HALF + (k // 2 + 1))
                            pe.wait_ge(s_wl[b], r * HALF + (k // 2 + 1))
                            for m in range(2):
                                if k == 0:
                                    pe.wait_ge(s_e[m], r)
                                for n, (wp, hp) in enumerate(PASSES):
                                    for t0, c0 in QUARTERS:
                                        last = pe.matmul(PB[m][:, c0:c0 + TG], WDP[wp][b][:, m * P:(m + 1) * P], HP[hp][b][:, t0:t0 + TG],
                                                         start=(k == 0 and n == 0), stop=(k == FC - 1 and n == 2))
                                if k == FC - 1 and m == 0:
                                    last.then_inc(s_f[0], 1)
                            last.then_inc(s_used[b], 1)
                    for m in range(2):
                        pe.wait_ge(s_s[m], ROUNDS)
                        pe.wait_ge(s_e[m], ROUNDS)
                    for t0, c0 in QUARTERS:
                        last = pe.matmul(PB[0][:, c0:c0 + TG], C("ONES"), SUM[:, t0:t0 + TG], start=True, stop=True)
                    last.then_inc(s_f[0], 1)

                @block.scalar
                def _(act):
                    def high(r, k):
                        b = k % 2
                        act.wait_ge(s_used[b], r * HALF + k // 2)
                        act.activation(HP[0][b], HH[:, k, :], ACT.Copy).then_inc(s_hh[b], 1)
                        act.activation(WDP[0][b], WD[k // HALF][:, k % HALF, :], ACT.Copy).then_inc(s_wh[b], 1)

                    def square(m, r):
                        act.wait_ge(s_s[m], r)
                        alone(act)
                        act.wait_ge(s_e[m], r + 1)
                        alone(act)
                        act.activation(SQ2[m], X1[:, bass.ds(r * 2 + m, 1), :].rearrange("p o t -> p (o t)"), ACT.Square).then_inc(s_q[m], 1)

                    for k in range(FC):
                        if k in FIRST:
                            act.wait_ge(s_hi[FIRST.index(k)], 16)
                        if k % HALF == 0:
                            act.wait_ge(s_wd[k // HALF], 16)
                        high(0, k)
                    with act.Fori(1, ROUNDS) as r:
                        for k in range(FC):
                            if k % HALF == 0:
                                act.wait_ge(s_wd[k // HALF], r * 16 + 16)
                            high(r, k)
                            if k in (4, 8):
                                square(k // 4 - 1, r - 1)
                    for m in range(2):
                        square(m, ROUNDS - 1)
                    norm_of_squares(act, s_f[0], ROUNDS + 1, s_r)

                @block.vector
                def _(dve):
                    own = Own(dve, own_v, counts["dve"])
                    own(dve.memset(SUM, 0.0))
                    own.settle()

                    def low(r, k):
                        b = k % 2
                        dve.wait_ge(s_hh[b], r * HALF + (k // 2 + 1))
                        dve.tensor_tensor(HP[1][b], HH[:, k, :], HP[0][b], ALU.subtract).then_inc(s_hl[b], 1)

                    def residual(m, r):
                        if m == 0:
                            dve.wait_ge(s_f[0], r + 1)
                        else:
                            dve.wait_ge(s_used[1], r * HALF + HALF)
                        x = X1[:, bass.ds(r * 2 + m, 1), :].rearrange("p o t -> p (o t)")
                        dve.tensor_tensor(quarters(x), quarters(x), PBV[m], ALU.add).then_inc(s_e[m], 1)

                    def add_squares(m, r):
                        dve.wait_ge(s_q[m], r + 1)
                        if m == 0:
                            dve.wait_ge(s_s[1], r)
                        else:
                            dve.wait_ge(s_s[0], r + 1)
                        dve.tensor_tensor(SUM, SUM, SQ2[m], ALU.add).then_inc(s_s[m], 1)

                    for k in range(FC):
                        if k in FIRST:
                            dve.wait_ge(s_hi[FIRST.index(k)], 16)
                        low(0, k)
                    with dve.Fori(1, ROUNDS) as r:
                        for k in range(FC):
                            low(r, k)
                            if k < 2:
                                residual(k, r - 1)
                            if k in (6, 10):
                                add_squares((k - 6) // 4, r - 1)
                    for m in range(2):
                        residual(m, ROUNDS - 1)
                    for m in range(2):
                        add_squares(m, ROUNDS - 1)
                    dve.wait_ge(s_r, 1)
                    for m in range(2):
                        dve.wait_ge(s_e[m], ROUNDS)
                    for c in range(KD):
                        dve.scalar_tensor_tensor(out=X1[:, c, :], in0=X1[:, c, :], scalar=V("gf", c), in1=RN2, op0=ALU.mult, op1=ALU.mult).then_inc(s_y, 1)


def lay_out(i):
    f = {n: np.ascontiguousarray(np.asarray(v)) for n, v in i.items()}

    def rows(w):
        return w.reshape(-1, P, w.shape[1]).transpose(1, 0, 2)

    def groups(w, n):
        return w.reshape(-1, P, w.shape[1] // n, n).transpose(2, 1, 0, 3).reshape(w.shape[1] // n, P, -1)
    w_in = f["w_in"][0]
    o_qkva, o_small, o_z, o_qkvb = 0, 1536, 1544, 2056
    o_qi, o_ki, o_wi, o_g = 3592, 4104, 4168, 4176
    x = np.concatenate([f["x_prompt"].reshape(SEQ, DM), f["x_sample"].reshape(NS, DM)])
    const, comb, onehot = shape_constants()

    def cols(v, n):
        return v.reshape(n, P).T
    wf = f["conv_f_w"][0].reshape(3, 2 * FC, P).transpose(2, 1, 0).reshape(P, -1)
    wa = f["conv_a_w"][0].reshape(4, A_CH, P).transpose(2, 1, 0).reshape(P, -1)
    vec = np.concatenate([
        cols(f["norm1_g"][0], KD), cols(f["norm2_g"][0], KD), cols(f["final_g"], KD), f["norm_a_g"][0][:, None],
        wa, wf, cols(f["conv_f_b"][0], 2 * FC), np.broadcast_to(f["a_log"][0], (P, H)),
        np.broadcast_to(f["dt_bias"][0], (P, H)), np.broadcast_to(f["rel_bias"].T.reshape(-1), (P, H * N_BUCKETS))], axis=1)
    pt = f["page_table"]
    w_up = f["w_up"][0]
    pairs = np.stack([w_up[:, :FF].reshape(DM, FC, P), w_up[:, FF:].reshape(DM, FC, P)], axis=2).reshape(DM, 2 * FF)
    down = f["w_down"][0].reshape(2, FC // 2, P, KD // 2, 2 * P).transpose(3, 0, 2, 1, 4).reshape(KD, P, -1)
    m = {
        "CONST": const, "VEC": vec, "COMB": comb, "HOT": onehot, "RELB": f["rel_bias"],
        "X": rows(x.T.copy()),
        "WIX": rows(np.concatenate([w_in[:, o_qi:o_qi + 512], w_in[:, o_ki:o_ki + 64], w_in[:, o_ki:o_ki + 64]], axis=1)),
        "WSM": rows(np.concatenate([w_in[:, o_wi:o_wi + 8], w_in[:, o_small:o_small + 8]], axis=1)),
        "WG": groups(np.concatenate([w_in[:, o_qkva:o_qkva + 1536], w_in[:, o_z:o_z + 512], w_in[:, o_qkvb:o_qkvb + 1536],
                                     w_in[:, o_g:o_g + 2048]], axis=1), 512),
        "CI": f["cache_idx_k"].reshape(CI_ROWS, 1024),
        "CK": f["cache_k"].reshape(CK_ROWS, 512), "CV": f["cache_v"].reshape(CK_ROWS, 512),
        "PTI": pt.reshape(4, P).T, "PTR": np.repeat(pt, DEC_T, axis=0),
        "WPA": rows(f["w_proj_a"][0]), "WPB": rows(f["w_proj_b"][0]), "WO": groups(f["w_out"][0], 512),
        "WUP": groups(pairs, 256), "WDN": down,
        "SA": f["state_a_conv"][0].reshape(DEC_B * 3, A_CH, P).transpose(2, 1, 0),
        "SF": f["state_ffn_conv"][0].reshape(DEC_B * 2, 2 * FC, P).transpose(2, 1, 0),
        "S0": f["state_a_rec"][0].transpose(2, 0, 1, 3),
    }
    return {n: np.ascontiguousarray(v) for n, v in m.items()}


OUTS = {
    "Y": (KD, P, T), "KP": (H, P, SEQ), "KS": (NS, 512), "VP": (SEQ, 512), "VS": (NS, 512), "KIDX": (DI, T),
    "COA": (P, A_CH, 3 + 3 * DEC_B), "REC": (P, H, DH), "RECS": (P, DEC_B, H, DH), "COF": (P, 2 * FC, 2 + 2 * DEC_B),
}
SCRATCH = {"PR": (PR_N, P, T), "H": (FC, P, T), "QS": (NS, 512), "TOE": (H, P, REV)}


def build(nc, arrays):
    a = {n: nc.dram_tensor(f"in_{n}", v.shape, mybir.dt.from_np(v.dtype), kind="ExternalInput").ap() for n, v in arrays.items()}
    o = {n: nc.dram_tensor(f"out_{n}", shape, F32, kind="ExternalOutput").ap() for n, shape in OUTS.items()}
    s = {n: nc.dram_tensor(f"tmp_{n}", shape, F32, kind="Internal").ap() for n, shape in SCRATCH.items()}
    program(nc, a, o, s)


def kernel(**inputs):
    import concourse.bacc as bacc
    from concourse.bass_utils import run_bass_kernel_spmd
    arrays = lay_out(inputs)
    nc = bacc.Bacc("TRN2", target_bir_lowering=False, num_devices=1)
    build(nc, arrays)
    r = run_bass_kernel_spmd(nc, [{f"in_{n}": v for n, v in arrays.items()}], core_ids=[0]).results[0]
    g = {n: np.asarray(r[f"out_{n}"]) for n in OUTS}
    y = g["Y"].reshape(DM, T).T
    kp = g["KP"].reshape(512, SEQ).T
    ca = g["COA"].transpose(2, 1, 0).reshape(3 + 3 * DEC_B, -1)
    cf = g["COF"].transpose(2, 1, 0).reshape(2 + 2 * DEC_B, -1)
    ki = g["KIDX"].T
    out = (
        y[:SEQ].reshape(1, SEQ, DM), y[SEQ:].reshape(DEC_B, DEC_T, DM),
        kp.reshape(1, 1, SEQ, H, DH), g["VP"].reshape(1, 1, SEQ, H, DH), ki[:SEQ].reshape(1, 1, SEQ, DI),
        ca[:3].reshape(1, 1, 3, -1), g["REC"].transpose(1, 0, 2).reshape(1, 1, H, DH, DH), cf[:2].reshape(1, 1, 2, -1),
        g["KS"].reshape(1, DEC_B, DEC_T, H, DH), g["VS"].reshape(1, DEC_B, DEC_T, H, DH), ki[SEQ:].reshape(1, DEC_B, DEC_T, DI),
        ca[3:].reshape(1, DEC_B, 3, -1), g["RECS"].transpose(1, 2, 0, 3).reshape(1, DEC_B, H, DH, DH),
        cf[2:].reshape(1, DEC_B, 2, -1),
    )
    return tuple(np.ascontiguousarray(v) for v in out)
```
